# Optimizing a Trainium2 kernel written in Bass

```python
import math
import jax
import jax.numpy as jnp
from jax import lax
import numpy as np

D_MODEL = 1024
BATCH = 1
SEQ = 1024
DEPTH = 2
DEC_BATCH = 8
DEC_SEQ = 4
PAST_LEN = 2048
PAGE_SIZE = 128

D_MIX = D_MODEL
D_A = D_MIX // 2
HEAD_A = 64
N_HEADS_A = D_A // HEAD_A
LORA_W = 64
LORA_A = 64
LORA_G = 128
D_A_PROJ = 3 * D_A + LORA_W + LORA_A + LORA_G
SPLITS_A = (D_A, 2 * D_A, 3 * D_A, 3 * D_A + LORA_W, 3 * D_A + LORA_W + LORA_A)
D_B = D_MIX - D_A
S5_GROUP = 16
N_GROUPS_B = D_B // S5_GROUP
S5_STATE = 64
D_IN_AB = D_A_PROJ + D_B
HEAD_C = 128
HALF_C = HEAD_C // 2
N_HEADS_C = D_MIX // HEAD_C
SCALE_C = HALF_C ** -0.5
Q_BLOCK = 128
D_FF = 4 * D_MODEL
RMS_EPS = 1e-6
GN_EPS = 64e-5
DECAY_SCALE = math.exp(-0.5)
LAMBDA_INIT = 0.8 - 0.6 * math.exp(-0.3 * 1)
NEG_INF = -1e30
F32 = jnp.float32

kernel_name = 'hybrid_rwkv7_s5_diffattn_decoder_step'

def rmsnorm(x, g):
    xf = x.astype(F32)
    y = xf * lax.rsqrt(jnp.mean(xf * xf, axis=-1, keepdims=True) + RMS_EPS)
    return (y * g.astype(F32)).astype(x.dtype)

def rwkv7_time_mix(zs, s0, W):
    B_, T, _ = zs.shape
    zf = zs.astype(F32)
    r, k, v, dw, da, dg = jnp.split(zf, SPLITS_A, axis=-1)
    decay = jnp.exp(-DECAY_SCALE * jax.nn.sigmoid(W['rwkv_w0'] + jnp.tanh(dw) @ W['rwkv_w_up']))
    a = jax.nn.sigmoid(W['rwkv_a0'] + da @ W['rwkv_a_up'])
    g = jax.nn.sigmoid(dg) @ W['rwkv_g_up']
    heads = lambda t: t.reshape(B_, T, N_HEADS_A, HEAD_A)
    kk = heads(k * W['rwkv_k_k'])
    kk = kk / jnp.maximum(jnp.sqrt(jnp.sum(kk * kk, axis=-1, keepdims=True)), 1e-12)
    k = k * (1.0 + (a - 1.0) * W['rwkv_k_a'])
    rh, wh, kh, vh, ah = heads(r), heads(decay), heads(k), heads(v), heads(a)

    def step(S, inp):
        r_t, w_t, k_t, v_t, kk_t, a_t = inp
        sa = jnp.einsum('bhvk,bhk->bhv', S, kk_t)
        S = (S * w_t[:, :, None, :]
             - sa[..., None] * (kk_t * a_t)[:, :, None, :]
             + v_t[..., None] * k_t[:, :, None, :])
        return S, jnp.einsum('bhvk,bhk->bhv', S, r_t)

    xs = tuple(jnp.moveaxis(t, 1, 0) for t in (rh, wh, kh, vh, kk, ah))
    s_last, o = lax.scan(step, s0.astype(F32), xs)
    o = jnp.moveaxis(o, 0, 1)
    mu = jnp.mean(o, axis=-1, keepdims=True)
    var = jnp.mean(jnp.square(o - mu), axis=-1, keepdims=True)
    on = ((o - mu) * lax.rsqrt(var + GN_EPS)).reshape(B_, T, D_A)
    on = on * W['rwkv_lnx_w'] + W['rwkv_lnx_b']
    bonus = jnp.sum(rh * kh * W['rwkv_r_k'], axis=-1, keepdims=True) * vh
    out = (on + bonus.reshape(B_, T, D_A)) * g
    return out.astype(zs.dtype), s_last

def _complex_affine_combine(e1, e2):
    a1r, a1i, b1r, b1i = e1
    a2r, a2i, b2r, b2i = e2
    return (a2r * a1r - a2i * a1i, a2r * a1i + a2i * a1r,
            a2r * b1r - a2i * b1i + b2r, a2r * b1i + a2i * b1r + b2i)

def s5_mix(u, h0_re, h0_im, W):
    B_, T, _ = u.shape
    uf = u.astype(F32).reshape(B_, T, N_GROUPS_B, S5_GROUP)
    dt = jnp.exp(W['s5_log_dt'].astype(F32))[:, None]
    lr, li = W['s5_lam_re'].astype(F32), W['s5_lam_im'].astype(F32)
    mag = jnp.exp(lr * dt)
    ar, ai = mag * jnp.cos(li * dt), mag * jnp.sin(li * dt)
    den = lr * lr + li * li
    fr = ((ar - 1.0) * lr + ai * li) / den
    fi = (ai * lr - (ar - 1.0) * li) / den
    b_re, b_im = W['s5_b_re'].astype(F32), W['s5_b_im'].astype(F32)
    bb_re = fr[..., None] * b_re - fi[..., None] * b_im
    bb_im = fr[..., None] * b_im + fi[..., None] * b_re
    bu_re = jnp.einsum('btgn,gpn->btgp', uf, bb_re)
    bu_im = jnp.einsum('btgn,gpn->btgp', uf, bb_im)
    a_re = jnp.broadcast_to(ar, (1, T) + ar.shape)
    a_im = jnp.broadcast_to(ai, (1, T) + ai.shape)
    A_re, A_im, H_re, H_im = lax.associative_scan(
        _complex_affine_combine, (a_re, a_im, bu_re, bu_im), axis=1)
    h0r, h0i = h0_re.astype(F32)[:, None], h0_im.astype(F32)[:, None]
    hr = H_re + A_re * h0r - A_im * h0i
    hi = H_im + A_re * h0i + A_im * h0r
    y = (jnp.einsum('btgp,gnp->btgn', hr, W['s5_c_re'].astype(F32))
         - jnp.einsum('btgp,gnp->btgn', hi, W['s5_c_im'].astype(F32))
         + W['s5_d'].astype(F32) * uf)
    y = jax.nn.gelu(y).reshape(B_, T, D_B)
    out = y * jax.nn.sigmoid(y @ W['s5_w_glu'].astype(F32) + W['s5_b_glu'].astype(F32))
    return out.astype(u.dtype), hr[:, -1], hi[:, -1]

def rwkv_s5_mixer(h, shift_prev, wkv_prev, sre_prev, sim_prev, W):
    z = h @ W['w_in_ab']
    za, u = z[..., :D_A_PROJ], z[..., D_A_PROJ:]
    za_prev = jnp.concatenate([shift_prev[:, None, :].astype(za.dtype), za[:, :-1]], axis=1)
    zs = za + W['rwkv_mu'] * (za_prev - za)
    y_a, wkv_new = rwkv7_time_mix(zs, wkv_prev, W)
    y_b, sre_new, sim_new = s5_mix(u, sre_prev, sim_prev, W)
    return jnp.concatenate([y_a, y_b], axis=-1), za[:, -1], wkv_new, sre_new, sim_new

def diff_weights(s, lam):
    p = jax.nn.softmax(s, axis=-1)
    return p[:, :, 0] - lam * p[:, :, 1]

def attend_prompt(q, k, v, lam):
    B_, T = q.shape[:2]
    nb = T // Q_BLOCK
    qb = jnp.moveaxis((q.astype(F32) * SCALE_C).reshape(B_, nb, Q_BLOCK, N_HEADS_C, 2, HALF_C), 1, 0)
    kf, vf = k.astype(F32), v.astype(F32)
    kpos = jnp.arange(T)

    def one_block(args):
        q_blk, i = args
        s = jnp.einsum('bqhcd,bkhcd->bhcqk', q_blk, kf)
        qpos = i * Q_BLOCK + jnp.arange(Q_BLOCK)
        s = jnp.where(kpos[None, :] <= qpos[:, None], s, NEG_INF)
        return jnp.einsum('bhqk,bkhd->bqhd', diff_weights(s, lam), vf)

    o = lax.map(one_block, (qb, jnp.arange(nb)))
    return jnp.moveaxis(o, 0, 1).reshape(B_, T, N_HEADS_C, HEAD_C)

def attend_sample(q, k, v, lam, k_past, v_past):
    B_, T = q.shape[:2]
    P = k_past.shape[1]
    qf = q.astype(F32) * SCALE_C
    kp = k_past.astype(F32).reshape(B_, P, N_HEADS_C, 2, HALF_C)
    s_past = jnp.einsum('bqhcd,bkhcd->bhcqk', qf, kp)
    s_new = jnp.einsum('bqhcd,bkhcd->bhcqk', qf, k.astype(F32))
    s_new = jnp.where(jnp.tril(jnp.ones((T, T), dtype=bool)), s_new, NEG_INF)
    a = diff_weights(jnp.concatenate([s_past, s_new], axis=-1), lam)
    return (jnp.einsum('bhqk,bkhd->bqhd', a[..., :P], v_past.astype(F32))
            + jnp.einsum('bhqk,bkhd->bqhd', a[..., P:], v.astype(F32)))

def diff_attn_mixer(h, lam, attend, W):
    B_, T, _ = h.shape
    q, k, v = jnp.split(h @ W['diff_w_qkv'], 3, axis=-1)
    q = q.reshape(B_, T, N_HEADS_C, 2, HALF_C)
    k = k.reshape(B_, T, N_HEADS_C, 2, HALF_C)
    v = v.reshape(B_, T, N_HEADS_C, HEAD_C)
    o = attend(q, k, v, lam)
    o = (o * lax.rsqrt(jnp.mean(o * o, axis=-1, keepdims=True) + RMS_EPS)
         * W['diff_subln'].astype(F32) * (1.0 - LAMBDA_INIT))
    return o.reshape(B_, T, D_MIX).astype(h.dtype), k.reshape(B_, T, N_HEADS_C, HEAD_C), v

def trunk(x, c, shift0, wkv0, sre0, sim0, attend, W):
    lam = (jnp.exp(jnp.sum(W['diff_lq1'].astype(F32) * W['diff_lk1'].astype(F32)))
           - jnp.exp(jnp.sum(W['diff_lq2'].astype(F32) * W['diff_lk2'].astype(F32))) + LAMBDA_INIT)
    cond = jax.nn.silu(c)
    for layer in range(DEPTH):
        mod = cond @ W['w_ada'][layer] + W['b_ada'][layer]
        sh_m, sc_m, g_m, sh_f, sc_f, g_f = jnp.split(mod[:, None, :], 6, axis=-1)
        h = rmsnorm(x, W['norm_mix'][layer]) * (1.0 + sc_m) + sh_m
        if layer % 2 == 0:
            y, shift1, wkv1, sre1, sim1 = rwkv_s5_mixer(h, shift0, wkv0, sre0, sim0, W)
        else:
            y, k_rows, v_rows = diff_attn_mixer(h, lam, attend, W)
        x = x + g_m * (y @ W['w_out'][layer])
        h = rmsnorm(x, W['norm_mlp'][layer]) * (1.0 + sc_f) + sh_f
        x = x + g_f * (jnp.square(jax.nn.relu(h @ W['w_up'][layer])) @ W['w_down'][layer])
    return rmsnorm(x, W['norm_f']), shift1, wkv1, sre1, sim1, k_rows, v_rows

def setup_inputs(seed: int = 0) -> dict:
    key = jax.random.key(seed)
    keys = iter(jax.random.split(key, 64))

    def nrm(shape, scale):
        return scale * jax.random.normal(next(keys), shape, jnp.float32)

    def gain(shape):
        return 1.0 + nrm(shape, 0.1)

    n_pages = PAST_LEN // PAGE_SIZE
    n_used = DEC_BATCH * n_pages
    n_pool = (5 * n_used + 3) // 4
    page_table = jax.random.permutation(next(keys), n_pool)[:n_used].reshape(DEC_BATCH, n_pages).astype(jnp.int32)
    lam_im = (jnp.pi * jnp.broadcast_to(jnp.arange(S5_STATE, dtype=jnp.float32), (N_GROUPS_B, S5_STATE))
              + nrm((N_GROUPS_B, S5_STATE), 0.01))
    log_dt = jax.random.uniform(next(keys), (N_GROUPS_B,), jnp.float32, math.log(1e-3), math.log(1e-1))
    return {
        'x_prompt': nrm((BATCH, SEQ, D_MODEL), 1.0),
        'x_sample': nrm((DEC_BATCH, DEC_SEQ, D_MODEL), 1.0),
        'state_shift': nrm((DEC_BATCH, D_A_PROJ), 1.0),
        'state_wkv': nrm((DEC_BATCH, N_HEADS_A, HEAD_A, HEAD_A), 0.1),
        'state_ssm_re': nrm((DEC_BATCH, N_GROUPS_B, S5_STATE), 0.1),
        'state_ssm_im': nrm((DEC_BATCH, N_GROUPS_B, S5_STATE), 0.1),
        'cache_k': nrm((n_pool, PAGE_SIZE, N_HEADS_C, HEAD_C), 1.0),
        'cache_v': nrm((n_pool, PAGE_SIZE, N_HEADS_C, HEAD_C), 1.0),
        'page_table': page_table,
        'c_prompt': nrm((BATCH, D_MODEL), 1.0),
        'c_sample': nrm((DEC_BATCH, D_MODEL), 1.0),
        'norm_mix': gain((DEPTH, D_MODEL)),
        'norm_mlp': gain((DEPTH, D_MODEL)),
        'norm_f': gain((D_MODEL,)),
        'w_ada': nrm((DEPTH, D_MODEL, 6 * D_MODEL), 0.5 * D_MODEL ** -0.5),
        'b_ada': nrm((DEPTH, 6 * D_MODEL), 0.02),
        'w_out': nrm((DEPTH, D_MIX, D_MODEL), D_MIX ** -0.5),
        'w_up': nrm((DEPTH, D_MODEL, D_FF), D_MODEL ** -0.5),
        'w_down': nrm((DEPTH, D_FF, D_MODEL), D_FF ** -0.5),
        'w_in_ab': nrm((D_MODEL, D_IN_AB), D_MODEL ** -0.5),
        'rwkv_mu': jax.random.uniform(next(keys), (D_A_PROJ,), jnp.float32),
        'rwkv_w0': nrm((D_A,), 0.5),
        'rwkv_w_up': nrm((LORA_W, D_A), LORA_W ** -0.5),
        'rwkv_a0': nrm((D_A,), 0.5),
        'rwkv_a_up': nrm((LORA_A, D_A), LORA_A ** -0.5),
        'rwkv_g_up': nrm((LORA_G, D_A), LORA_G ** -0.5),
        'rwkv_k_k': gain((D_A,)),
        'rwkv_k_a': gain((D_A,)),
        'rwkv_r_k': nrm((N_HEADS_A, HEAD_A), 0.1),
        'rwkv_lnx_w': gain((D_A,)),
        'rwkv_lnx_b': nrm((D_A,), 0.01),
        's5_lam_re': -0.5 + nrm((N_GROUPS_B, S5_STATE), 0.01),
        's5_lam_im': lam_im,
        's5_log_dt': log_dt,
        's5_b_re': nrm((N_GROUPS_B, S5_STATE, S5_GROUP), S5_GROUP ** -0.5),
        's5_b_im': nrm((N_GROUPS_B, S5_STATE, S5_GROUP), S5_GROUP ** -0.5),
        's5_c_re': nrm((N_GROUPS_B, S5_GROUP, S5_STATE), 0.5),
        's5_c_im': nrm((N_GROUPS_B, S5_GROUP, S5_STATE), 0.5),
        's5_d': nrm((N_GROUPS_B, S5_GROUP), 0.5),
        's5_w_glu': nrm((D_B, D_B), D_B ** -0.5),
        's5_b_glu': nrm((D_B,), 0.01),
        'diff_w_qkv': nrm((D_MODEL, 3 * D_MIX), D_MODEL ** -0.5),
        'diff_lq1': nrm((HALF_C,), 0.1),
        'diff_lk1': nrm((HALF_C,), 0.1),
        'diff_lq2': nrm((HALF_C,), 0.1),
        'diff_lk2': nrm((HALF_C,), 0.1),
        'diff_subln': gain((HEAD_C,)),
    }

def reference(x_prompt, x_sample, state_shift, state_wkv, state_ssm_re, state_ssm_im,
              cache_k, cache_v, page_table, c_prompt, c_sample,
              norm_mix, norm_mlp, norm_f, w_ada, b_ada, w_out, w_up, w_down,
              w_in_ab, rwkv_mu, rwkv_w0, rwkv_w_up, rwkv_a0, rwkv_a_up, rwkv_g_up,
              rwkv_k_k, rwkv_k_a, rwkv_r_k, rwkv_lnx_w, rwkv_lnx_b,
              s5_lam_re, s5_lam_im, s5_log_dt, s5_b_re, s5_b_im, s5_c_re, s5_c_im,
              s5_d, s5_w_glu, s5_b_glu,
              diff_w_qkv, diff_lq1, diff_lk1, diff_lq2, diff_lk2, diff_subln):
    W = dict(norm_mix=norm_mix, norm_mlp=norm_mlp, norm_f=norm_f, w_ada=w_ada, b_ada=b_ada,
             w_out=w_out, w_up=w_up, w_down=w_down, w_in_ab=w_in_ab,
             rwkv_mu=rwkv_mu, rwkv_w0=rwkv_w0, rwkv_w_up=rwkv_w_up, rwkv_a0=rwkv_a0,
             rwkv_a_up=rwkv_a_up, rwkv_g_up=rwkv_g_up, rwkv_k_k=rwkv_k_k, rwkv_k_a=rwkv_k_a,
             rwkv_r_k=rwkv_r_k, rwkv_lnx_w=rwkv_lnx_w, rwkv_lnx_b=rwkv_lnx_b,
             s5_lam_re=s5_lam_re, s5_lam_im=s5_lam_im, s5_log_dt=s5_log_dt,
             s5_b_re=s5_b_re, s5_b_im=s5_b_im, s5_c_re=s5_c_re, s5_c_im=s5_c_im,
             s5_d=s5_d, s5_w_glu=s5_w_glu, s5_b_glu=s5_b_glu,
             diff_w_qkv=diff_w_qkv, diff_lq1=diff_lq1, diff_lk1=diff_lk1,
             diff_lq2=diff_lq2, diff_lk2=diff_lk2, diff_subln=diff_subln)
    bp = x_prompt.shape[0]
    y_prompt, p_shift, p_wkv, p_ssm_re, p_ssm_im, p_k, p_v = trunk(
        x_prompt, c_prompt,
        jnp.zeros((bp, D_A_PROJ), x_prompt.dtype),
        jnp.zeros((bp, N_HEADS_A, HEAD_A, HEAD_A), F32),
        jnp.zeros((bp, N_GROUPS_B, S5_STATE), F32),
        jnp.zeros((bp, N_GROUPS_B, S5_STATE), F32),
        attend_prompt, W)
    db = page_table.shape[0]
    k_past = cache_k[page_table].reshape(db, -1, N_HEADS_C, HEAD_C)
    v_past = cache_v[page_table].reshape(db, -1, N_HEADS_C, HEAD_C)
    attend_s = lambda q, k, v, lam: attend_sample(q, k, v, lam, k_past, v_past)
    y_sample, s_shift, s_wkv, s_ssm_re, s_ssm_im, s_k, s_v = trunk(
        x_sample, c_sample, state_shift, state_wkv, state_ssm_re, state_ssm_im, attend_s, W)
    return (y_prompt, y_sample, p_shift, p_wkv, p_ssm_re, p_ssm_im, p_k, p_v,
            s_shift, s_wkv, s_ssm_re, s_ssm_im, s_k, s_v)


_drawn_inputs = setup_inputs


def setup_inputs(seed=0):
    import zlib

    import numpy as np

    out = dict(_drawn_inputs(seed))
    spreads = {}
    factors = {'rwkv_lnx_w': 4.7,
     'rwkv_lnx_b': 37.097,
     's5_lam_re': 11.411,
     's5_w_glu': 3.528,
     's5_b_glu': 64.0,
     'diff_lk1': 29.72,
     'diff_lq2': 33.977,
     'diff_lk2': 46.528,
     'diff_subln': 2.781}
    for name, (base, spread) in spreads.items():
        noise = np.random.default_rng([zlib.crc32(name.encode()), seed]).standard_normal(out[name].shape)
        drawn = base * np.exp(spread * noise) if base else spread * noise
        out[name] = jnp.asarray(drawn.astype(out[name].dtype))
    for name, factor in factors.items():
        out[name] = (out[name] * factor).astype(out[name].dtype)
    return out
```

```python
import math
from contextlib import ExitStack

import numpy as np
import concourse.bass as bass
from concourse import mybir

F32 = mybir.dt.float32
I32 = mybir.dt.int32
ALU = mybir.AluOpType
ACT = mybir.ActivationFunctionType
AX = mybir.AxisListType

P = 128
D = 1024
KT = D // P
TP, NB, TS = 1024, 8, 4
NS = NB * TS
T = TP + NS
CH = T // 3
CHUNKS = [(i * CH, (i + 1) * CH) for i in range(3)]
TILES = [(i * P, P) for i in range(TP // P)] + [(TP, NS)]
N_PAIR = 4
ZT = 14
C64 = 64
N_G, G_CH, S_ST = 32, 16, 64
L8 = 8
NC8 = TP // L8
H_C, PAGE, N_PAGES, N_POOL = 8, 128, 16, 160
EPS, GN_EPS = 1e-6, 64e-5
DECAY = math.exp(-0.5)
LAM0 = 0.8 - 0.6 * math.exp(-0.3)
NEG = -1e30
TWO_PI_HI = 6.28125
TWO_PI_LO = 2 * math.pi - TWO_PI_HI
ROUND = 1.5 * 2.0 ** 23
PI_IN = 3.1415925

VEC = {}
for _name, _rows in (("norm_mix", 16), ("norm_mlp", 16), ("norm_f", 8), ("rwkv_mu", 14), ("rwkv_w0", 4),
                     ("rwkv_a0", 4), ("rwkv_k_k", 4), ("rwkv_k_a", 4), ("rwkv_r_k", 4), ("rwkv_lnx_w", 4),
                     ("rwkv_lnx_b", 4), ("s5_b_glu", 4), ("diff_subln", 1)):
    VEC[_name] = (sum(n for _, n in VEC.values()), _rows)
N_VEC = sum(n for _, n in VEC.values())
SH_M, SC_M, G_M, SH_F, SC_F, G_F = range(0, 48, 8)

AT_ADA, AT_IN = 0, 48
AT_PAIRS = AT_IN + 1
AT_U = AT_PAIRS + 2 * N_PAIR
AT_GLU = AT_U + 2
AT_OUT = [AT_GLU + 1, None]
AT_MLP = [AT_OUT[0] + 4, None]
AT_QKV = AT_MLP[0] + 32
AT_OUT[1] = AT_QKV + 12
AT_MLP[1] = AT_OUT[1] + 4
N_ITEMS = AT_MLP[1] + 32


def weight_stream(w):
    def dense(src, k0, c0, n):
        return [[(src[k0:k0 + 1024, :], c0 + i * 256, 256)] for i in range(n)]

    def mlp(layer):
        return [x for q in range(4)
                for x in dense(w["w_up"][layer], 0, q * 1024, 4) + dense(w["w_down"][layer], q * 1024, 0, 4)]

    w_in = w["w_in_ab"]
    items = dense(w["w_ada"][0], 0, 0, 24) + dense(w["w_ada"][1], 0, 0, 24) + dense(w_in, 0, 1536, 1)
    for j in range(N_PAIR):
        items.append([(w_in, j * P, P), (w_in, 512 + j * P, P)])
        items.append([(w_in, 1024 + j * P, P)])
    items += dense(w_in, 0, 1792, 2) + [[(w["s5_w_glu"], 0, 512)]]
    items += dense(w["w_out"][0], 0, 0, 4) + mlp(0)
    items += dense(w["diff_w_qkv"], 0, 0, 12)
    items += dense(w["w_out"][1], 0, 0, 4) + mlp(1)
    assert len(items) == N_ITEMS
    return items


KIND = {step: kind for kind, steps in {
    "start": "step masks consts cond_sig silu vecs_turned cond_turned condT lam_dots lam_exps xin_turned xin_copied "
             "mod_copied mod_turned mod_biased zb_zero",
    "norm": "squares squares_used std h_ready",
    "tile": "set_done set_free relu x_mid x_part x_ready hidden mixed weights_used zb_ready zb_used",
    "mix_in": "lora_ready sg_ready lw_sig a_ready g_ready kk_sq rk_prod lx e_lx e_l e_nl kk_norm gn_std s0_turned s0_copied "
              "sfin_turned sout_ready gn_sq mix_ready",
    "chunk": "tm_turned tm_ready grams gram_masked d2 d2_copied d4 d4_copied d8 d8_copied f4p f_level level_p1 "
             "level_copied level_p2 akkv m_ready rhs_ready xy xy_copied zq zq_copied tt tt_ready rw_free o_sample "
             "o_ready mb_ready tts tts_ready states_new states_final",
    "state": "state state_new",
    "s5": "shift_turned shout_ready u_done u_copied s5_turned crow_turned crow_copied ut_turned ut_copied toeplitz "
          "etx_copied ety_turned ety_copied left h_states y_done gelu_done y_turned y_copied s5_states_turned "
          "sfin_rows d_rows dt_exp angles s5_funcs powers glu_sig glu_used usa_zero",
    "attend": "v_done v_copied qs_saved k_turned k_copied scores scores_free row_max probs pt_turned pt_copied o_done "
              "o_copied",
    "sample": "qpad_zero qpad s_new page_turned page_copied page_scored page_used s_max s_exp s_coef pts_done "
              "pts_copied os_ready os_copied os_turned os_done o_sq o_std o_normed",
    "rows": "y_row_turned y_row_copied",
}.items() for step in steps.split()}


class Ledger:

    def __init__(self, nc, ctx, known):
        self.nc, self.ctx, self.known = nc, ctx, known
        self.sems, self.count, self.at = {}, {}, {}

    def sem(self, name):
        if name not in self.sems:
            self.sems[name] = self.ctx.enter_context(self.nc.semaphore(name))
        return self.sems[name]

    def sig(self, engine, *steps, by=1):
        name = f"{engine}_{KIND.get(steps[0][0], steps[0][0])}"
        self.count[name] = self.count.get(name, 0) + by
        for step in steps:
            self.at[step] = (name, self.count[name])
        return self.sem(name), by

    def when(self, *step):
        if self.known is None:
            return self.sem("first_build"), 1
        name, value = self.known[step]
        return self.sem(name), value

    def own(self, engine, step):
        name = f"{engine}_{KIND.get(step[0], step[0])}"
        return self.sem(name), self.count[name]


class Region:

    def __init__(self, buf, size):
        self.buf, self.size, self.at = buf, size, 0

    def take(self, *shape, parts=P):
        n = int(np.prod(shape))
        assert self.at + n <= self.size, (self.at, n, self.size)
        ap = self.buf[0:parts, self.at:self.at + n]
        self.at += n
        if len(shape) == 1:
            return ap
        names = " ".join(f"d{i}" for i in range(len(shape)))
        return ap.rearrange(f"p ({names}) -> p {names}", **{f"d{i}": s for i, s in enumerate(shape)})


def mid(ap, n):
    return ap.unsqueeze(1).to_broadcast([ap.shape[0], n, ap.shape[1]])


def rep(ap, n):
    return ap.unsqueeze(len(ap.shape)).to_broadcast(list(ap.shape) + [n])


def smp(ap):
    return ap[:, TP:T].rearrange("p (b q) -> p b q", q=TS)


S5_ROWS = ("LOGDT", "LI", "DT", "AR", "AI", "MAG8", "FR", "FI", "C1", "S1", "A4R", "A4I", "P8C", "P8S", "LR", "DC",
           "TH", "W1", "W2", "W3", "W4")
U16, U32, U64, UI64, L16, L32, L64, NUI64, CAUSAL = range(9)
U4, UI4, L4, NUI4 = range(4)
GROUPS = [(g, [(2 * g * P, P), (2 * g * P + P, P)], P) for g in range(4)] + [(4, [(TP, NS)], NS)]


class Memory:

    def __init__(self, nc, ctx):
        def sb(name, shape, dt=F32):
            return ctx.enter_context(nc.sbuf_tensor(name, shape, dt))

        def tiles(buf):
            return buf[:, 0:KT * T].rearrange("p (k t) -> p k t", t=T)

        self.xbuf, self.hbuf, self.mbuf = (sb(n, [P, KT * T]) for n in ("xbuf", "hbuf", "mbuf"))
        self.xT, self.hT, self.mT = tiles(self.xbuf), tiles(self.hbuf), tiles(self.mbuf)
        self.ring = sb("ring", [P, 4, 2048])
        WORK = 15900
        work = self.work = sb("work", [P, WORK])
        self.ident, self.mean1, self.bd1 = (sb(n, [P, P]) for n in ("ident", "mean1", "bd1"))
        self.msk = sb("msk", [P, 9, P])
        self.msk4 = sb("msk4", [NS, 4, NS])
        self.vecT = sb("vecT", [P, P])
        self.bT = sb("bT", [P, 96])
        self.modT = sb("modT", [P, 2, 48, 9])
        self.gain = sb("gain", [P, 2, 2, KT, 9])
        self.condT = sb("condT", [P, KT, 9])
        self.shiftT = sb("shiftT", [P, ZT, NB])
        self.lastz = sb("lastz", [P, ZT, 9])
        self.lam = sb("lam", [P, 8])
        self.eps = sb("eps", [P, 2])
        self.banks = ctx.enter_context(nc.psum_tensor("banks", [P, 8, 512], F32))
        self.spill = nc.dram_tensor("x_spill", (P, KT * T), F32, kind="Internal").ap()

        h = self.hbuf
        self.vrows = h[:, 7100:7228]
        self.brows, self.crows, self.csig = h[0:96, 0:P], h[0:9, 1024:2048], h[0:9, 6000:7024]
        self.srows = h[0:8, 2048:2048 + ZT * P]
        self.lrows = h[0:1, 4096:4352]
        self.modrow = h[0:9, 4608:4864]
        self.sq = work[:, 0:2 * T].rearrange("p (i t) -> p i t", i=2)
        self.rstd = work[:, 2 * T:3 * T]

        r = Region(work, WORK)
        self.zb = r.take(1025 + 40)
        chunkwise = Region(work[:, 8:8 + 1024], 1024)
        self.XY, self.ZTt, self.QTt = chunkwise.take(2, 2, 2, C64), chunkwise.take(2, P), chunkwise.take(2, P)
        self.lora, self.sgd = r.take(T), r.take(T)
        self.lorw = r.take(2, 512)
        self.KR = r.take(2, T)
        self.Kf, self.Vf, self.Af, self.Gf, self.BON = (r.take(T) for _ in range(5))
        self.S0in = r.take(NB, P)
        self.SBD = r.take(9, P)
        self.PW = r.take(2, 4, P)
        self.TT = r.take(4, P)
        self.SOUT = r.take(9, C64)
        r = Region(self.xbuf, KT * T)
        self.LW, self.Lc, self.T1, self.KH, self.BH, self.rowm = (r.take(T) for _ in range(6))
        self.QO = self.LW
        self.WC = r.take(16 + 8)
        self.eb = r.take(NB)
        self.AKK, self.ARK, self.ARB = (r.take(4, P) for _ in range(3))
        self.RHS = r.take(2, 2, 2, C64)
        r = Region(self.mbuf[:, 4 * T:8 * T], 4 * T)
        self.TM = r.take(2, 4, P)
        self.Dd, self.Dt, self.FF, self.FT = (r.take(4, P) for _ in range(4))
        self.O32, self.O64 = r.take(4, P), r.take(4, P)
        self.MB = self.mbuf[:, 4 * T + 3072:4 * T + 4096].rearrange("p (b i f) -> p b i f", b=4, i=2)

        r = Region(self.xbuf, KT * T)
        self.U = r.take(N_G, L8, G_CH)
        self.yT = r.take(4, T)
        r = Region(work, WORK)
        self.UsA = r.take(N_G, 12, G_CH, parts=8)
        self.sT = r.take(T)
        self.BX, self.BY, self.CX, self.CY = (r.take(N_G, G_CH) for _ in range(4))
        self.h0 = r.take(2, NB, N_G)
        self.h4, self.hfin = r.take(NB, N_G), r.take(N_G)
        self.c = {name: r.take(N_G) for name in S5_ROWS}
        self.s5rows = r.take(4, P)
        self.rows2 = r.take(2, P)
        self.BBp = r.take(8, 15, G_CH)
        self.shout = self.BBp.rearrange("p a b c -> p (a b c)")[0:9, 0:ZT * P]
        self.phc = r.take(4, 8)
        self.Hs = r.take(8, NC8 + 1)
        self.COS = r.take(8, P)
        self.SIN = self.sT[:, 0:1024].rearrange("p (g c) -> p g c", g=8)
        r = Region(self.hbuf, KT * T)
        self.UT = r.take(8, 144)
        self.CAp, self.ABx, self.ABy = r.take(8, 16, G_CH), r.take(8, L8, G_CH), r.take(8, L8, G_CH)
        self.CYr, self.q1, self.q2 = r.take(8, G_CH), r.take(8, G_CH), r.take(8, G_CH)
        self.ETx, self.Tm = r.take(8, P), r.take(8, P)
        self.Yq = self.ETx
        self.Yqs = r.take(4, P, parts=NB)
        r = Region(self.mbuf[:, 4 * T:8 * T], 4 * T)
        self.ETy, self.G1, self.G2, self.q3 = (r.take(8, P) for _ in range(4))

        self.qT, self.kT, self.oT = self.mT, self.xT, self.hT
        r = Region(work, WORK)
        self.V = r.take(9, D)
        self.Pp = r.take(2, 2, D)
        self.PTp = r.take(8, P)
        self.kout = self.Pp.rearrange("p a b d -> p (a b) d")
        self.st = r.take(2, 16)
        self.kTs = r.take(KT, NS)
        self.sq2 = self.Pp.rearrange("p a b d -> p (a b d)")[:, 0:T]
        self.r2 = self.Pp.rearrange("p a b d -> p (a b d)")[:, T:3 * T].rearrange("p (i t) -> p i t", i=2)
        self.qTs, self.nmask, self.csel = r.take(KT, NS), r.take(15, 4), r.take(NS)
        r = Region(self.xbuf, KT * T)
        self.KTp = r.take(2, KT, P)
        self.Ps = r.take(2048 + NS, parts=64)
        self.PTs = r.take(17, NS)
        self.Os = r.take(D, parts=NS)
        self.Sn = r.take(NS, parts=64)
        self.Cm = r.take(NS, parts=64)
        self.qpad = r.take(2, 576)
        self.ss = r.take(16)
        self.sel4 = r.take(4)
        self.pt = sb("page_table_sb", [1, P], I32)

        self.yrow = self.mbuf[:, 0:2 * D].rearrange("p (i d) -> p i d", i=2)

    def mask(self, i, n=P):
        return self.msk4[:, i, :] if n == NS else self.msk[:, i, :]

    def vec(self, name, i=0):
        r = VEC[name][0] + i
        return self.vecT[:, r:r + 1]

    def slot(self, n):
        return self.ring[:, n % 4, :]

    def wblock(self, n, width=256, at=0):
        return self.slot(n)[:, at:at + 8 * width].rearrange("p (k m) -> p k m", k=8)

    def page(self, n):
        return self.ring[:, (n % 8) // 2, (n % 2) * 1024:(n % 2) * 1024 + 1024]


def decoder_step(nc, a, o, known):
    with ExitStack() as ctx:
        led = Ledger(nc, ctx, known)
        m = Memory(nc, ctx)
        block = ctx.enter_context(nc.Block())
        sync_program(nc, block, led, m, a, o)
        gpsimd_program(nc, block, led, m, a, o)
        tensor_program(nc, block, led, m)
        vector_program(nc, block, led, m)
        scalar_program(nc, block, led, m)
        return led.at


def sync_program(nc, block, led, m, a, o):
    sig, when = led.sig, led.when

    @block.sync
    def _(sp):
        def load(dst, src, step):
            sp.dma_start(dst, src).then_inc(*sig("dma", step, by=16))

        for name, (r, n) in VEC.items():
            src = a[name]
            if len(src.shape) == 2:
                src = src.rearrange("a b -> (a b)")
            load(m.vrows[r:r + n, :], src.rearrange("(r c) -> r c", c=P), ("params_in",))
        load(m.brows, a["b_ada"].rearrange("l (r c) -> (l r) c", c=P), ("params_in",))
        load(m.crows[0:1, :], a["c_prompt"], ("params_in",))
        load(m.crows[1:9, :], a["c_sample"], ("params_in",))
        load(m.srows, a["state_shift"], ("params_in",))
        load(m.lorw[0:64, 0, :], a["rwkv_w_up"], ("params_in",))
        load(m.lorw[64:128, 0, :], a["rwkv_a_up"], ("params_in",))
        load(m.lorw[:, 1, :], a["rwkv_g_up"], ("params_in",))
        load(m.pt[:, :], a["page_table"].rearrange("b (o n) -> o (b n)", o=1), ("params_in",))
        for i, n in enumerate(("diff_lq1", "diff_lk1", "diff_lq2", "diff_lk2")):
            load(m.lrows[:, 64 * i:64 * i + 64], a[n].rearrange("(o c) -> o c", o=1), ("params_in",))

        stream = weight_stream(a)

        def weights(first, last):
            for n in range(first, last):
                if n >= 4:
                    sp.wait_ge(*when("weights_used", n - 4))
                if n == AT_OUT[1]:
                    sp.wait_ge(*when("pages_done"))
                at = 0
                for src, c0, cols in stream[n]:
                    kt = src.shape[0] // P
                    dst = m.slot(n)[:, at:at + kt * cols].rearrange("p (k c) -> p k c", k=kt)
                    sp.dma_start(dst, src[:, c0:c0 + cols].rearrange("(k p) c -> p k c", p=P)) \
                      .then_inc(*sig(f"slot{n % 4}", ("weights_in", n), by=16))
                    at += kt * cols

        for i, (t0, n) in enumerate(TILES):
            if i >= 2:
                sp.wait_ge(*when("xin_used", i - 2))
            src = a["x_prompt"][0, t0:t0 + n, :] if i < 8 else a["x_sample"].rearrange("b q d -> (b q) d")
            sp.dma_start(m.yrow[0:n, i % 2, :], src).then_inc(*sig(f"slot{i % 2}", ("xin", i), by=16))
        sp.wait_ge(*when("x_ready", 0))
        sp.dma_start(m.spill, m.xbuf[:, :]).then_inc(*sig("dma", ("spilled", 0), by=16))
        weights(0, AT_GLU + 1)
        sp.wait_ge(*when("mixed", 0))
        sp.dma_start(m.xbuf[:, :], m.spill).then_inc(*sig("dma", ("x_back", 0), by=16))
        weights(AT_GLU + 1, AT_QKV)
        sp.wait_ge(*when("x_ready", 1))
        sp.dma_start(m.spill, m.xbuf[:, :]).then_inc(*sig("dma", ("spilled", 1), by=16))
        weights(AT_QKV, AT_OUT[1])
        for b in range(NB):
            for kind, cache in enumerate(("cache_k", "cache_v")):
                for p in range(N_PAGES):
                    n = (b * 2 + kind) * N_PAGES + p
                    if n < 8:
                        sp.wait_ge(*when("weights_used", AT_OUT[1] - 4 + n // 2))
                    else:
                        sp.wait_ge(*when("page_used", n - 8))
                    i = b * N_PAGES + p
                    page = sp.value_load(m.pt[0:1, i:i + 1], min_val=0, max_val=N_POOL - 1)
                    sp.dma_start(m.page(n), a[cache][bass.ds(page, 1)].rearrange("o t h d -> (o t) (h d)")) \
                      .then_inc(*sig(f"page{n % 8}", ("page_in", n), by=16))
        sp.wait_ge(*when("attention_done"))
        sp.dma_start(m.xbuf[:, :], m.spill).then_inc(*sig("dma", ("x_back", 1), by=16))
        weights(AT_OUT[1], N_ITEMS)


def gpsimd_program(nc, block, led, m, a, o):
    sig, when = led.sig, led.when

    @block.gpsimd
    def _(pool):
        def do(ins, *steps):
            steps = steps or (("step",),)
            ins.then_inc(*sig("pool", *steps))
            pool.wait_ge(*led.own("pool", steps[0]))

        def sel(ap, op, base, pattern, cm, fill=0.0):
            do(nc.gpsimd.affine_select(out=ap, in_=ap, compare_op=op, fill=fill, base=base,
                                       pattern=pattern, channel_multiplier=cm))

        def dma(dst, src, step):
            pool.dma_start(dst, src).then_inc(*sig("pooldma", step, by=16))

        do(nc.gpsimd.memset(m.ident[:, :], 0.0))
        sel(m.ident[:, :], ALU.not_equal, 0, [[-1, P]], 1, fill=1.0)
        do(nc.gpsimd.memset(m.mean1[:, :], 1.0 / D))
        do(nc.gpsimd.memset(m.msk[:, :, :], 1.0))
        do(nc.gpsimd.memset(m.bd1[:, :], 1.0))
        do(nc.gpsimd.memset(m.msk[:, CAUSAL, :], 0.0))

        do(nc.gpsimd.memset(m.msk4[:, :, :], 1.0))

        def block_diagonal(ap, n):
            blocks = ap.shape[1] // n
            v = ap.rearrange("p (b c) -> p b c", c=n)
            sel(v, ALU.is_ge, 0, [[-n, blocks], [0, n]], 1)
            sel(v, ALU.is_ge, n - 1, [[n, blocks], [0, n]], -1)

        block_diagonal(m.bd1[:, :], C64)
        for mk, n, kind in ([(m.msk[:, i, :], n, kind) for i, n, kind in
                             ((U16, 16, "u"), (U32, 32, "u"), (U64, 64, "u"), (UI64, 64, "ui"), (L16, 16, "l"),
                              (L32, 32, "l"), (L64, 64, "l"))] +
                            [(m.msk4[:, i, :], 4, kind) for i, kind in ((U4, "u"), (UI4, "ui"), (L4, "l"))]):
            cols = mk.shape[1]
            block_diagonal(mk, n)
            if kind == "u":
                sel(mk, ALU.is_gt, 0, [[1, cols]], -1)
            elif kind == "ui":
                sel(mk, ALU.is_ge, 0, [[1, cols]], -1)
            else:
                sel(mk, ALU.is_gt, 0, [[-1, cols]], 1)
        sel(m.msk[:, CAUSAL, :], ALU.is_ge, 0, [[-1, P]], 1, fill=NEG)
        do(nc.gpsimd.memset(m.eps[:, 0:1], EPS))
        do(nc.gpsimd.memset(m.eps[:, 1:2], GN_EPS), ("masks",))
        pool.wait_ge(*when("h_ready", 0, 0))
        do(nc.gpsimd.memset(m.zb[:, 0:1], 0.0), ("zb_zero",))
        do(nc.gpsimd.memset(m.S0in[:, :, :], 0.0))
        for j in range(N_PAIR):
            if j:
                pool.wait_ge(*when("s0_turned", j - 1))
            for hh in range(2):
                dma(m.S0in[64 * hh:64 * hh + 64, :, 64 * hh:64 * hh + 64],
                    a["state_wkv"][:, 2 * j + hh].rearrange("b v k -> v b k"), ("s0_in", j))
            pool.wait_ge(*when("sout_ready", j))
            dma(o["p_wkv"][0, 2 * j:2 * j + 2].rearrange("h v k -> (h v) k"), m.SOUT[:, 0, :], ("sout_out", j))
            dma(o["s_wkv"][:, 2 * j:2 * j + 2].rearrange("b h v k -> (h v) b k"), m.SOUT[:, 1:9, :], ("sout_out", j))

        pool.wait_ge(*when("mix_ready", N_PAIR - 1))
        pool.wait_ge(*when("sout_out", N_PAIR - 1))
        do(nc.gpsimd.memset(m.UsA, 0.0), ("usa_zero",))
        for h in range(2):
            dma(m.s5rows[0:32, 0, 64 * h:64 * h + 64], a["s5_lam_re"], ("s5_in",))
            dma(m.s5rows[0:32, 1, 64 * h:64 * h + 64], a["s5_lam_im"], ("s5_in",))
            hs = slice(64 * h, 64 * h + 64)
            for dst, src in ((m.BX, ("s5_b_re", "s5_b_im")[h]), (m.BY, ("s5_b_im", "s5_b_re")[h])):
                dma(dst[hs, :, :], a[src].rearrange("g p n -> p g n"), ("s5_in",))
        dma(m.c["LOGDT"], a["s5_log_dt"].rearrange("(o g) -> o g", o=1).to_broadcast([P, N_G]), ("s5_in",))
        dma(m.s5rows[0:32, 2, 0:16], a["s5_d"], ("s5_in",))
        for i in range(4):
            for v, (x, y) in enumerate((("s5_c_re", "s5_c_im"), ("s5_c_im", "s5_c_re"))):
                k = i * 2 + v
                if k >= 2:
                    pool.wait_ge(*when("crow_turned", k - 2))
                for h, src in enumerate((x, y)):
                    pool.dma_start(m.rows2[:, k % 2, 64 * h:64 * h + 64],
                                   a[src][8 * i:8 * i + 8].rearrange("g n p -> (g n) p")) \
                        .then_inc(*sig(f"rows{k % 2}", ("crow_in", k), by=16))
        for i in range(2):
            for v, (x, y) in enumerate((("re", "im"), ("im", "re"))):
                k = 8 + i * 2 + v
                pool.wait_ge(*when("crow_turned", k - 2))
                for h, src in enumerate((x, y)):
                    pool.dma_start(m.rows2[:, k % 2, 64 * h:64 * h + 64],
                                   a[f"state_ssm_{src}"][4 * i:4 * i + 4].rearrange("b g p -> (b g) p")) \
                        .then_inc(*sig(f"rows{k % 2}", ("crow_in", k), by=16))
        pool.wait_ge(*when("shout_ready"))
        dma(o["p_shift"], m.shout[0:1, :], ("shift_out",))
        dma(o["s_shift"], m.shout[1:9, :], ("shift_out",))
        for i in range(3):
            pool.wait_ge(*when("sfin_rows", i))
            for h, n in enumerate(("re", "im")):
                hs = slice(64 * h, 64 * h + 64)
                if i < 2:
                    dma(o[f"s_ssm_{n}"][4 * i:4 * i + 4].rearrange("b g p -> (b g) p"), m.s5rows[:, i, hs], ("s5_out",))
                else:
                    dma(o[f"p_ssm_{n}"][0], m.s5rows[0:32, 2, hs], ("s5_out",))
        for i, (t0, n) in enumerate(TILES):
            def rows(t):
                return t[0, t0:t0 + n].rearrange("t h d -> t (h d)")

            def srows(t):
                return t.rearrange("b q h d -> (b q) (h d)")
            pool.wait_ge(*when("v_rows", i))
            dma(rows(o["p_v"]) if i < 8 else srows(o["s_v"]), m.V[0:n, i, :], ("out",))
        for i, (t0, n) in enumerate(TILES):
            pool.wait_ge(*when("k_rows", i))
            dst = o["p_k"][0, t0:t0 + n].rearrange("t h d -> t (h d)") if i < 8 else \
                o["s_k"].rearrange("b q h d -> (b q) (h d)")
            pool.dma_start(dst, m.kout[0:n, i % 4, :]).then_inc(*sig(f"kout{i % 4}", ("k_out", i), by=16))
        for i, (t0, n) in enumerate(TILES):
            pool.wait_ge(*when("y_rows", i))
            dst = o["y_prompt"][0, t0:t0 + n, :] if i < 8 else o["y_sample"].rearrange("b q d -> (b q) d")
            pool.dma_start(dst, m.yrow[0:n, i % 2, :]).then_inc(*sig(f"yout{i % 2}", ("y_out", i), by=16))
        for i in (7, 8):
            pool.wait_ge(*when("y_out", i))
        for i in range(5, 9):
            pool.wait_ge(*when("k_out", i))
        pool.wait_ge(*when("out"))
        pool.wait_ge(*when("s5_out"))


def tensor_program(nc, block, led, m):
    sig, when = led.sig, led.when
    banks = m.banks

    @block.tensor
    def _(pe):
        def mm(out, lhsT, rhs, start=True, stop=True):
            return nc.tensor.matmul(out, lhsT, rhs, start=start, stop=stop)

        def tr(out, in_):
            k = in_.shape[0]
            return nc.tensor.transpose(out, in_, m.ident[0:k, 0:k])

        n_tile = [0]

        def ptile(lhs, rhs, kts=KT, used=None):
            n = n_tile[0]
            n_tile[0] += 1
            if n >= 2:
                pe.wait_ge(*when("set_free", n - 2))
            for k in range(kts):
                for c, (t0, t1) in enumerate(CHUNKS):
                    last = mm(banks[:, 3 * (n % 2) + c, 0:CH], lhs(k), rhs(k)[:, t0:t1], k == 0, k == kts - 1)
            last.then_inc(*sig("pe", ("set_done", n), *([("weights_used", used)] if used is not None else [])))

        def dense_tiles(n0, items, src):
            for n in range(n0, n0 + items):
                pe.wait_ge(*when("weights_in", n))
                for half in range(2):
                    w = m.wblock(n)[:, :, half * P:half * P + P]
                    ptile(lambda k: w[:, k, :], lambda k: src[:, k, :], used=n if half else None)

        pe.wait_ge(*when("consts"))
        pe.wait_ge(*when("params_in"))
        tr(banks[:, 0, 0:N_VEC], m.vrows[0:N_VEC, :])
        tr(banks[:, 0, 128:224], m.brows)
        for k in range(ZT):
            last = tr(banks[:, 2, k * NB:k * NB + NB], m.srows[:, k * P:k * P + P])
        last.then_inc(*sig("pe", ("vecs_turned",)))
        pe.wait_ge(*when("silu"))
        for k in range(KT):
            last = tr(banks[:, 1, k * 9:k * 9 + 9], m.crows[:, k * P:k * P + P])
        last.then_inc(*sig("pe", ("cond_turned",)))

        for i, (t0, n) in enumerate(TILES):
            pe.wait_ge(*when("xin", i))
            for half in range(2):
                if i:
                    pe.wait_ge(*when("xin_copied", i - 1, half))
                for q in range(4):
                    k = half * 4 + q
                    last = tr(banks[:, 6 + half, q * P:q * P + n], m.yrow[0:n, i % 2, k * P:k * P + P])
                last.then_inc(*sig("pe", ("xin_turned", i, half)))

        pe.wait_ge(*when("condT"))
        pe.wait_ge(*when("lam_exps"))
        mm(banks[:, 4, 0:2], m.mean1[0:1, :], m.lam[0:1, 2:4])
        for n in range(AT_ADA, AT_IN):
            pe.wait_ge(*when("weights_in", n))
            if n >= 2:
                pe.wait_ge(*when("mod_copied", n - 2))
            for k in range(KT):
                last = mm(banks[0:9, n % 2, 0:256], m.condT[:, k, :], m.wblock(n)[:, k, :], k == 0, k == KT - 1)
            last.then_inc(*sig("pe", ("weights_used", n)))
            pe.wait_ge(*when("mod_copied", n))
            if n >= 1:
                pe.wait_ge(*when("mod_biased", n - 1))
            for h in range(2):
                last = tr(banks[:, 3, h * 16:h * 16 + 9], m.modrow[:, h * P:h * P + P])
            last.then_inc(*sig("pe", ("mod_turned", n)))

        def norm_sums(tag):
            for k in range(KT):
                pe.wait_ge(*when("squares", tag, k))
                for c, (t0, t1) in enumerate(CHUNKS):
                    last = mm(banks[:, c, 0:CH], m.mean1[:, :], m.sq[:, k % 2, t0:t1], k == 0, k == KT - 1)
                last.then_inc(*sig("pe", ("squares_used", tag, k)))

        def free_banks():
            for n in (n_tile[0] - 2, n_tile[0] - 1):
                if n >= 0:
                    pe.wait_ge(*when("set_free", n))

        norm_sums((0, 0))
        pe.wait_ge(*when("h_ready", 0, 0))
        dense_tiles(AT_IN, 1, m.hT)
        for j in range(N_PAIR):
            rk, vv = AT_PAIRS + 2 * j, AT_PAIRS + 2 * j + 1
            pe.wait_ge(*when("weights_in", rk))
            ptile(lambda k: m.wblock(rk, P)[:, k, :], lambda k: m.hT[:, k, :])
            ptile(lambda k: m.wblock(rk, P, 1024)[:, k, :], lambda k: m.hT[:, k, :], used=rk)
            pe.wait_ge(*when("weights_in", vv))
            ptile(lambda k: m.wblock(vv, P)[:, k, :], lambda k: m.hT[:, k, :], used=vv)
            js = slice(j * P, j * P + P)
            pe.wait_ge(*when("lora_ready"))
            ptile(lambda k: m.lorw[0:64, 0, js], lambda k: m.lora[0:64, :], kts=1)
            ptile(lambda k: m.lorw[64:128, 0, js], lambda k: m.lora[64:128, :], kts=1)
            pe.wait_ge(*when("sg_ready"))
            ptile(lambda k: m.lorw[:, 1, js], lambda k: m.sgd, kts=1)
            pe.wait_ge(*when("kk_sq", j))
            ptile(lambda k: m.bd1[:, :], lambda k: m.T1, kts=1)
            pe.wait_ge(*when("rk_prod", j))
            ptile(lambda k: m.bd1[:, :], lambda k: m.T1, kts=1)
            pe.wait_ge(*when("s0_in", j))
            for b in range(NB):
                last = tr(banks[:, 6 + b // 4, (b % 4) * P:(b % 4) * P + P], m.S0in[:, b, :])
            last.then_inc(*sig("pe", ("s0_turned", j)))
            pe.wait_ge(*when("s0_copied", j))
            free_banks()
            for g, tl, n in GROUPS:
                tensor_rwkv_group(pe, led, m, mm, tr, j, g, tl, n)
            pe.wait_ge(*when("states_final", j))
            for i in range(9):
                last = tr(banks[:, i // 4, (i % 4) * P:(i % 4) * P + P], m.SBD[:, i, :])
            last.then_inc(*sig("pe", ("sfin_turned", j)))
            pe.wait_ge(*when("sout_ready", j))
            pe.wait_ge(*when("o_ready", j))
            ptile(lambda k: m.bd1[:, :], lambda k: m.QO, kts=1)
            pe.wait_ge(*when("gn_sq", j))
            ptile(lambda k: m.bd1[:, :], lambda k: m.T1, kts=1)

        free_banks()
        for k in range(ZT):
            last = tr(banks[0:9, k // 4, (k % 4) * P:(k % 4) * P + P], m.lastz[:, k, :])
        last.then_inc(*sig("pe", ("shift_turned",)))
        pe.wait_ge(*when("usa_zero"))
        pe.wait_ge(*when("shout_ready"))
        for half in range(2):
            n = AT_U + half
            pe.wait_ge(*when("weights_in", n))
            for q in range(12):
                i = half * 12 + q
                if i >= 4:
                    pe.wait_ge(*when("u_copied", i - 4))
                if q < 8:
                    out, cols = banks[:, i % 4, 0:256], slice(q, TP, L8)
                else:
                    out, cols = banks[0:NB, i % 4, 0:256], slice(TP + q - 8, T, TS)
                for k in range(KT):
                    last = mm(out, m.hT[:, k, cols], m.wblock(n)[:, k, :], k == 0, k == KT - 1)
                last.then_inc(*sig("pe", ("u_done", i), *([("weights_used", n)] if q == 11 else [])))
        pe.wait_ge(*when("s5_in"))
        pe.wait_ge(*when("d_rows"))
        for i in range(3):
            last = tr(banks[:, 6, i * 32:i * 32 + 32], m.s5rows[0:32, i, :])
        last.then_inc(*sig("pe", ("s5_turned",)))
        for k in range(12):
            pe.wait_ge(*when("crow_in", k))
            if k >= 2:
                pe.wait_ge(*when("crow_copied", k - 2))
            tr(banks[:, 4 + k % 2, 0:P], m.rows2[:, k % 2, :]).then_inc(*sig("pe", ("crow_turned", k)))

        for q in range(4):
            tensor_s5_quarter(pe, led, m, mm, tr, q)
        pe.wait_ge(*when("s5_states"))
        for i in range(2):
            tr(banks[:, 7, i * P:i * P + P], m.h4[:, 4 * i:4 * i + 4, :].rearrange("p b g -> p (b g)"))
        tr(banks[0:32, 7, 256:384], m.hfin).then_inc(*sig("pe", ("s5_states_turned",)))
        for part in range(3):
            pe.wait_ge(*when("y_copied", 3, part))
        pe.wait_ge(*when("weights_in", AT_GLU))
        for ft in range(4):
            w = m.slot(AT_GLU).rearrange("p (k c) -> p k c", k=4)
            ptile(lambda k: w[:, k, ft * P:ft * P + P], lambda k: m.yT[:, k, :], kts=4,
                  used=AT_GLU if ft == 3 else None)

        def out_and_mlp(layer):
            pe.wait_ge(*when("mixed", layer))
            dense_tiles(AT_OUT[layer], 4, m.mT if layer == 0 else m.oT)
            free_banks()
            norm_sums((layer, 1))
            pe.wait_ge(*when("h_ready", layer, 1))
            for q in range(4):
                dense_tiles(AT_MLP[layer] + 8 * q, 4, m.hT)
                pe.wait_ge(*when("hidden", layer, q))
                dense_tiles(AT_MLP[layer] + 8 * q + 4, 4, m.mT)
            free_banks()

        out_and_mlp(0)

        norm_sums((1, 0))
        pe.wait_ge(*when("h_ready", 1, 0))
        dense_tiles(AT_QKV, 8, m.hT)
        for n in range(AT_QKV + 8, AT_QKV + 12):
            pe.wait_ge(*when("weights_in", n))
            for i, (t0, cnt) in enumerate(TILES):
                e = (n - AT_QKV - 8) * 9 + i
                if e >= 2:
                    pe.wait_ge(*when("v_copied", e - 2))
                for k in range(KT):
                    last = mm(banks[0:cnt, 6 + e % 2, 0:256], m.hT[:, k, t0:t0 + cnt], m.wblock(n)[:, k, :],
                              k == 0, k == KT - 1)
                last.then_inc(*sig("pe", ("v_done", e), *([("weights_used", n)] if i == 8 else [])))
        free_banks()
        for i, (t0, cnt) in enumerate(TILES):
            for half in range(2):
                if i:
                    pe.wait_ge(*when("k_copied", i - 1, half))
                for qq in range(4):
                    last = tr(banks[0:cnt, half, qq * P:qq * P + P], m.kT[:, half * 4 + qq, t0:t0 + cnt])
                last.then_inc(*sig("pe", ("k_turned", i, half)))
        for half in range(2):
            pe.wait_ge(*when("k_copied", 8, half))
        for e in (34, 35):
            pe.wait_ge(*when("v_copied", e))
        steps = [(h, i) for h in range(H_C) for i in range(8)]

        def scores(s):
            h, i = steps[s]
            if s:
                pe.wait_ge(*when("scores_free", s - 1))
            for c in range(2):
                cs = slice(64 * c, 64 * c + 64)
                for k0 in range(0, (i + 1) * P, 512):
                    k1 = min(k0 + 512, (i + 1) * P)
                    last = mm(banks[:, 2 * c + k0 // 512, 0:k1 - k0], m.qT[cs, h, i * P:i * P + P], m.kT[cs, h, k0:k1])
            last.then_inc(*sig("pe", ("scores", s)))

        def values(s):
            h, i = steps[s]
            pe.wait_ge(*when("probs", s))
            for b0 in range(0, i + 1, 4):
                bank = 4 + b0 // 4
                if s:
                    pe.wait_ge(*when("pt_copied", s - 1))
                for kb in range(b0, min(b0 + 4, i + 1)):
                    last = tr(banks[:, bank, (kb % 4) * P:(kb % 4) * P + P], m.Pp[:, s % 2, 0, kb * P:kb * P + P])
            last.then_inc(*sig("pe", ("pt_turned", s)))
            pe.wait_ge(*when("pt_copied", s))
            if s >= 2:
                pe.wait_ge(*when("o_copied", s - 2))
            for kb in range(i + 1):
                last = mm(banks[:, 6 + s % 2, 0:P], m.V[:, kb, h * P:h * P + P], m.PTp[:, kb, :], kb == 0, kb == i)
            last.then_inc(*sig("pe", ("o_done", s)))

        scores(0)
        for s in range(len(steps)):
            if s + 1 < len(steps):
                scores(s + 1)
            values(s)
        tensor_sample_attention(pe, led, m, mm, tr)
        pe.wait_ge(*when("oT_done"))
        for h in range(H_C):
            pe.wait_ge(*when("o_sq", h))
            ptile(lambda k: m.mean1[:, :], lambda k: m.sq2, kts=1)
        out_and_mlp(1)
        norm_sums((2, 0))
        pe.wait_ge(*when("h_ready", 2, 0))
        for i, (t0, cnt) in enumerate(TILES):
            for half in range(2):
                if i:
                    pe.wait_ge(*when("y_row_copied", i - 1, half))
                for q in range(4):
                    last = tr(banks[0:cnt, 6 + half, q * P:q * P + P], m.hT[:, half * 4 + q, t0:t0 + cnt])
                last.then_inc(*sig("pe", ("y_row_turned", i, half)))


def tensor_rwkv_group(pe, led, m, mm, tr, j, g, tl, n):
    sig, when = led.sig, led.when
    banks = m.banks
    nt, sample = len(tl), n == NS
    units = [(t, h) for t in range(nt) for h in range(2)]
    Dd, Dt, FF, FT, PW, TM, XY, KR = m.Dd, m.Dt, m.FF, m.FT, m.PW, m.TM, m.XY, m.KR

    def cell(bank, i, rows=n, cols=n):
        return banks[0:rows, bank, i * P:i * P + cols]

    if g:
        pe.wait_ge(*when("rw_free", j, g))
    for t, (t0, _) in enumerate(tl):
        for i, src in enumerate((m.KH, m.BH, m.Vf, KR[:, 0, :])):
            last = tr(cell(t, i, n, P), src[:, t0:t0 + n])
    last.then_inc(*sig("pe", ("tm_turned", j, g)))
    for h in range(2):
        hs = slice(64 * h, 64 * h + 64)
        for t, (t0, _) in enumerate(tl):
            both = KR[hs, :, t0:t0 + n]

            def two(bank):
                return banks[0:n, bank, t * 256:t * 256 + 256].rearrange("p (i t) -> p i t", i=2)[:, :, 0:n]
            mm(two(2 + h), m.Kf[hs, t0:t0 + n], both)
            mm(two(4 + h), m.Af[hs, t0:t0 + n], both)
            last = mm(cell(6 + h, t), KR[hs, 0, t0:t0 + n], m.Af[hs, t0:t0 + n])
    last.then_inc(*sig("pe", ("grams", j, g)))
    pe.wait_ge(*when("tm_ready", j, g))
    pe.wait_ge(*when("gram_masked", j, g))
    for i in range(2 * nt):
        mm(cell(0, i), Dt[0:n, i, 0:n], Dd[0:n, i, 0:n])
        last = mm(cell(1, i), Dd[0:n, i, 0:n], Dt[0:n, i, 0:n])
    last.then_inc(*sig("pe", ("d2", j, g)))
    pe.wait_ge(*when("d2_copied", j, g))
    for i in range(2 * nt):
        last = mm(cell(7, i), PW[0:n, 0, i, 0:n], FF[0:n, i, 0:n])
        if not sample:
            mm(cell(2, i), PW[:, 1, i, :], PW[:, 0, i, :])
            last = mm(cell(3, i), PW[:, 0, i, :], PW[:, 1, i, :])
    last.then_inc(*sig("pe", ("d4", j, g)))
    if not sample:
        pe.wait_ge(*when("d4_copied", j, g))
        for i in range(4):
            mm(cell(7, i), PW[:, 0, i, :], FF[:, i, :])
            last = mm(cell(0, i), PW[:, 1, i, :], PW[:, 0, i, :])
        last.then_inc(*sig("pe", ("d8", j, g)))
        pe.wait_ge(*when("d8_copied", j, g))
        for i in range(4):
            last = mm(cell(7, i), PW[:, 0, i, :], FF[:, i, :])
        last.then_inc(*sig("pe", ("f4p", j, g)))
        for lv, off in ((0, m.O32), (1, m.O64)):
            pe.wait_ge(*when("f_level", j, g, lv))
            for i in range(4):
                tr(cell(1, i), FF[:, i, :])
                last = mm(cell(2, i), off[:, i, :], FF[:, i, :])
            last.then_inc(*sig("pe", ("level_p1", j, g, lv)))
            pe.wait_ge(*when("level_copied", j, g, lv))
            for i in range(4):
                last = mm(cell(3, i), FT[:, i, :], PW[:, 0, i, :])
            last.then_inc(*sig("pe", ("level_p2", j, g, lv)))
    for t, h in units:
        u = 2 * t + h
        last = mm(banks[0:n, 4, u * C64:u * C64 + C64], m.AKK[0:n, u, 0:n], TM[0:n, t, 2, h * C64:h * C64 + C64])
    last.then_inc(*sig("pe", ("akkv", j, g)))
    pe.wait_ge(*when("m_ready", j, g))
    pe.wait_ge(*when("rhs_ready", j, g))
    for t, h in units:
        last = mm(cell(5, 2 * t + h, n, P), FF[0:n, 2 * t + h, 0:n], m.RHS[0:n, t, h, :, :])
    last.then_inc(*sig("pe", ("xy", j, g)))
    pe.wait_ge(*when("xy_copied", j, g))
    for t in range(nt):
        def both_heads(bank):
            return banks[:, bank, 0:256].rearrange("p (h t) -> p h t", h=2)[:, :, 0:n]
        us = slice(2 * t, 2 * t + 2)
        mm(both_heads(t), XY[0:n, t, 0, :, :], m.ARB[0:n, us, 0:n])
        mm(both_heads(2 + t), TM[0:n, t, 2, :], m.ARK[0:n, us, 0:n], True, False)
        last = mm(both_heads(2 + t), XY[0:n, t, 1, :, :], m.ARB[0:n, us, 0:n], False, True)
    last.then_inc(*sig("pe", ("zq", j, g)))
    SBD, TT, ZTt = m.SBD, m.TT, m.ZTt
    if not sample:
        for t in range(2):
            for c in range(2):
                cs = slice(64 * c, 64 * c + 64)
                last = mm(cell(6 + c, t), XY[cs, t, 0, :, :], TM[cs, t, 1, :])
        last.then_inc(*sig("pe", ("tt", j, g)))
        pe.wait_ge(*when("zq_copied", j, g))
        pe.wait_ge(*when("tt_ready", j, g))
        for q in range(4):
            t, c = q // 2, q % 2
            cs = slice(64 * c, 64 * c + 64)
            if q:
                pe.wait_ge(*when("state", j, g, q))
            mm(banks[:, 5 + q % 2, 0:C64], SBD[:, 0, :], ZTt[:, t, 64 * c:64 * c + 64])
            mm(cell(4, q), TT[:, q, :], SBD[:, 0, :], True, False)
            mm(cell(4, q), TM[cs, t, 0, :], TM[cs, t, 2, :], False, False)
            last = mm(cell(4, q), TM[cs, t, 1, :], XY[cs, t, 1, :, :], False, True)
            last.then_inc(*sig("pe", ("state_new", j, g, q)))
    else:
        pe.wait_ge(*when("zq_copied", j, g))
        for b in range(NB):
            last = mm(banks[:, 0, b * TS:b * TS + TS], SBD[:, 1 + b, :], ZTt[:, 0, TS * b:TS * b + TS])
        last.then_inc(*sig("pe", ("o_sample", j)))
        for half in range(2):
            pe.wait_ge(*when("mb_ready", j, half))
            for q in range(4):
                last = mm(cell(6 + half, q, P, P), XY[0:NS, 0, 0, :, :], m.MB[0:NS, q, 1, :])
            last.then_inc(*sig("pe", ("tts", j, half)))
            pe.wait_ge(*when("tts_ready", j, half))
            for q in range(4):
                out = cell(4 + half, q, P, P)
                mm(out, TT[:, q, :], SBD[:, 1 + half * 4 + q, :], True, False)
                mm(out, m.MB[0:NS, q, 0, :], TM[0:NS, 0, 2, :], False, False)
                last = mm(out, m.MB[0:NS, q, 1, :], XY[0:NS, 0, 1, :, :], False, True)
            last.then_inc(*sig("pe", ("states_new", j, half)))


def tensor_s5_quarter(pe, led, m, mm, tr, q):
    sig, when = led.sig, led.when
    banks = m.banks
    pe.wait_ge(*when("u_copied", 23))
    if q:
        for part in range(3):
            pe.wait_ge(*when("y_copied", q - 1, part))
    for gg in range(8):
        g, c0 = 8 * q + gg, (gg % 2) * 256
        tr(banks[:, gg // 2, c0:c0 + P], m.U[:, g, :, :].rearrange("p j n -> p (j n)"))
        tr(banks[:, gg // 2, c0 + 128:c0 + 136], m.UsA[:, g, 4:12, :].rearrange("p j n -> p (j n)"))
        last = tr(banks[:, gg // 2, c0 + 136:c0 + 144], m.UsA[:, g, 0:8, :].rearrange("p j n -> p (j n)"))
    last.then_inc(*sig("pe", ("ut_turned", q)))
    pe.wait_ge(*when("powers", q))
    for gg in range(8):
        for j in range(L8):
            last = mm(banks[:, 4 + gg // 4, (gg % 4) * P:(gg % 4) * P + P],
                      m.BBp[:, gg, 7 - j:15 - j, :].rearrange("p j n -> p (j n)"),
                      m.CAp[:, gg, 7 - j:15 - j, :].rearrange("p j n -> p (j n)"), j == 0, j == L8 - 1)
    for gg in range(8):
        last = tr(banks[:, 6 + gg // 4, (gg % 4) * P:(gg % 4) * P + P], m.ABx[:, gg, :, :].rearrange("p j n -> p (j n)"))
    last.then_inc(*sig("pe", ("toeplitz", q)))
    pe.wait_ge(*when("etx_copied", q))
    for gg in range(8):
        last = tr(banks[:, 6 + gg // 4, (gg % 4) * P:(gg % 4) * P + P], m.ABy[:, gg, :, :].rearrange("p j n -> p (j n)"))
    last.then_inc(*sig("pe", ("ety_turned", q)))
    pe.wait_ge(*when("ety_copied", q))
    pe.wait_ge(*when("ut_copied", q))
    for gg in range(8):
        c0 = (gg % 2) * 256
        mm(banks[:, gg // 2, c0:c0 + 144], m.ETx[:, gg, :], m.UT[:, gg, :])
        last = mm(banks[:, 4 + gg // 2, c0:c0 + 144], m.ETy[:, gg, :], m.UT[:, gg, :])
    last.then_inc(*sig("pe", ("left", q)))
    pe.wait_ge(*when("h_states", q))
    for gg in range(8):
        g = 8 * q + gg
        out = banks[:, gg // 4, (gg % 4) * P:(gg % 4) * P + P]
        outs = banks[0:NB, 2 + gg // 4, (gg % 4) * P:(gg % 4) * P + P]
        carry = m.CAp[:, gg, 8:16, :].rearrange("p j n -> p (j n)")
        mm(out, m.UT[:, gg, 0:P], m.Tm[:, gg, :], True, False)
        mm(out, m.Hs[:, gg, 0:P], carry, False, True)
        mm(outs, m.UT[:, gg, P:P + NB], m.Tm[:, gg, :], True, False)
        last = mm(outs, m.h0[:, 0, :, g], carry, False, True)
    last.then_inc(*sig("pe", ("y_done", q)))
    pe.wait_ge(*when("gelu_done", q))
    for part in range(3):
        for jj in range(4):
            c0 = jj * P
            if part < 2:
                last = tr(banks[:, 4 + part, c0:c0 + P], m.Yq[:, 4 * part + jj, :])
            else:
                last = tr(banks[:, 6, c0:c0 + NB], m.Yqs[:, jj, :])
    last.then_inc(*sig("pe", ("y_turned", q)))


def tensor_sample_attention(pe, led, m, mm, tr):
    sig, when = led.sig, led.when
    banks = m.banks
    pe.wait_ge(*when("o_copied", 63))
    pe.wait_ge(*when("o_copied", 62))

    def turn_page(b, p):
        n = b * 2 * N_PAGES + p
        e = b * N_PAGES + p
        pe.wait_ge(*when("page_in", n))
        for half in range(2):
            if e:
                pe.wait_ge(*when("page_copied", e - 1, half))
            for q in range(4):
                h = half * 4 + q
                last = tr(banks[:, 4 + half, q * P:q * P + P], m.page(n)[:, h * P:h * P + P])
            last.then_inc(*sig("pe", ("page_turned", e, half), *([("page_used", n)] if half else [])))

    for b in range(NB):
        pe.wait_ge(*when("qpad", b))
        if b:
            pe.wait_ge(*when("s_exp", b - 1))
            pe.wait_ge(*when("os_done", b - 1))
        qp = m.qpad[:, b % 2, :].rearrange("p (h s) -> p h s", s=72)

        def qh(h):
            return m.qpad[:, b % 2, h * 64:h * 64 + 64]
        for h in range(H_C):
            last = mm(banks[0:64, 6, 0:NS], qh(h), m.kTs[:, h, :], h == 0, h == H_C - 1)
        last.then_inc(*sig("pe", ("s_new", b)))
        turn_page(b, 0)
        for p in range(N_PAGES):
            if p + 1 < N_PAGES:
                turn_page(b, p + 1)
            e = b * N_PAGES + p
            for h in range(H_C):
                if h % 4 == 0:
                    pe.wait_ge(*when("page_copied", e, h // 4))
                last = mm(banks[0:64, p // 4, (p % 4) * P:(p % 4) * P + P], qh(h), m.KTp[:, p % 2, h, :],
                          h == 0, h == H_C - 1)
            last.then_inc(*sig("pe", ("page_scored", e)))
        pe.wait_ge(*when("s_coef", b))
        pe.wait_ge(*when("s_exp", b))
        pe.wait_ge(*when("page_copied", b * N_PAGES + 15, 0))
        pe.wait_ge(*when("page_copied", b * N_PAGES + 15, 1))
        for p in range(N_PAGES):
            mm(banks[:, 4, p * NS:p * NS + NS], m.Ps[:, p * P:p * P + P], m.Cm)
        mm(banks[0:NS, 5, 0:NS], m.Ps[:, 2048:2048 + NS], m.Cm).then_inc(*sig("pe", ("pts_done", b)))
        pe.wait_ge(*when("pts_copied", b))
        for p in range(N_PAGES + 1):
            n = (b * 2 + 1) * N_PAGES + p
            if p < N_PAGES:
                pe.wait_ge(*when("page_in", n))
            for half in range(2):
                hs = slice(half * 512, half * 512 + 512)
                if p < N_PAGES:
                    last = mm(banks[0:NS, 6 + half, :], m.PTs[:, p, :], m.page(n)[:, hs], p == 0, False)
                else:
                    last = mm(banks[0:NS, 6 + half, :], m.PTs[0:NS, p, :], m.V[0:NS, 8, hs], False, True)
            if p < N_PAGES:
                last.then_inc(*sig("pe", ("page_used", n), *([("pages_done",)] if (b, p) == (NB - 1, N_PAGES - 1) else [])))
            else:
                last.then_inc(*sig("pe", ("os_ready", b)))
        pe.wait_ge(*when("os_copied", b))
        for h in range(H_C):
            last = tr(banks[:, 4, h * NS:h * NS + NS], m.Os[:, h * P:h * P + P])
        last.then_inc(*sig("pe", ("os_turned", b)))


def vector_program(nc, block, led, m):
    sig, when = led.sig, led.when
    banks, v = m.banks, nc.vector
    vec, mask = m.vec, m.mask

    @block.vector
    def _(ve):
        def do(ins, *steps):
            steps = steps or (("step",),)
            ins.then_inc(*sig("vector", *steps))
            ve.wait_ge(*led.own("vector", steps[0]))

        def tt(out, x, y, op, *steps):
            do(v.tensor_tensor(out, x, y, op), *steps)

        def ts(out, x, s1, o1, s2=None, o2=None, steps=()):
            do(v.tensor_scalar(out, x, s1, None, o1) if o2 is None else v.tensor_scalar(out, x, s1, s2, o1, o2), *steps)

        def stt(out, x, s, y, o1, o2, *steps):
            do(v.scalar_tensor_tensor(out=out, in0=x, scalar=s, in1=y, op0=o1, op1=o2), *steps)

        def cp(out, x, *steps):
            do(v.tensor_copy(out, x), *steps)

        def red(out, x, op, *steps):
            do(v.tensor_reduce(out, x, AX.X, op), *steps)

        n_tile = [0]

        def next_set():
            n = n_tile[0]
            n_tile[0] += 1
            return n, 3 * (n % 2)

        V_ = dict(ve=ve, do=do, tt=tt, ts=ts, stt=stt, cp=cp, red=red)
        ident = m.ident

        ve.wait_ge(*when("masks"))
        tt(m.msk[:, L64, :], m.msk[:, L64, :], m.msk[:, L32, :], ALU.subtract)
        tt(m.msk[:, L32, :], m.msk[:, L32, :], m.msk[:, L16, :], ALU.subtract)
        ts(m.msk[:, NUI64, :], m.msk[:, UI64, :], -1.0, ALU.mult)
        ts(m.msk4[:, NUI4, :], m.msk4[:, UI4, :], -1.0, ALU.mult, steps=[("consts",)])
        ve.wait_ge(*when("cond_sig"))
        tt(m.crows, m.crows, m.csig, ALU.mult, ("silu",))
        ve.wait_ge(*when("vecs_turned"))
        cp(m.vecT[:, 0:N_VEC], banks[:, 0, 0:N_VEC])
        cp(m.bT[:, :], banks[:, 0, 128:224])
        cp(m.shiftT[:, :, :], banks[:, 2, 0:ZT * NB].rearrange("p (k b) -> p k b", b=NB))
        ve.wait_ge(*when("cond_turned"))
        cp(m.condT[:, :, :], banks[:, 1, 0:72].rearrange("p (k b) -> p k b", b=9), ("condT",))
        ve.wait_ge(*when("params_in"))
        for i in range(2):
            q, k = m.lrows[:, 128 * i:128 * i + 64], m.lrows[:, 128 * i + 64:128 * i + 128]
            tt(q, q, k, ALU.mult)
            red(m.lam[0:1, i:i + 1], q, ALU.add, *([("lam_dots",)] if i else []))
        for n in range(48):
            layer, s = n // 24, (n % 24) * 2
            ve.wait_ge(*when("mod_turned", n))
            tt(m.modT[:, layer, s:s + 2, :], banks[:, 3, 0:32].rearrange("p (m b) -> p m b", b=16)[:, :, 0:9],
               rep(m.bT[:, layer * 48 + s:layer * 48 + s + 2], 9), ALU.add, ("mod_biased", n))
        cp(m.lam[:, 4:6], banks[:, 4, 0:2])
        tt(m.lam[:, 6:7], m.lam[:, 4:5], m.lam[:, 5:6], ALU.subtract)
        ts(m.lam[:, 6:7], m.lam[:, 6:7], -float(D), ALU.mult, -LAM0, ALU.add)
        for layer in range(2):
            for w, (sc, nm) in enumerate(((SC_M, "norm_mix"), (SC_F, "norm_mlp"))):
                r = VEC[nm][0] + 8 * layer
                g = m.gain[:, layer, w, :, :]
                ts(g, m.modT[:, layer, sc:sc + 8, :], 1.0, ALU.add)
                tt(g, g, rep(m.vecT[:, r:r + 8], 9), ALU.mult)

        def norm(layer, w):
            ve.wait_ge(*when("std", (layer, w)))
            do(v.reciprocal(m.rstd, m.rstd))
            for k in range(KT):
                h, x = m.hT[:, k, :], m.xT[:, k, :]
                last = [("h_ready", layer, w)] if k == KT - 1 else []
                if layer == 2:
                    stt(h, x, vec("norm_f", k), m.rstd, ALU.mult, ALU.mult, *last)
                    continue
                G, sh = m.gain[:, layer, w, k, :], m.modT[:, layer, (SH_M, SH_F)[w] + k, :]
                stt(h[:, 0:TP], x[:, 0:TP], G[:, 0:1], m.rstd[:, 0:TP], ALU.mult, ALU.mult)
                ts(h[:, 0:TP], h[:, 0:TP], sh[:, 0:1], ALU.add)
                tt(smp(h), smp(x), smp(m.rstd), ALU.mult)
                tt(smp(h), smp(h), rep(G[:, 1:9], TS), ALU.mult)
                tt(smp(h), smp(h), rep(sh[:, 1:9], TS), ALU.add, *last)

        norm(0, 0)
        ve.wait_ge(*when("spilled", 0))
        do(v.memset(m.rowm, 1.0))
        do(v.memset(m.rowm[:, 0:TP:C64], 0.0))
        do(v.memset(m.rowm[:, TP:T:TS], 0.0))
        red(m.eb, ident[:, 0:NS].rearrange("p (b q) -> p b q", q=TS), ALU.add)

        def shifted(dst, zi, n):
            mu = vec("rwkv_mu", zi)
            z, zp = m.zb[:, 1:1 + TP], m.zb[:, 0:TP]
            s = m.zb[:, 1025:1065].rearrange("p (b q) -> p b q", q=5)
            ve.wait_ge(*when("zb_ready", n))
            tt(dst[:, 0:TP], zp, z, ALU.subtract)
            stt(dst[:, 0:TP], dst[:, 0:TP], mu, z, ALU.mult, ALU.add)
            tt(smp(dst), s[:, :, 0:4], s[:, :, 1:5], ALU.subtract)
            stt(smp(dst), smp(dst), mu, s[:, :, 1:5], ALU.mult, ALU.add, ("zb_used", n))

        shifted(m.lora, 12, next_set()[0])
        shifted(m.sgd, 13, next_set()[0])
        for j in range(N_PAIR):
            KR, Kf, Vf, Af, T1, KH, BH, LW, Lc, QO, WC = (m.KR, m.Kf, m.Vf, m.Af, m.T1, m.KH, m.BH, m.LW, m.Lc,
                                                          m.QO, m.WC)
            for zi, dst in ((0, KR[:, 1, :]), (4, Kf), (8, Vf)):
                shifted(dst, zi + j, next_set()[0])
            for _ in range(3):
                next_set()
            ve.wait_ge(*when("lw_sig", j))
            ts(LW, LW, -DECAY, ALU.mult)
            KK = KR[:, 0, :]
            ts(KK, Kf, vec("rwkv_k_k", j), ALU.mult)
            tt(T1, KK, KK, ALU.mult, ("kk_sq", j))
            next_set()
            ve.wait_ge(*when("kk_norm", j))
            ts(T1, T1, 1e-12, ALU.max)
            do(v.reciprocal(T1, T1))
            tt(KK, KK, T1, ALU.mult)
            ve.wait_ge(*when("a_ready", j))
            ts(T1, Af, -1.0, ALU.add, vec("rwkv_k_a", j), ALU.mult)
            stt(Kf, T1, 1.0, Kf, ALU.add, ALU.mult)
            stt(T1, KR[:, 1, :], vec("rwkv_r_k", j), Kf, ALU.mult, ALU.mult, ("rk_prod", j))
            n, s = next_set()
            ve.wait_ge(*when("set_done", n))
            for c, (t0, t1) in enumerate(CHUNKS):
                tt(m.BON[:, t0:t1], banks[:, s + c, 0:CH], Vf[:, t0:t1], ALU.mult, *([("set_free", n)] if c == 2 else []))
            do(v.tensor_tensor_scan(Lc, m.rowm, LW, 0.0, ALU.mult, ALU.add))
            tt(T1, Lc, LW, ALU.subtract, ("lx", j))
            tt(Af, KK, Af, ALU.mult)
            ve.wait_ge(*when("e_lx", j))
            tt(KK, KK, T1, ALU.mult)
            ve.wait_ge(*when("e_l", j))
            tt(KR[:, 1, :], KR[:, 1, :], KH, ALU.mult)
            cp(WC[:, 0:16], KH[:, 63:TP:C64])
            cp(WC[:, 16:24], KH[:, TP + 3:T:TS])
            ve.wait_ge(*when("e_nl", j))
            tt(Kf, Kf, BH, ALU.mult)
            tt(Af, Af, BH, ALU.mult)

            def ch(ap):
                return ap[:, 0:TP].rearrange("p (c t) -> p c t", t=C64)
            wcp, wcs = rep(WC[:, 0:16], C64), rep(WC[:, 16:24], TS)
            tt(ch(KH), ch(Kf), wcp, ALU.mult)
            tt(smp(KH), smp(Kf), wcs, ALU.mult)
            tt(ch(BH), ch(Af), wcp, ALU.mult)
            tt(smp(BH), smp(Af), wcs, ALU.mult)
            ts(BH, BH, -1.0, ALU.mult)
            do(v.memset(m.SBD[:, 0, :], 0.0))
            ve.wait_ge(*when("s0_turned", j))
            for half in range(2):
                cp(m.SBD[:, 1 + 4 * half:5 + 4 * half, :], banks[:, 6 + half, :].rearrange("p (b k) -> p b k", b=4),
                   *([("s0_copied", j)] if half else []))
            for g, tl, n in GROUPS:
                vector_rwkv_group(nc, led, m, V_, j, g, tl, n)
            ve.wait_ge(*when("sfin_turned", j))
            if j:
                ve.wait_ge(*when("sout_out", j - 1))
            for i0, cnt, bank in ((0, 4, 0), (4, 4, 1), (8, 1, 2)):
                for hh in range(2):
                    hs = slice(64 * hh, 64 * hh + 64)
                    cp(m.SOUT[hs, i0:i0 + cnt, :],
                       banks[hs, bank, 0:cnt * P].rearrange("p (i k) -> p i k", k=P)[:, :, 64 * hh:64 * hh + 64],
                       *([("sout_ready", j)] if (i0, hh) == (8, 1) else []))
            n, s = next_set()
            ve.wait_ge(*when("set_done", n))
            for c, (t0, t1) in enumerate(CHUNKS):
                stt(QO[:, t0:t1], banks[:, s + c, 0:CH], -1.0 / C64, QO[:, t0:t1], ALU.mult, ALU.add,
                    *([("set_free", n)] if c == 2 else []))
            tt(T1, QO, QO, ALU.mult, ("gn_sq", j))
            next_set()
            ve.wait_ge(*when("gn_std", j))
            do(v.reciprocal(T1, T1))
            tt(QO, QO, T1, ALU.mult)
            ts(QO, QO, vec("rwkv_lnx_w", j), ALU.mult, vec("rwkv_lnx_b", j), ALU.add)
            tt(QO, QO, m.BON, ALU.add)
            ve.wait_ge(*when("g_ready", j))
            tt(m.mT[:, j, :], QO, m.Gf, ALU.mult, ("mix_ready", j))

        vector_s5(nc, led, m, V_)
        for ft in range(4):
            n, s = next_set()
            ve.wait_ge(*when("glu_sig", ft))
            tt(m.mT[:, 4 + ft, :], m.yT[:, ft, :], m.sT, ALU.mult, ("glu_used", ft), *([("mixed", 0)] if ft == 3 else []))

        def residual(layer, gsec, tiles, final):
            for k in range(tiles):
                n, s = next_set()
                ve.wait_ge(*when("set_done", n))
                gate, x = m.modT[:, layer, gsec + k, :], m.xT[:, k, :]
                tail = TP - 2 * CH
                ps = banks[:, s + 2, tail:CH].rearrange("p (b q) -> p b q", q=TS)
                for c in range(3):
                    t0, t1 = CHUNKS[c][0], min(CHUNKS[c][1], TP)
                    stt(x[:, t0:t1], banks[:, s + c, 0:t1 - t0], gate[:, 0:1], x[:, t0:t1], ALU.mult, ALU.add)
                tmp = m.rstd[:, 0:NS].rearrange("p (b q) -> p b q", q=TS)
                tt(tmp, ps, rep(gate[:, 1:9], TS), ALU.mult, ("set_free", n))
                tt(smp(x), smp(x), tmp, ALU.add, *([final] if k == tiles - 1 else []))

        def out_and_mlp(layer):
            ve.wait_ge(*when("x_back", layer))
            residual(layer, G_M, 8, ("x_mid", layer))
            norm(layer, 1)
            for q in range(4):
                for k in range(8):
                    n, s = next_set()
                    ve.wait_ge(*when("relu", n))
                    tt(m.mT[:, k, :], m.mT[:, k, :], m.mT[:, k, :], ALU.mult, *([("hidden", layer, q)] if k == 7 else []))
                residual(layer, G_F, 8, ("x_ready", layer + 1) if q == 3 else ("x_part", layer, q))

        out_and_mlp(0)

        norm(1, 0)
        for _ in range(16):
            next_set()
        for h in range(H_C):
            for i in range(8):
                s = h * 8 + i
                nk = (i + 1) * P
                P0, P1, st = m.Pp[:, s % 2, 0, 0:nk], m.Pp[:, s % 2, 1, 0:nk], m.st[:, s % 2, :]
                ve.wait_ge(*when("scores", s))
                for c in range(2):
                    diag = banks[:, 2 * c + i // 4, (i % 4) * P:(i % 4) * P + P]
                    tt(diag, diag, mask(CAUSAL), ALU.add)
                    row = banks[:, 2 * c:2 * c + 2, :].rearrange("p b k -> p (b k)")[:, 0:nk]
                    red(st[:, c:c + 1], row, ALU.max)
                ts(st[:, 2:4], st[:, 0:2], -1.0, ALU.mult, steps=[("row_max", s)])
                ve.wait_ge(*when("scores_free", s))
                do(v.reciprocal(st[:, 6:8], st[:, 4:6]))
                tt(st[:, 8:9], st[:, 7:8], m.lam[:, 6:7], ALU.mult)
                ts(P0, P0, st[:, 6:7], ALU.mult)
                stt(P0, P1, st[:, 8:9], P0, ALU.mult, ALU.add, ("probs", s))
        vector_sample_attention(nc, led, m, V_)
        ts(m.ss[:, 0:1], vec("diff_subln"), 1.0 - LAM0, ALU.mult)
        for h in range(H_C):
            next_set()
            ve.wait_ge(*when("o_std", h))
            do(v.reciprocal(m.r2[:, h % 2, :], m.r2[:, h % 2, :]))
            stt(m.oT[:, h, :], m.oT[:, h, :], m.ss[:, 0:1], m.r2[:, h % 2, :], ALU.mult, ALU.mult, ("o_normed", h),
                *([("mixed", 1), ("attention_done",)] if h == H_C - 1 else []))
        out_and_mlp(1)
        norm(2, 0)


def vector_rwkv_group(nc, led, m, V_, j, g, tl, n):
    when = led.when
    ve, do, tt, ts, stt, cp = (V_[x] for x in ("ve", "do", "tt", "ts", "stt", "cp"))
    banks, mask, ident = m.banks, m.mask, m.ident
    nt, sample = len(tl), n == NS
    k = 2 * nt
    up, upi, lo, nup, full = (U4, UI4, L4, NUI4, U4) if sample else (U16, UI64, L16, NUI64, U64)
    Dd, Dt, FF, FT, PW = m.Dd, m.Dt, m.FF, m.FT, m.PW
    ve.wait_ge(*when("grams", j, g))
    for h in range(2):
        def gram(bank, i):
            return banks[0:n, bank, 0:nt * 256].rearrange("p (t i c) -> p t i c", i=2, c=P)[:, :, i, 0:n]
        us = slice(h, k, 2)
        for dst, src, mk in ((m.AKK, gram(2 + h, 0), full), (m.ARK, gram(2 + h, 1), upi),
                             (m.ARB, gram(4 + h, 1), nup), (Dt, gram(4 + h, 0), up)):
            tt(dst[0:n, us, 0:n], src, mid(mask(mk, n), nt), ALU.mult)
        g3 = banks[0:n, 6 + h, 0:nt * P].rearrange("p (t c) -> p t c", c=P)[:, :, 0:n]
        tt(Dd[0:n, us, 0:n], g3, mid(mask(lo, n), nt), ALU.mult)
        if not sample:
            tt(m.O32[:, us, :], g3, mid(mask(L32), nt), ALU.mult)
            tt(m.O64[:, us, :], g3, mid(mask(L64), nt), ALU.mult)
    F = FF[0:n, 0:k, 0:n]
    ts(F, Dt[0:n, 0:k, 0:n], -1.0, ALU.mult)
    tt(F, F, mid(ident[0:n, 0:n], k), ALU.add, ("gram_masked", j, g))

    def cells(bank):
        return banks[0:n, bank, 0:k * P].rearrange("p (u t) -> p u t", t=P)[:, :, 0:n]
    ve.wait_ge(*when("d2", j, g))
    cp(PW[0:n, 0, 0:k, 0:n], cells(0))
    cp(PW[0:n, 1, 0:k, 0:n], cells(1), ("d2_copied", j, g))
    ve.wait_ge(*when("d4", j, g))
    if sample:
        tt(F, F, cells(7), ALU.add, ("m_ready", j, g))
    else:
        tt(F, F, cells(7), ALU.add)
        cp(PW[:, 0, :, :], cells(2))
        cp(PW[:, 1, :, :], cells(3), ("d4_copied", j, g))
        ve.wait_ge(*when("d8", j, g))
        tt(F, F, cells(7), ALU.add)
        cp(PW[:, 0, :, :], cells(0), ("d8_copied", j, g))
        ve.wait_ge(*when("f4p", j, g))
        tt(F, F, cells(7), ALU.add, ("f_level", j, g, 0))
        for lv in range(2):
            ve.wait_ge(*when("level_p1", j, g, lv))
            cp(FT, cells(1))
            cp(PW[:, 0, :, :], cells(2), ("level_copied", j, g, lv))
            ve.wait_ge(*when("level_p2", j, g, lv))
            tt(F, F, cells(3), ALU.subtract, ("f_level", j, g, 1) if lv == 0 else ("m_ready", j, g))
    ve.wait_ge(*when("akkv", j, g))
    ve.wait_ge(*when("tm_ready", j, g))
    cp(m.RHS[0:n, 0:nt, :, 1, :], banks[0:n, 4, 0:k * C64].rearrange("p (t h v) -> p t h v", h=2, v=C64))
    cp(m.RHS[0:n, 0:nt, :, 0, :], m.TM[0:n, 0:nt, 3, :].rearrange("p t (h v) -> p t h v", h=2), ("rhs_ready", j, g))
    ve.wait_ge(*when("xy", j, g))
    for t in range(nt):
        cp(m.XY[0:n, t, :, :, :], banks[0:n, 5, t * 256:t * 256 + 256].rearrange("p (h i v) -> p i h v", h=2, i=2),
           *([("xy_copied", j, g)] if t == nt - 1 else []))
    ve.wait_ge(*when("zq", j, g))
    for t, (t0, _) in enumerate(tl):
        for h in range(2):
            hs = slice(64 * h, 64 * h + 64)
            tt(m.ZTt[hs, t, 0:n], m.KR[hs, 1, t0:t0 + n], banks[hs, t, h * P:h * P + n], ALU.add)
            cp(m.QTt[hs, t, 0:n], banks[hs, 2 + t, h * P:h * P + n],
               *([("zq_copied", j, g)] if (t, h) == (nt - 1, 1) else []))
    TT, SBD, QO, WC = m.TT, m.SBD, m.QO, m.WC
    if not sample:
        ve.wait_ge(*when("tt", j, g))
        for c in range(2):
            tt(TT[:, c::2, :], banks[:, 6 + c, 0:256].rearrange("p (t k) -> p t k", t=2), mid(m.bd1[:, :], 2), ALU.mult)
        for q in range(4):
            ci = 4 * g + q
            stt(TT[:, q, :], ident[:, :], WC[:, ci:ci + 1], TT[:, q, :], ALU.mult, ALU.add,
                *([("tt_ready", j, g)] if q == 3 else []))
        for q in range(4):
            ve.wait_ge(*when("state_new", j, g, q))
            t0 = (4 * g + q) * C64
            tt(SBD[:, 0, :], banks[:, 4, q * P:q * P + P], m.bd1[:, :], ALU.mult,
               *([("state", j, g, q + 1)] if q < 3 else []))
            tt(QO[:, t0:t0 + C64], banks[:, 5 + q % 2, 0:C64], m.QTt[:, q // 2, (q % 2) * C64:(q % 2) * C64 + C64],
               ALU.add, *([("rw_free", j, g + 1)] if q == 3 else []))
        return
    ve.wait_ge(*when("o_sample", j))
    tt(QO[:, TP:T], banks[:, 0, 0:NS], m.QTt[:, 0, 0:NS], ALU.add, ("o_ready", j))
    for half in range(2):
        for q in range(4):
            b = half * 4 + q
            ts(m.MB[0:NS, q, :, :], m.TM[0:NS, 0, 0:2, :], m.eb[0:NS, b:b + 1], ALU.mult,
               steps=[("mb_ready", j, half)] if q == 3 else [])
        ve.wait_ge(*when("tts", j, half))
        tt(TT, banks[:, 6 + half, :].rearrange("p (u t) -> p u t", t=P), mid(m.bd1[:, :], 4), ALU.mult)
        for q in range(4):
            b = half * 4 + q
            stt(TT[:, q, :], ident[:, :], WC[:, 16 + b:17 + b], TT[:, q, :], ALU.mult, ALU.add,
                *([("tts_ready", j, half)] if q == 3 else []))
        ve.wait_ge(*when("states_new", j, half))
        tt(SBD[:, 1 + 4 * half:5 + 4 * half, :], banks[:, 4 + half, :].rearrange("p (b k) -> p b k", b=4),
           mid(m.bd1[:, :], 4), ALU.mult, *([("states_final", j)] if half else []))


def vector_s5(nc, led, m, V_):
    when = led.when
    ve, do, tt, ts, stt, cp = (V_[x] for x in ("ve", "do", "tt", "ts", "stt", "cp"))
    banks, v = m.banks, nc.vector
    A, S, M = ALU.add, ALU.subtract, ALU.mult
    LI, DT, AR, AI, MAG8, FR, FI, C1, S1, A4R, A4I, P8C, P8S, LR, DC, TH, W1, W2, W3, W4 = (
        m.c[name] for name in S5_ROWS[1:])
    ve.wait_ge(*when("s5_in"))
    rows = m.s5rows
    for jj in range(1, L8):
        cp(rows[0:32, 2, jj * 16:jj * 16 + 16], rows[0:32, 2, 0:16], *([("d_rows",)] if jj == 7 else []))
    ts(m.BY[64:128, :, :], m.BY[64:128, :, :], -1.0, M)
    ve.wait_ge(*when("s5_turned"))
    cp(LR, banks[:, 6, 0:32])
    cp(LI, banks[:, 6, 32:64])
    cp(DC, banks[:, 6, 64:96])
    ve.wait_ge(*when("dt_exp"))
    tt(W1, LR, DT, M)
    tt(TH, LI, DT, M)
    ts(W2, TH, 1.0 / (2 * math.pi), M, ROUND, A)
    ts(W2, W2, ROUND, S)
    stt(TH, W2, -TWO_PI_HI, TH, M, A)
    stt(TH, W2, -TWO_PI_LO, TH, M, A)
    ts(W3, TH, PI_IN, ALU.min, -PI_IN, ALU.max)
    ts(W4, W3, math.pi / 2, A)
    ts(W2, W4, math.pi, ALU.is_gt, -2 * math.pi, M)
    tt(W4, W4, W2, A)
    ts(W4, W4, PI_IN, ALU.min, -PI_IN, ALU.max, steps=[("angles",)])
    ve.wait_ge(*when("s5_funcs"))
    tt(AR, W1, C1, M)
    tt(AI, W1, S1, M)

    def cmul(xr, xi, yr, yi, outr, outi, t1, t2):
        tt(t1, xr, yr, M)
        tt(t2, xi, yi, M)
        tt(t1, t1, t2, S)
        tt(t2, xr, yi, M)
        tt(outi, xi, yr, M)
        tt(outi, outi, t2, A)
        cp(outr, t1)

    tt(W2, LR, LR, M)
    tt(W3, LI, LI, M)
    tt(W2, W2, W3, A)
    do(v.reciprocal(W2, W2))
    ts(W3, AR, -1.0, A)
    tt(FR, W3, LR, M)
    tt(W4, AI, LI, M)
    tt(FR, FR, W4, A)
    tt(FR, FR, W2, M)
    tt(FI, AI, LR, M)
    tt(W4, W3, LI, M)
    tt(FI, FI, W4, S)
    tt(FI, FI, W2, M)
    fr, fi = rep(FR, G_CH), rep(FI, G_CH)
    t1, t2 = m.q3.rearrange("p g c -> p (g c)")[:, 0:512].rearrange("p (g n) -> p g n", n=G_CH), \
        m.q3.rearrange("p g c -> p (g c)")[:, 512:1024].rearrange("p (g n) -> p g n", n=G_CH)
    tt(t1, m.BX, fr, M)
    tt(t2, m.BY, fi, M)
    tt(t1, t1, t2, S)
    tt(t2, m.BX, fi, M)
    tt(m.BY, m.BY, fr, M)
    tt(m.BY, m.BY, t2, A)
    cp(m.BX, t1)
    cmul(AR, AI, AR, AI, A4R, A4I, W2, W3)
    tt(W2, A4R, A4R, M)
    tt(W3, A4I, A4I, M)
    tt(W4, A4R, A4I, M)
    tt(A4R, W2, W3, S)
    tt(A4I, W4, W4, A)
    x, y = C1, S1
    for _ in range(3):
        tt(W2, x, x, M)
        tt(W3, y, y, M)
        tt(W4, x, y, M)
        tt(P8C, W2, W3, S)
        tt(P8S, W4, W4, A)
        x, y = P8C, P8S
    for k in range(12):
        ve.wait_ge(*when("crow_turned", k))
        src = banks[:, 4 + k % 2, 0:P]
        if k < 8:
            dst = (m.CX, m.CY)[k % 2][:, 8 * (k // 2):8 * (k // 2) + 8, :]
            neg = k % 2 == 0
            src = src.rearrange("p (g n) -> p g n", n=G_CH)
        else:
            dst = m.h0[:, k % 2, 4 * ((k - 8) // 2):4 * ((k - 8) // 2) + 4, :]
            neg = k % 2 == 1
            src = src.rearrange("p (b g) -> p b g", g=N_G)
        cp(dst[0:64], src[0:64])
        ts(dst[64:128], src[64:128], -1.0 if neg else 1.0, M, steps=[("crow_copied", k)])
    ve.wait_ge(*when("shift_out"))
    do(v.memset(m.BBp, 0.0))
    do(v.memset(m.Hs[:, :, 0:1], 0.0))
    for q in range(4):
        gs = slice(8 * q, 8 * q + 8)
        ar, ai = rep(AR[:, gs], G_CH), rep(AI[:, gs], G_CH)
        ve.wait_ge(*when("u_copied", 23))
        if q:
            ve.wait_ge(*when("y_done", q - 1))
        do(v.memset(m.CAp[:, :, 0:7, :], 0.0))

        def power(xo, yo, xi, yi):
            tt(xo, xi, ar, M)
            tt(m.q1, yi, ai, M)
            tt(m.q2, xi, ai, M)
            tt(xo, xo, m.q1, S)
            tt(yo, yi, ar, M)
            tt(yo, yo, m.q2, A)
        cp(m.CAp[:, :, 7, :], m.CX[:, gs, :])
        cp(m.CYr, m.CY[:, gs, :])
        for i in range(8):
            power(m.CAp[:, :, 8 + i, :], m.CYr, m.CAp[:, :, 7 + i, :], m.CYr)
        cp(m.ABx[:, :, 7, :], m.BX[:, gs, :])
        cp(m.ABy[:, :, 7, :], m.BY[:, gs, :])
        cp(m.BBp[:, :, 7, :], m.BX[:, gs, :])
        for i in range(7, 0, -1):
            power(m.ABx[:, :, i - 1, :], m.ABy[:, :, i - 1, :], m.ABx[:, :, i, :], m.ABy[:, :, i, :])
        cp(m.phc[:, 0, :], P8C[:, gs])
        cp(m.phc[:, 1, :], P8S[:, gs], ("powers", q))
        COS, SIN, ph = m.COS, m.SIN, m.phc
        do(v.memset(COS[:, :, 0:1], 1.0))
        do(v.memset(SIN[:, :, 0:1], 0.0))
        n = 1
        while n < NC8:
            pc, ps_ = rep(ph[:, 0, :], n), rep(ph[:, 1, :], n)
            lo, hi, tmp = slice(0, n), slice(n, 2 * n), m.G1[:, :, 0:n]
            tt(COS[:, :, hi], COS[:, :, lo], pc, M)
            tt(tmp, SIN[:, :, lo], ps_, M)
            tt(COS[:, :, hi], COS[:, :, hi], tmp, S)
            tt(SIN[:, :, hi], SIN[:, :, lo], pc, M)
            tt(tmp, COS[:, :, lo], ps_, M)
            tt(SIN[:, :, hi], SIN[:, :, hi], tmp, A)
            tt(ph[:, 2, :], ph[:, 0, :], ph[:, 0, :], M)
            tt(ph[:, 3, :], ph[:, 1, :], ph[:, 1, :], M)
            tt(ph[:, 1, :], ph[:, 0, :], ph[:, 1, :], M)
            ts(ph[:, 1, :], ph[:, 1, :], 2.0, M)
            tt(ph[:, 0, :], ph[:, 2, :], ph[:, 3, :], S)
            n *= 2
        ve.wait_ge(*when("toeplitz", q))
        for gg in range(8):
            g = 8 * q + gg
            stt(m.Tm[:, gg, :], m.ident[:, :], DC[:, g:g + 1], banks[:, 4 + gg // 4, (gg % 4) * P:(gg % 4) * P + P], M, A)
        for half in range(2):
            cp(m.ETx[:, 4 * half:4 * half + 4, :], banks[:, 6 + half, :].rearrange("p (g c) -> p g c", g=4),
               *([("etx_copied", q)] if half else []))
        ve.wait_ge(*when("ety_turned", q))
        for half in range(2):
            cp(m.ETy[:, 4 * half:4 * half + 4, :], banks[:, 6 + half, :].rearrange("p (g c) -> p g c", g=4),
               *([("ety_copied", q)] if half else []))
        ve.wait_ge(*when("left", q))
        for half in range(4):
            hs = slice(2 * half, 2 * half + 2)
            bx = banks[:, half, :].rearrange("p (g c) -> p g c", g=2)
            by = banks[:, 4 + half, :].rearrange("p (g c) -> p g c", g=2)
            cos, sin, tmp = COS[:, hs, :], SIN[:, hs, :], m.q3[:, hs, :]
            tt(m.G1[:, hs, :], bx[:, :, 0:P], cos, M)
            tt(tmp, by[:, :, 0:P], sin, M)
            tt(m.G1[:, hs, :], m.G1[:, hs, :], tmp, A)
            tt(m.G2[:, hs, :], by[:, :, 0:P], cos, M)
            tt(tmp, bx[:, :, 0:P], sin, M)
            tt(m.G2[:, hs, :], m.G2[:, hs, :], tmp, S)
            for gg in range(2):
                g = 8 * q + 2 * half + gg
                t = m.q1.rearrange("p g n -> p (g n)")
                ts(t[:, 0:8], m.h0[:, 0, :, g], A4R[:, g:g + 1], M)
                tt(t[:, 0:8], t[:, 0:8], bx[:, gg, 136:144], A)
                ts(t[:, 8:16], m.h0[:, 1, :, g], A4I[:, g:g + 1], M)
                tt(m.h4[:, :, g], t[:, 0:8], t[:, 8:16], S)
        for gg in range(8):
            g = 8 * q + gg
            mag = MAG8[:, g:g + 1].to_broadcast([P, NC8])
            for G in (m.G1, m.G2):
                do(v.tensor_tensor_scan(G[:, gg, :], mag, G[:, gg, :], 0.0, M, A))
        tt(m.Hs[:, :, 1:129], m.G1, COS, M)
        tt(m.q3, m.G2, SIN, M)
        tt(m.Hs[:, :, 1:129], m.Hs[:, :, 1:129], m.q3, S)
        cp(m.hfin[:, gs], m.Hs[:, :, 128], ("h_states", q), *([("s5_states",)] if q == 3 else []))


def vector_sample_attention(nc, led, m, V_):
    when = led.when
    ve, do, tt, ts, stt, cp, red = (V_[x] for x in ("ve", "do", "tt", "ts", "stt", "cp", "red"))
    banks, v, ident = m.banks, nc.vector, m.ident
    ve.wait_ge(*when("o_done", 63))
    ve.wait_ge(*when("qs_saved"))
    id64 = ident[0:64, 0:64]
    red(m.csel[0:64, :].rearrange("p (h q) -> p h q", q=4), id64.rearrange("p (h c q) -> p h q c", c=2, q=4), ALU.add)
    c1 = id64.rearrange("p (h c q) -> p h c q", c=2, q=4)[:, :, 1, :]
    tmp = m.Sn[:, 0:32]
    cp(tmp.rearrange("p (h q) -> p h q", q=4), c1)
    red(m.ss[0:64, 8:9], tmp, ALU.add)
    ts(m.ss[0:64, 9:10], m.lam[0:64, 6:7], -1.0, ALU.add)
    tt(m.ss[0:64, 8:9], m.ss[0:64, 8:9], m.ss[0:64, 9:10], ALU.mult)
    ts(m.ss[0:64, 8:9], m.ss[0:64, 8:9], 1.0, ALU.add)
    red(m.sel4[0:64, :], id64.rearrange("p (a q) -> p q a", q=4), ALU.add)
    do(v.memset(m.nmask[0:64, :, :], NEG))
    nm = m.nmask[0:64, 7, :]
    do(v.memset(nm[:, 0:1], 0.0))
    for i in range(1, 4):
        tt(nm[:, i:i + 1], nm[:, i - 1:i], m.sel4[0:64, i - 1:i], ALU.add)
    ts(nm, nm, NEG, ALU.mult)
    do(v.memset(m.qpad, 0.0), ("qpad_zero",))

    def qpad(b):
        if b >= 2:
            ve.wait_ge(*when("page_scored", (b - 2) * N_PAGES + 15))
        pad = m.qpad[:, b % 2, :].rearrange("p (h s) -> p h s", s=72)
        for c in range(2):
            cs = slice(64 * c, 64 * c + 64)
            cp(pad[cs, :, 4 * c:4 * c + 4], m.qTs[cs, :, b * 4:b * 4 + 4], *([("qpad", b)] if c else []))

    qpad(0)
    qpad(1)
    for b in range(NB):
        ss = m.ss[0:64, :]
        ve.wait_ge(*when("s_new", b))
        if b:
            ve.wait_ge(*when("pts_done", b - 1))
        tt(m.Sn, banks[0:64, 6, 0:NS], m.nmask[0:64, 7 - b:15 - b, :].rearrange("p b k -> p (b k)"), ALU.add)
        red(ss[:, 0:1], m.Sn, ALU.max)
        for p in range(N_PAGES):
            e = b * N_PAGES + p
            ve.wait_ge(*when("page_turned", e, 1))
            if e >= 2:
                ve.wait_ge(*when("page_scored", e - 2))
            cp(m.KTp[:, p % 2, 4:8, :], banks[:, 5, :].rearrange("p (h k) -> p h k", h=4), ("page_copied", e, 1))
        ve.wait_ge(*when("page_scored", b * N_PAGES + 15))
        red(ss[:, 1:2], banks[0:64, 0:4, :].rearrange("p b k -> p (b k)"), ALU.max)
        tt(ss[:, 2:3], ss[:, 0:1], ss[:, 1:2], ALU.max)
        ts(ss[:, 3:4], ss[:, 2:3], -1.0, ALU.mult, steps=[("s_max", b)])
        ve.wait_ge(*when("s_exp", b))
        tt(ss[:, 6:7], ss[:, 4:5], ss[:, 5:6], ALU.add)
        do(v.reciprocal(ss[:, 6:7], ss[:, 6:7]))
        tt(ss[:, 6:7], ss[:, 6:7], ss[:, 8:9], ALU.mult)
        ts(m.Cm, m.csel[0:64, :], ss[:, 6:7], ALU.mult, steps=[("s_coef", b)])
        ve.wait_ge(*when("pts_done", b))
        cp(m.PTs[:, 0:16, :], banks[:, 4, :].rearrange("p (a q) -> p a q", a=16))
        cp(m.PTs[0:NS, 16, :], banks[0:NS, 5, 0:NS], ("pts_copied", b))
        if b + 2 < NB:
            qpad(b + 2)
        ve.wait_ge(*when("os_ready", b))
        cp(m.Os[:, 0:512], banks[0:NS, 6, :])
        cp(m.Os[:, 512:1024], banks[0:NS, 7, :], ("os_copied", b))
        ve.wait_ge(*when("os_turned", b))
        src = banks[:, 4, 0:256].rearrange("p (h s) -> p h s", s=32)
        for h in range(H_C):
            cp(m.oT[:, h, TP + 4 * b:TP + 4 * b + 4], src[:, h, 4 * h:4 * h + 4],
               *([("os_done", b)] + ([("oT_done",)] if b == NB - 1 else []) if h == H_C - 1 else []))


def scalar_program(nc, block, led, m):
    sig, when = led.sig, led.when
    banks, vec = m.banks, m.vec

    @block.scalar
    def _(ac):
        def do(ins, *steps):
            steps = steps or (("step",),)
            ins.then_inc(*sig("scalar", *steps))
            ac.wait_ge(*led.own("scalar", steps[0]))

        def act(out, x, f, *steps, bias=0.0, scale=1.0, accum=None):
            kw = {"accum_out": accum} if accum is not None else {}
            do(nc.scalar.activation(out, x, f, bias=bias, scale=scale, **kw), *steps)

        def cp(out, x, *steps):
            do(nc.scalar.copy(out, x), *steps)

        n_tile = [0]

        def next_set():
            n = n_tile[0]
            n_tile[0] += 1
            return n, 3 * (n % 2)

        ac.wait_ge(*when("params_in"))
        act(m.csig, m.crows, ACT.Sigmoid, ("cond_sig",))
        for i, (t0, n) in enumerate(TILES):
            for half in range(2):
                ac.wait_ge(*when("xin_turned", i, half))
                cp(m.xT[:, 4 * half:4 * half + 4, t0:t0 + n],
                   banks[:, 6 + half, :].rearrange("p (q t) -> p q t", q=4)[:, :, 0:n], ("xin_copied", i, half),
                   *([("xin_used", i)] + ([("x_ready", 0)] if i == 8 else []) if half else []))
        ac.wait_ge(*when("lam_dots"))
        act(m.lam[0:1, 2:4], m.lam[0:1, 0:2], ACT.Exp, ("lam_exps",))
        for n in range(48):
            ac.wait_ge(*when("weights_used", n))
            if n:
                ac.wait_ge(*when("mod_turned", n - 1))
            cp(m.modrow, banks[0:9, n % 2, 0:256], ("mod_copied", n))

        def squares(layer, w):
            for k in range(KT):
                if k >= 2:
                    ac.wait_ge(*when("squares_used", (layer, w), k - 2))
                act(m.sq[:, k % 2, :], m.xT[:, k, :], ACT.Square, ("squares", (layer, w), k))
            ac.wait_ge(*when("squares_used", (layer, w), KT - 1))
            for c, (t0, t1) in enumerate(CHUNKS):
                act(m.rstd[:, t0:t1], banks[:, c, 0:CH], ACT.Sqrt, *([("std", (layer, w))] if c == 2 else []),
                    bias=m.eps[:, 0:1])

        squares(0, 0)
        def roots(dst, step, **kw):
            n, s = next_set()
            ac.wait_ge(*when("set_done", n))
            for c, (t0, t1) in enumerate(CHUNKS):
                act(dst[:, t0:t1], banks[:, s + c, 0:CH], ACT.Sqrt, *([step, ("set_free", n)] if c == 2 else []), **kw)

        last_z = [None]

        def z_rows(zi):
            n, s = next_set()
            ac.wait_ge(*when("set_done", n))
            if last_z[0] is None:
                ac.wait_ge(*when("zb_zero"))
            else:
                ac.wait_ge(*when("zb_used", last_z[0]))
            last_z[0] = n
            sv = m.zb[:, 1025:1065].rearrange("p (b q) -> p b q", q=5)
            cp(sv[:, :, 0], m.shiftT[:, zi, :])
            cp(m.zb[:, 1:1 + CH], banks[:, s, 0:CH])
            cp(m.zb[:, 1 + CH:1 + 2 * CH], banks[:, s + 1, 0:CH])
            cp(m.zb[:, 1 + 2 * CH:1 + TP], banks[:, s + 2, 0:TP - 2 * CH])
            cp(sv[:, :, 1:5], banks[:, s + 2, TP - 2 * CH:CH].rearrange("p (b q) -> p b q", q=TS),
               ("zb_ready", n), ("set_free", n))
            cp(m.lastz[:, zi, 0:1], m.zb[:, TP:TP + 1])
            cp(m.lastz[:, zi, 1:9], sv[:, :, 4])

        z_rows(12)
        ac.wait_ge(*when("zb_used", last_z[0]))
        act(m.lora[0:64, :], m.lora[0:64, :], ACT.Tanh, ("lora_ready",))
        z_rows(13)
        ac.wait_ge(*when("zb_used", last_z[0]))
        act(m.sgd, m.sgd, ACT.Sigmoid, ("sg_ready",))
        for j in range(N_PAIR):
            for base in (0, 4, 8):
                z_rows(base + j)
            ac.wait_ge(*when(*(("mix_ready", j - 1) if j else ("spilled", 0))))
            for dst, func, bias, step in ((m.LW, ACT.Sigmoid, "rwkv_w0", "lw_sig"), (m.Af, ACT.Sigmoid, "rwkv_a0", "a_ready"),
                                          (m.Gf, None, None, "g_ready")):
                n, s = next_set()
                ac.wait_ge(*when("set_done", n))
                for c, (t0, t1) in enumerate(CHUNKS):
                    steps = [(step, j), ("set_free", n)] if c == 2 else []
                    if func is None:
                        cp(dst[:, t0:t1], banks[:, s + c, 0:CH], *steps)
                    else:
                        act(dst[:, t0:t1], banks[:, s + c, 0:CH], func, *steps, bias=vec(bias, j))
            roots(m.T1, ("kk_norm", j))
            next_set()
            ac.wait_ge(*when("lx", j))
            act(m.T1, m.T1, ACT.Exp, ("e_lx", j))
            act(m.KH, m.Lc, ACT.Exp, ("e_l", j))
            act(m.BH, m.Lc, ACT.Exp, ("e_nl", j), scale=-1.0)
            for g, tl, n in GROUPS:
                ac.wait_ge(*when("tm_turned", j, g))
                for t in range(len(tl)):
                    cp(m.TM[0:n, t, :, :], banks[0:n, t, :].rearrange("p (i f) -> p i f", i=4),
                       *([("tm_ready", j, g)] if t == len(tl) - 1 else []))
            next_set()
            roots(m.T1, ("gn_std", j), scale=1.0 / C64, bias=m.eps[:, 1:2])

        ac.wait_ge(*when("shift_turned"))
        ac.wait_ge(*when("mix_ready", 3))
        ac.wait_ge(*when("sout_out", 3))
        for i, (bank, cnt) in enumerate(((0, 512), (1, 512), (2, 512), (3, 256))):
            cp(m.shout[:, i * 512:i * 512 + cnt], banks[0:9, bank, 0:cnt], *([("shout_ready",)] if i == 3 else []))
        ac.wait_ge(*when("usa_zero"))
        for i in range(24):
            half, q = i // 12, i % 12
            gs = slice(16 * half, 16 * half + 16)
            ac.wait_ge(*when("u_done", i))
            if q < 8:
                cp(m.U[:, gs, q, :], banks[:, i % 4, 0:256].rearrange("p (g n) -> p g n", n=G_CH), ("u_copied", i))
            else:
                cp(m.UsA[:, gs, q - 4, :], banks[0:NB, i % 4, 0:256].rearrange("p (g n) -> p g n", n=G_CH), ("u_copied", i))
        ac.wait_ge(*when("s5_in"))
        c = m.c
        act(c["DT"], c["LOGDT"], ACT.Exp, ("dt_exp",))
        ac.wait_ge(*when("angles"))
        act(c["MAG8"], c["W1"], ACT.Exp, scale=float(L8))
        act(c["W1"], c["W1"], ACT.Exp)
        act(c["S1"], c["W3"], ACT.Sin)
        act(c["C1"], c["W4"], ACT.Sin, ("s5_funcs",))
        for q in range(4):
            ac.wait_ge(*when("ut_turned", q))
            if q:
                ac.wait_ge(*when("y_done", q - 1))
            for i in range(4):
                cp(m.UT[:, 2 * i:2 * i + 2, :], banks[:, i, :].rearrange("p (g c) -> p g c", g=2)[:, :, 0:144],
                   *([("ut_copied", q)] if i == 3 else []))
            ac.wait_ge(*when("y_done", q))
            for i in range(2):
                g0 = 64 * i
                src = banks[:, i, :].rearrange("p (g j n) -> p g j n", g=4, n=G_CH)
                dst = m.Yq[:, :, g0:g0 + 64].rearrange("p j (g n) -> p g j n", n=G_CH)
                for gg in range(4):
                    act(dst[:, gg], src[:, gg], ACT.Gelu_apprx_tanh)
                src = banks[0:NB, 2 + i, :].rearrange("p (g j n) -> p g j n", g=4, n=G_CH)[:, :, 0:4, :]
                dst = m.Yqs[:, :, g0:g0 + 64].rearrange("p j (g n) -> p g j n", n=G_CH)
                for gg in range(4):
                    act(dst[:, gg], src[:, gg], ACT.Gelu_apprx_tanh, *([("gelu_done", q)] if (i, gg) == (1, 3) else []))
            ac.wait_ge(*when("y_turned", q))
            for part in range(3):
                src = banks[:, 4 + part, :].rearrange("p (j c) -> p j c", j=4)
                if part < 2:
                    dst = m.yT[:, q, 0:TP].rearrange("p (c j) -> p j c", j=L8)[:, 4 * part:4 * part + 4, :]
                else:
                    dst, src = smp(m.yT[:, q, :]).rearrange("p b j -> p j b"), src[:, :, 0:NB]
                cp(dst, src, ("y_copied", q, part))
        ac.wait_ge(*when("s5_states_turned"))
        cp(m.s5rows[:, 0, :], banks[:, 7, 0:P], ("sfin_rows", 0))
        cp(m.s5rows[:, 1, :], banks[:, 7, P:2 * P], ("sfin_rows", 1))
        cp(m.s5rows[0:32, 2, :], banks[0:32, 7, 256:384], ("sfin_rows", 2))
        for ft in range(4):
            n, s = next_set()
            ac.wait_ge(*when("set_done", n))
            if ft:
                ac.wait_ge(*when("glu_used", ft - 1))
            for c, (t0, t1) in enumerate(CHUNKS):
                act(m.sT[:, t0:t1], banks[:, s + c, 0:CH], ACT.Sigmoid, *([("glu_sig", ft), ("set_free", n)] if c == 2 else []),
                    bias=vec("s5_b_glu", ft))

        def out_and_mlp(layer):
            for _ in range(8):
                next_set()
            ac.wait_ge(*when("x_mid", layer))
            squares(layer, 1)
            for q in range(4):
                for k in range(8):
                    n, s = next_set()
                    ac.wait_ge(*when("set_done", n))
                    for c, (t0, t1) in enumerate(CHUNKS):
                        act(m.mT[:, k, t0:t1], banks[:, s + c, 0:CH], ACT.Relu,
                            *([("relu", n), ("set_free", n)] if c == 2 else []))
                for _ in range(8):
                    next_set()
            ac.wait_ge(*when("x_ready", layer + 1))

        out_and_mlp(0)
        squares(1, 0)
        ac.wait_ge(*when("h_ready", 1, 0))
        ac.wait_ge(*when("spilled", 1))
        for i in range(16):
            n, s = next_set()
            ac.wait_ge(*when("set_done", n))
            for c, (t0, t1) in enumerate(CHUNKS):
                steps = [("set_free", n)] + ([("qk_ready",)] if i == 15 else []) if c == 2 else []
                if i < 8:
                    act(m.qT[:, i, t0:t1], banks[:, s + c, 0:CH], ACT.Copy, *steps, scale=0.125)
                else:
                    cp(m.kT[:, i - 8, t0:t1], banks[:, s + c, 0:CH], *steps)
        cp(m.kTs, m.kT[:, :, TP:T])
        cp(m.qTs, m.qT[:, :, TP:T], ("qs_saved",))
        ac.wait_ge(*when("s5_out"))
        for e in range(36):
            i, t0, cnt = e % 9, *TILES[e % 9]
            c0 = (e // 9) * 256
            ac.wait_ge(*when("v_done", e))
            cp(m.V[0:cnt, i, c0:c0 + 256], banks[0:cnt, 6 + e % 2, 0:256], ("v_copied", e),
               *([("v_rows", i)] if e >= 27 else []))
        for i, (t0, cnt) in enumerate(TILES):
            for half in range(2):
                ac.wait_ge(*when("k_turned", i, half))
                if i >= 4 and half == 0:
                    ac.wait_ge(*when("k_out", i - 4))
                cp(m.kout[0:cnt, i % 4, half * 512:half * 512 + 512], banks[0:cnt, half, :], ("k_copied", i, half),
                   *([("k_rows", i)] if half else []))
        for i in range(5, 9):
            ac.wait_ge(*when("k_out", i))
        for s in range(64):
            h, i = s // 8, s % 8
            nk = (i + 1) * P
            st = m.st[:, s % 2, :]

            def finish(s):
                h, i = s // 8, s % 8
                ac.wait_ge(*when("pt_turned", s))
                for b0 in range(0, i + 1, 4):
                    b1 = min(b0 + 4, i + 1)
                    cp(m.PTp[:, b0:b1, :], banks[:, 4 + b0 // 4, 0:(b1 - b0) * P].rearrange("p (b q) -> p b q", q=P),
                       *([("pt_copied", s)] if b1 == i + 1 else []))
                ac.wait_ge(*when("o_done", s))
                cp(m.oT[:, h, i * P:i * P + P], banks[:, 6 + s % 2, 0:P], ("o_copied", s))

            ac.wait_ge(*when("row_max", s))
            if s >= 2:
                ac.wait_ge(*when("pt_turned", s - 2))
            for c in range(2):
                row = banks[:, 2 * c:2 * c + 2, :].rearrange("p b k -> p (b k)")[:, 0:nk]
                act(m.Pp[:, s % 2, c, 0:nk], row, ACT.Exp, *([("scores_free", s)] if c else []),
                    bias=st[:, 2 + c:3 + c], accum=st[:, 4 + c:5 + c])
            if s:
                finish(s - 1)
        finish(63)
        scalar_sample_attention(nc, ac, led, m, act, cp)
        ac.wait_ge(*when("oT_done"))
        for h in range(H_C):
            act(m.sq2, m.oT[:, h, :], ACT.Square, ("o_sq", h))
            if h >= 2:
                ac.wait_ge(*when("o_normed", h - 2))
            roots(m.r2[:, h % 2, :], ("o_std", h), scale=float(D // P), bias=m.eps[:, 0:1])
        out_and_mlp(1)
        squares(2, 0)
        for i, (t0, cnt) in enumerate(TILES):
            for half in range(2):
                ac.wait_ge(*when("y_row_turned", i, half))
                if i >= 2 and half == 0:
                    ac.wait_ge(*when("y_out", i - 2))
                cp(m.yrow[0:cnt, i % 2, half * 512:half * 512 + 512], banks[0:cnt, 6 + half, :],
                   ("y_row_copied", i, half), *([("y_rows", i)] if half else []))


def scalar_sample_attention(nc, ac, led, m, act, cp):
    when = led.when
    banks = m.banks
    for b in range(NB):
        for p in range(N_PAGES):
            e = b * N_PAGES + p
            ac.wait_ge(*when("page_turned", e, 0))
            if e >= 2:
                ac.wait_ge(*when("page_scored", e - 2))
            cp(m.KTp[:, p % 2, 0:4, :], banks[:, 4, :].rearrange("p (h k) -> p h k", h=4), ("page_copied", e, 0))
        ac.wait_ge(*when("s_max", b))
        ss = m.ss[0:64, :]
        if b:
            ac.wait_ge(*when("pts_done", b - 1))
        act(m.Ps[:, 0:2048], banks[0:64, 0:4, :].rearrange("p b k -> p (b k)"), ACT.Exp, bias=ss[:, 3:4],
            accum=ss[:, 4:5])
        act(m.Ps[:, 2048:2048 + NS], m.Sn, ACT.Exp, ("s_exp", b), bias=ss[:, 3:4], accum=ss[:, 5:6])


_OUTS = [("y_prompt", (1, 1024, 1024)), ("y_sample", (8, 4, 1024)), ("p_shift", (1, 1792)), ("p_wkv", (1, 8, 64, 64)),
         ("p_ssm_re", (1, 32, 64)), ("p_ssm_im", (1, 32, 64)), ("p_k", (1, 1024, 8, 128)), ("p_v", (1, 1024, 8, 128)),
         ("s_shift", (8, 1792)), ("s_wkv", (8, 8, 64, 64)), ("s_ssm_re", (8, 32, 64)), ("s_ssm_im", (8, 32, 64)),
         ("s_k", (8, 4, 8, 128)), ("s_v", (8, 4, 8, 128))]


def kernel(**inputs):
    import concourse.bacc as bacc
    from concourse.bass_utils import run_bass_kernel_spmd as run

    arrays = {f"in_{k}": np.ascontiguousarray(v) for k, v in inputs.items()}

    def build(known):
        nc = bacc.Bacc("TRN2", target_bir_lowering=False, num_devices=1)
        a = {k[3:]: nc.dram_tensor(k, v.shape, mybir.dt.from_np(v.dtype), kind="ExternalInput").ap()
             for k, v in arrays.items()}
        o = {n: nc.dram_tensor(f"out_{n}", s, F32, kind="ExternalOutput").ap() for n, s in _OUTS}
        return nc, decoder_step(nc, a, o, known)

    _, known = build(None)
    nc, _ = build(known)
    r = run(nc, [arrays], core_ids=[0])
    return tuple(r.results[0][f"out_{n}"] for n, _ in _OUTS)
```

```python
import math
from contextlib import ExitStack

import numpy as np
import concourse.bass as bass
from concourse import mybir

F32 = mybir.dt.float32
I32 = mybir.dt.int32
ALU = mybir.AluOpType
ACT = mybir.ActivationFunctionType
AX = mybir.AxisListType

P = 128
D = 1024
KT = D // P
TP, NB, TS = 1024, 8, 4
NS = NB * TS
T = TP + NS
CH = T // 3
CHUNKS = [(i * CH, (i + 1) * CH) for i in range(3)]
TILES = [(i * P, P) for i in range(TP // P)] + [(TP, NS)]
N_PAIR = 4
ZT = 14
C64 = 64
N_G, G_CH, S_ST = 32, 16, 64
L8 = 8
NC8 = TP // L8
H_C, PAGE, N_PAGES, N_POOL = 8, 128, 16, 160
EPS, GN_EPS = 1e-6, 64e-5
DECAY = math.exp(-0.5)
LAM0 = 0.8 - 0.6 * math.exp(-0.3)
NEG = -1e30
TWO_PI_HI = 6.28125
TWO_PI_LO = 2 * math.pi - TWO_PI_HI
ROUND = 1.5 * 2.0 ** 23
PI_IN = 3.1415925

VEC = {}
for _name, _rows in (("norm_mix", 16), ("norm_mlp", 16), ("norm_f", 8), ("rwkv_mu", 14), ("rwkv_w0", 4),
                     ("rwkv_a0", 4), ("rwkv_k_k", 4), ("rwkv_k_a", 4), ("rwkv_r_k", 4), ("rwkv_lnx_w", 4),
                     ("rwkv_lnx_b", 4), ("s5_b_glu", 4), ("diff_subln", 1)):
    VEC[_name] = (sum(n for _, n in VEC.values()), _rows)
N_VEC = sum(n for _, n in VEC.values())
SH_M, SC_M, G_M, SH_F, SC_F, G_F = range(0, 48, 8)

N_ADA, ADA_FIRST = 48, 8
ADA_PAIR = (N_ADA - ADA_FIRST) // N_PAIR
ADA_BATCH = (3, 3, ADA_PAIR - 6)
AT_IN = ADA_FIRST
AT_PAIRS = AT_IN + 1
AT_U = AT_PAIRS + (2 + ADA_PAIR) * N_PAIR
AT_GLU = AT_U + 2
AT_OUT = [AT_GLU + 1, None]
AT_MLP = [AT_OUT[0] + 4, None]
AT_QKV = AT_MLP[0] + 32
AT_OUT[1] = AT_QKV + 12
AT_MLP[1] = AT_OUT[1] + 4
N_ITEMS = AT_MLP[1] + 32


def at_pair(j):
    return AT_PAIRS + (2 + ADA_PAIR) * j


def at_ada(n):
    return n if n < ADA_FIRST else at_pair((n - ADA_FIRST) // ADA_PAIR) + 2 + (n - ADA_FIRST) % ADA_PAIR


def ada_batches(j):
    n = ADA_FIRST + j * ADA_PAIR
    for count in ADA_BATCH:
        yield n, n + count
        n += count


def weight_stream(w):
    def dense(src, k0, c0, n):
        return [[(src[k0:k0 + 1024, :], c0 + i * 256, 256)] for i in range(n)]

    def mlp(layer):
        return [x for q in range(4)
                for x in dense(w["w_up"][layer], 0, q * 1024, 4) + dense(w["w_down"][layer], q * 1024, 0, 4)]

    w_in = w["w_in_ab"]
    ada = dense(w["w_ada"][0], 0, 0, 24) + dense(w["w_ada"][1], 0, 0, 24)
    items = ada[:ADA_FIRST] + dense(w_in, 0, 1536, 1)
    for j in range(N_PAIR):
        items.append([(w_in, j * P, P), (w_in, 512 + j * P, P)])
        items.append([(w_in, 1024 + j * P, P)])
        items += ada[ADA_FIRST + j * ADA_PAIR:ADA_FIRST + (j + 1) * ADA_PAIR]
    items += dense(w_in, 0, 1792, 2) + [[(w["s5_w_glu"], 0, 512)]]
    items += dense(w["w_out"][0], 0, 0, 4) + mlp(0)
    items += dense(w["diff_w_qkv"], 0, 0, 12)
    items += dense(w["w_out"][1], 0, 0, 4) + mlp(1)
    assert len(items) == N_ITEMS
    return items


KIND = {step: kind for kind, steps in {
    "start": "step masks consts cond_sig silu vecs_turned cond_turned condT lam_dots lam_exps xin_turned xin_copied "
             "mod_sums mod_copied mod_turned mod_biased zb_zero",
    "norm": "squares ssq sq_added std h_ready",
    "tile": "x_tile set_done set_free relu x_mid x_part x_ready hidden mixed weights_used zb_ready zb_used",
    "mix_in": "lora_ready sg_ready lw_sig a_ready g_ready kk_sq rk_prod lx e_lx e_l e_nl kk_norm gn_std s0_turned s0_copied "
              "sfin_turned sout_ready gn_sq mix_ready",
    "chunk": "tm_turned tm_ready grams gram_masked d2 d2_copied d2_copied_t d4 d4_copied d4_copied_t d8 d8_added "
             "d8_copied f4p f_level level_p1 level_copied_t q_copied "
             "level_copied level_p2 akkv m_ready rhs_ready xy xy_copied zq zq_copied tt tt_ready rw_free o_sample "
             "o_ready mb_ready tts tts_ready states_new states_final",
    "state": "state state_new",
    "s5": "shift_turned shout_ready u_done u_copied s5_turned crow_turned crow_copied ut_turned ut_copied toeplitz "
          "etx_copied ety_turned ety_copied left h_states y_done gelu_done y_turned y_copied s5_states_turned "
          "sfin_rows d_rows dt_exp angles s5_funcs powers glu_sig glu_used usa_zero",
    "attend": "v_done v_copied qs_saved k_turned k_copied scores scores_free row_max probs pt_turned pt_copied o_done "
              "o_copied",
    "sample": "qpad_zero qpad s_new page_turned page_copied page_scored page_used s_max s_exp s_coef pts_done "
              "pts_copied os_ready os_copied os_turned os_done o_sq o_std o_normed",
    "rows": "y_row_turned y_row_copied",
}.items() for step in steps.split()}


class Ledger:

    def __init__(self, nc, ctx, known):
        self.nc, self.ctx, self.known = nc, ctx, known
        self.sems, self.count, self.at = {}, {}, {}

    def sem(self, name):
        if name not in self.sems:
            self.sems[name] = self.ctx.enter_context(self.nc.semaphore(name))
        return self.sems[name]

    def sig(self, engine, *steps, by=1):
        name = f"{engine}_{KIND.get(steps[0][0], steps[0][0])}"
        self.count[name] = self.count.get(name, 0) + by
        for step in steps:
            self.at[step] = (name, self.count[name])
        return self.sem(name), by

    def when(self, *step):
        if self.known is None:
            return self.sem("first_build"), 1
        name, value = self.known[step]
        return self.sem(name), value

    def own(self, engine, step):
        name = f"{engine}_{KIND.get(step[0], step[0])}"
        return self.sem(name), self.count[name]


class Region:

    def __init__(self, buf, size):
        self.buf, self.size, self.at = buf, size, 0

    def take(self, *shape, parts=P):
        n = int(np.prod(shape))
        assert self.at + n <= self.size, (self.at, n, self.size)
        ap = self.buf[0:parts, self.at:self.at + n]
        self.at += n
        if len(shape) == 1:
            return ap
        names = " ".join(f"d{i}" for i in range(len(shape)))
        return ap.rearrange(f"p ({names}) -> p {names}", **{f"d{i}": s for i, s in enumerate(shape)})


def mid(ap, n):
    return ap.unsqueeze(1).to_broadcast([ap.shape[0], n, ap.shape[1]])


def rep(ap, n):
    return ap.unsqueeze(len(ap.shape)).to_broadcast(list(ap.shape) + [n])


def smp(ap):
    return ap[:, TP:T].rearrange("p (b q) -> p b q", q=TS)


S5_ROWS = ("LOGDT", "LI", "DT", "AR", "AI", "MAG8", "FR", "FI", "C1", "S1", "A4R", "A4I", "P8C", "P8S", "LR", "DC",
           "TH", "W1", "W2", "W3", "W4")
U64, UI64, U16, NUI64, L16, L32, L64, CAUSAL = range(8)
U4, UI4, U4B, NUI4, L4 = range(5)
N_TILE, N_STAGE, TILE_LAG = TP // P, 13, 7
S_TM, S_D2, S_D4, S_D8, S_F, S_L1, S_L2, S_M1, S_M2, S_XY, S_ZQ, S_C0, S_C1 = range(N_STAGE)


def tile_stages():
    for slot in range(TILE_LAG * (N_TILE - 1) + N_STAGE):
        for k in range(N_TILE):
            if 0 <= slot - TILE_LAG * k < N_STAGE:
                yield k, slot - TILE_LAG * k


class Memory:

    def __init__(self, nc, ctx):
        def sb(name, shape, dt=F32):
            return ctx.enter_context(nc.sbuf_tensor(name, shape, dt))

        def tiles(buf):
            return buf[:, 0:KT * T].rearrange("p (k t) -> p k t", t=T)

        self.xbuf, self.hbuf, self.mbuf = (sb(n, [P, KT * T]) for n in ("xbuf", "hbuf", "mbuf"))
        self.xT, self.hT, self.mT = tiles(self.xbuf), tiles(self.hbuf), tiles(self.mbuf)
        self.ring = sb("ring", [P, 4, 2048])
        WORK = 15900
        work = self.work = sb("work", [P, WORK])
        self.ident, self.mean1, self.bd1 = (sb(n, [P, P]) for n in ("ident", "mean1", "bd1"))
        self.msk = sb("msk", [P, 8, P])
        self.msk4 = sb("msk4", [NS, 5, NS])
        self.vecT = sb("vecT", [P, P])
        self.bT = sb("bT", [P, 96])
        self.modT = sb("modT", [P, 2, 48, 9])
        self.gain = sb("gain", [P, 2, 2, KT, 9])
        self.condT = sb("condT", [P, KT, 9])
        self.shiftT = sb("shiftT", [P, ZT, NB])
        self.lastz = sb("lastz", [P, ZT, 9])
        self.lam = sb("lam", [P, 8])
        self.eps = sb("eps", [P, 2])
        self.banks = ctx.enter_context(nc.psum_tensor("banks", [P, 8, 512], F32))
        self.spill = nc.dram_tensor("x_spill", (P, KT * T), F32, kind="Internal").ap()

        h = self.hbuf
        self.vrows = h[:, 7100:7228]
        self.brows, self.crows, self.csig = h[0:96, 0:P], h[0:9, 1024:2048], h[0:9, 6000:7024]
        self.srows = h[0:8, 2048:2048 + ZT * P]
        self.lrows = h[0:1, 4096:4352]
        self.modrow = self.mbuf[0:9, 3 * T:3 * T + 256]
        self.sq = work[:, 0:2 * T].rearrange("p (i t) -> p i t", i=2)
        self.rstd = work[:, 2 * T:3 * T]
        self.ssq = self.hT[:, KT - 1, :]

        r = Region(work, WORK)
        self.zb = r.take(1025 + 40)
        chunkwise = Region(work[:, 8:8 + 1024], 1024)
        self.XY, self.ZTt, self.QTt = chunkwise.take(2, 2, 2, C64), chunkwise.take(2, P), chunkwise.take(2, P)
        self.lora, self.sgd = r.take(T), r.take(T)
        self.lorw = r.take(2, 512)
        self.KR = r.take(2, T)
        self.Kf, self.Vf, self.Af, self.Gf, self.BON = (r.take(T) for _ in range(5))
        self.S0in = r.take(NB, P)
        self.SBD = r.take(9, P)
        self.PW = r.take(2, 4, P)
        self.TT = r.take(4, P)
        self.SOUT = r.take(9, C64)
        r = Region(self.xbuf, KT * T)
        self.LW, self.Lc, self.T1, self.KH, self.BH, self.rowm = (r.take(T) for _ in range(6))
        self.QO = self.LW
        self.WC = r.take(16 + 8)
        self.eb = r.take(NB)
        self.G4 = r.take(2, 2, 4, P)
        r = Region(self.mbuf[:, 4 * T:8 * T], 4 * T)
        self.TM = r.take(2, 4, P)
        self.FF, self.FT = r.take(4, P), r.take(4, P)
        self.RHS = r.take(2, 2, 2, C64)
        self.G3 = r.take(2, 2, 3, P)
        self.MB = self.mbuf[:, 4 * T + 3072:4 * T + 4096].rearrange("p (b i f) -> p b i f", b=4, i=2)

        r = Region(self.xbuf, KT * T)
        self.U = r.take(N_G, L8, G_CH)
        self.yT = r.take(4, T)
        r = Region(work, WORK)
        self.UsA = r.take(N_G, 12, G_CH, parts=8)
        self.sT = r.take(T)
        self.BX, self.BY, self.CX, self.CY = (r.take(N_G, G_CH) for _ in range(4))
        self.h0 = r.take(2, NB, N_G)
        self.h4, self.hfin = r.take(NB, N_G), r.take(N_G)
        self.c = {name: r.take(N_G) for name in S5_ROWS}
        self.s5rows = r.take(4, P)
        self.rows2 = r.take(2, P)
        self.BBp = r.take(8, 15, G_CH)
        self.shout = self.BBp.rearrange("p a b c -> p (a b c)")[0:9, 0:ZT * P]
        self.phc = r.take(4, 8)
        self.Hs = r.take(8, NC8 + 1)
        self.COS = r.take(8, P)
        self.SIN = self.sT[:, 0:1024].rearrange("p (g c) -> p g c", g=8)
        r = Region(self.hbuf, KT * T)
        self.UT = r.take(8, 144)
        self.CAp, self.ABx, self.ABy = r.take(8, 16, G_CH), r.take(8, L8, G_CH), r.take(8, L8, G_CH)
        self.CYr, self.q1, self.q2 = r.take(8, G_CH), r.take(8, G_CH), r.take(8, G_CH)
        self.ETx, self.Tm = r.take(8, P), r.take(8, P)
        self.Yq = self.ETx
        self.Yqs = r.take(4, P, parts=NB)
        r = Region(self.mbuf[:, 4 * T:8 * T], 4 * T)
        self.ETy, self.G1, self.G2, self.q3 = (r.take(8, P) for _ in range(4))

        self.qT, self.kT = self.mT, self.xT
        self.oT = self.qT
        r = Region(work, WORK)
        self.V = r.take(9, D)
        self.PTp = r.take(8, P)
        self.Pp = self.hbuf[:, 0:6 * D].rearrange("p (a b d) -> p a b d", a=3, b=2)
        self.kout = self.hbuf[:, 0:4 * D].rearrange("p (a d) -> p a d", a=4)
        self.st = r.take(3, 16)
        self.kTs = r.take(KT, NS)
        self.sq2 = self.hbuf[:, 3 * T:5 * T].rearrange("p (i t) -> p i t", i=2)
        self.r2 = self.hbuf[:, T:3 * T].rearrange("p (i t) -> p i t", i=2)
        self.qTs, self.nmask, self.csel = r.take(KT, NS), r.take(15, 4), r.take(NS)
        r = Region(self.xbuf, KT * T)
        self.KTp = r.take(2, KT, P)
        self.Ps = r.take(2048 + NS, parts=64)
        self.PTs = r.take(17, NS)
        self.Os = r.take(D, parts=NS)
        self.Sn = r.take(NS, parts=64)
        self.Cm = r.take(NS, parts=64)
        self.qpad = r.take(2, 576)
        self.ss = r.take(16)
        self.sel4 = r.take(4)
        self.pt = sb("page_table_sb", [1, P], I32)

        self.yrow = self.mbuf[:, 0:2 * D].rearrange("p (i d) -> p i d", i=2)

    def mask(self, i, n=P):
        return self.msk4[:, i, :] if n == NS else self.msk[:, i, :]

    def vec(self, name, i=0):
        r = VEC[name][0] + i
        return self.vecT[:, r:r + 1]

    def slot(self, n):
        return self.ring[:, n % 4, :]

    def wblock(self, n, width=256, at=0):
        return self.slot(n)[:, at:at + 8 * width].rearrange("p (k m) -> p k m", k=8)

    def page(self, n):
        return self.ring[:, (n % 8) // 2, (n % 2) * 1024:(n % 2) * 1024 + 1024]


def decoder_step(nc, a, o, known):
    with ExitStack() as ctx:
        led = Ledger(nc, ctx, known)
        m = Memory(nc, ctx)
        block = ctx.enter_context(nc.Block())
        sync_program(nc, block, led, m, a, o)
        gpsimd_program(nc, block, led, m, a, o)
        tensor_program(nc, block, led, m)
        vector_program(nc, block, led, m)
        scalar_program(nc, block, led, m)
        return led.at


def sync_program(nc, block, led, m, a, o):
    sig, when = led.sig, led.when

    @block.sync
    def _(sp):
        def load(dst, src, step):
            sp.dma_start(dst, src).then_inc(*sig("dma", step, by=16))

        for name, (r, n) in VEC.items():
            src = a[name]
            if len(src.shape) == 2:
                src = src.rearrange("a b -> (a b)")
            load(m.vrows[r:r + n, :], src.rearrange("(r c) -> r c", c=P), ("params_in",))
        load(m.brows, a["b_ada"].rearrange("l (r c) -> (l r) c", c=P), ("params_in",))
        load(m.crows[0:1, :], a["c_prompt"], ("params_in",))
        load(m.crows[1:9, :], a["c_sample"], ("params_in",))
        load(m.srows, a["state_shift"], ("params_in",))
        load(m.lorw[0:64, 0, :], a["rwkv_w_up"], ("params_in",))
        load(m.lorw[64:128, 0, :], a["rwkv_a_up"], ("params_in",))
        load(m.lorw[:, 1, :], a["rwkv_g_up"], ("params_in",))
        load(m.pt[:, :], a["page_table"].rearrange("b (o n) -> o (b n)", o=1), ("params_in",))
        for i, n in enumerate(("diff_lq1", "diff_lk1", "diff_lq2", "diff_lk2")):
            load(m.lrows[:, 64 * i:64 * i + 64], a[n].rearrange("(o c) -> o c", o=1), ("params_in",))

        stream = weight_stream(a)

        def weights(first, last):
            for n in range(first, last):
                if n >= 4:
                    sp.wait_ge(*when("weights_used", n - 4))
                if n == AT_OUT[1]:
                    sp.wait_ge(*when("pages_done"))
                at = 0
                for src, c0, cols in stream[n]:
                    kt = src.shape[0] // P
                    dst = m.slot(n)[:, at:at + kt * cols].rearrange("p (k c) -> p k c", k=kt)
                    sp.dma_start(dst, src[:, c0:c0 + cols].rearrange("(k p) c -> p k c", p=P)) \
                      .then_inc(*sig(f"slot{n % 4}", ("weights_in", n), by=16))
                    at += kt * cols

        for i, (t0, n) in enumerate(TILES):
            if i >= 2:
                sp.wait_ge(*when("xin_used", i - 2))
            src = a["x_prompt"][0, t0:t0 + n, :] if i < 8 else a["x_sample"].rearrange("b q d -> (b q) d")
            sp.dma_start(m.yrow[0:n, i % 2, :], src).then_inc(*sig(f"slot{i % 2}", ("xin", i), by=16))
        weights(0, 4)
        sp.wait_ge(*when("x_ready", 0))
        sp.dma_start(m.spill, m.xbuf[:, :]).then_inc(*sig("dma", ("spilled", 0), by=16))
        weights(4, AT_GLU + 4)
        sp.wait_ge(*when("mixed", 0))
        sp.dma_start(m.xbuf[:, :], m.spill).then_inc(*sig("dma", ("x_back", 0), by=16))
        weights(AT_GLU + 4, AT_QKV + 3)
        sp.wait_ge(*when("x_ready", 1))
        sp.dma_start(m.spill, m.xbuf[:, :]).then_inc(*sig("dma", ("spilled", 1), by=16))
        weights(AT_QKV + 3, AT_OUT[1])
        for b in range(NB):
            for kind, cache in enumerate(("cache_k", "cache_v")):
                for p in range(N_PAGES):
                    n = (b * 2 + kind) * N_PAGES + p
                    if n < 8:
                        sp.wait_ge(*when("weights_used", AT_OUT[1] - 4 + n // 2))
                    else:
                        sp.wait_ge(*when("page_used", n - 8))
                    i = b * N_PAGES + p
                    page = sp.value_load(m.pt[0:1, i:i + 1], min_val=0, max_val=N_POOL - 1)
                    sp.dma_start(m.page(n), a[cache][bass.ds(page, 1)].rearrange("o t h d -> (o t) (h d)")) \
                      .then_inc(*sig(f"page{n % 8}", ("page_in", n), by=16))
        weights(AT_OUT[1], AT_OUT[1] + 4)
        sp.wait_ge(*when("oT_done"))
        sp.dma_start(m.xbuf[:, :], m.spill).then_inc(*sig("dma", ("x_back", 1), by=16))
        weights(AT_OUT[1] + 4, N_ITEMS)


def gpsimd_program(nc, block, led, m, a, o):
    sig, when = led.sig, led.when

    @block.gpsimd
    def _(pool):
        def do(ins, *steps):
            steps = steps or (("step",),)
            ins.then_inc(*sig("pool", *steps))
            pool.wait_ge(*led.own("pool", steps[0]))

        def sel(ap, op, base, pattern, cm, fill=0.0):
            do(nc.gpsimd.affine_select(out=ap, in_=ap, compare_op=op, fill=fill, base=base,
                                       pattern=pattern, channel_multiplier=cm))

        def dma(dst, src, step):
            pool.dma_start(dst, src).then_inc(*sig("pooldma", step, by=16))

        do(nc.gpsimd.memset(m.ident[:, :], 0.0))
        sel(m.ident[:, :], ALU.not_equal, 0, [[-1, P]], 1, fill=1.0)
        do(nc.gpsimd.memset(m.mean1[:, :], 1.0 / D))
        do(nc.gpsimd.memset(m.msk[:, :, :], 1.0))
        do(nc.gpsimd.memset(m.bd1[:, :], 1.0))
        do(nc.gpsimd.memset(m.msk[:, CAUSAL, :], 0.0))

        do(nc.gpsimd.memset(m.msk4[:, :, :], 1.0))

        def block_diagonal(ap, n):
            blocks = ap.shape[1] // n
            v = ap.rearrange("p (b c) -> p b c", c=n)
            sel(v, ALU.is_ge, 0, [[-n, blocks], [0, n]], 1)
            sel(v, ALU.is_ge, n - 1, [[n, blocks], [0, n]], -1)

        block_diagonal(m.bd1[:, :], C64)
        for mk, n, kind in ([(m.msk[:, i, :], n, kind) for i, n, kind in
                             ((U16, 16, "u"), (U64, 64, "u"), (UI64, 64, "ui"), (L16, 16, "l"),
                              (L32, 32, "l"), (L64, 64, "l"))] +
                            [(m.msk4[:, i, :], 4, kind) for i, kind in ((U4, "u"), (UI4, "ui"), (U4B, "u"), (L4, "l"))]):
            cols = mk.shape[1]
            block_diagonal(mk, n)
            if kind == "u":
                sel(mk, ALU.is_gt, 0, [[1, cols]], -1)
            elif kind == "ui":
                sel(mk, ALU.is_ge, 0, [[1, cols]], -1)
            else:
                sel(mk, ALU.is_gt, 0, [[-1, cols]], 1)
        sel(m.msk[:, CAUSAL, :], ALU.is_ge, 0, [[-1, P]], 1, fill=NEG)
        do(nc.gpsimd.memset(m.eps[:, 0:1], EPS))
        do(nc.gpsimd.memset(m.eps[:, 1:2], GN_EPS), ("masks",))
        pool.wait_ge(*when("h_ready", 0, 0))
        do(nc.gpsimd.memset(m.zb[:, 0:1], 0.0), ("zb_zero",))
        do(nc.gpsimd.memset(m.S0in[:, :, :], 0.0))
        for j in range(N_PAIR):
            if j:
                pool.wait_ge(*when("s0_turned", j - 1))
            for hh in range(2):
                dma(m.S0in[64 * hh:64 * hh + 64, :, 64 * hh:64 * hh + 64],
                    a["state_wkv"][:, 2 * j + hh].rearrange("b v k -> v b k"), ("s0_in", j))
            pool.wait_ge(*when("sout_ready", j))
            dma(o["p_wkv"][0, 2 * j:2 * j + 2].rearrange("h v k -> (h v) k"), m.SOUT[:, 0, :], ("sout_out", j))
            dma(o["s_wkv"][:, 2 * j:2 * j + 2].rearrange("b h v k -> (h v) b k"), m.SOUT[:, 1:9, :], ("sout_out", j))

        pool.wait_ge(*when("mix_ready", N_PAIR - 1))
        pool.wait_ge(*when("sout_out", N_PAIR - 1))
        do(nc.gpsimd.memset(m.UsA, 0.0), ("usa_zero",))
        for h in range(2):
            dma(m.s5rows[0:32, 0, 64 * h:64 * h + 64], a["s5_lam_re"], ("s5_in",))
            dma(m.s5rows[0:32, 1, 64 * h:64 * h + 64], a["s5_lam_im"], ("s5_in",))
            hs = slice(64 * h, 64 * h + 64)
            for dst, src in ((m.BX, ("s5_b_re", "s5_b_im")[h]), (m.BY, ("s5_b_im", "s5_b_re")[h])):
                dma(dst[hs, :, :], a[src].rearrange("g p n -> p g n"), ("s5_in",))
        dma(m.c["LOGDT"], a["s5_log_dt"].rearrange("(o g) -> o g", o=1).to_broadcast([P, N_G]), ("s5_in",))
        dma(m.s5rows[0:32, 2, 0:16], a["s5_d"], ("s5_in",))
        for i in range(4):
            for v, (x, y) in enumerate((("s5_c_re", "s5_c_im"), ("s5_c_im", "s5_c_re"))):
                k = i * 2 + v
                if k >= 2:
                    pool.wait_ge(*when("crow_turned", k - 2))
                for h, src in enumerate((x, y)):
                    pool.dma_start(m.rows2[:, k % 2, 64 * h:64 * h + 64],
                                   a[src][8 * i:8 * i + 8].rearrange("g n p -> (g n) p")) \
                        .then_inc(*sig(f"rows{k % 2}", ("crow_in", k), by=16))
        for i in range(2):
            for v, (x, y) in enumerate((("re", "im"), ("im", "re"))):
                k = 8 + i * 2 + v
                pool.wait_ge(*when("crow_turned", k - 2))
                for h, src in enumerate((x, y)):
                    pool.dma_start(m.rows2[:, k % 2, 64 * h:64 * h + 64],
                                   a[f"state_ssm_{src}"][4 * i:4 * i + 4].rearrange("b g p -> (b g) p")) \
                        .then_inc(*sig(f"rows{k % 2}", ("crow_in", k), by=16))
        pool.wait_ge(*when("shout_ready"))
        dma(o["p_shift"], m.shout[0:1, :], ("shift_out",))
        dma(o["s_shift"], m.shout[1:9, :], ("shift_out",))
        for i in range(3):
            pool.wait_ge(*when("sfin_rows", i))
            for h, n in enumerate(("re", "im")):
                hs = slice(64 * h, 64 * h + 64)
                if i < 2:
                    dma(o[f"s_ssm_{n}"][4 * i:4 * i + 4].rearrange("b g p -> (b g) p"), m.s5rows[:, i, hs], ("s5_out",))
                else:
                    dma(o[f"p_ssm_{n}"][0], m.s5rows[0:32, 2, hs], ("s5_out",))
        for i, (t0, n) in enumerate(TILES):
            def rows(t):
                return t[0, t0:t0 + n].rearrange("t h d -> t (h d)")

            def srows(t):
                return t.rearrange("b q h d -> (b q) (h d)")
            pool.wait_ge(*when("v_rows", i))
            dma(rows(o["p_v"]) if i < 8 else srows(o["s_v"]), m.V[0:n, i, :], ("out",))
        for i, (t0, n) in enumerate(TILES):
            pool.wait_ge(*when("k_rows", i))
            dst = o["p_k"][0, t0:t0 + n].rearrange("t h d -> t (h d)") if i < 8 else \
                o["s_k"].rearrange("b q h d -> (b q) (h d)")
            pool.dma_start(dst, m.kout[0:n, i % 4, :]).then_inc(*sig(f"kout{i % 4}", ("k_out", i), by=16))
        for i, (t0, n) in enumerate(TILES):
            pool.wait_ge(*when("y_rows", i))
            dst = o["y_prompt"][0, t0:t0 + n, :] if i < 8 else o["y_sample"].rearrange("b q d -> (b q) d")
            pool.dma_start(dst, m.yrow[0:n, i % 2, :]).then_inc(*sig(f"yout{i % 2}", ("y_out", i), by=16))
        for i in (7, 8):
            pool.wait_ge(*when("y_out", i))
        for i in range(5, 9):
            pool.wait_ge(*when("k_out", i))
        pool.wait_ge(*when("out"))
        pool.wait_ge(*when("s5_out"))


def tensor_program(nc, block, led, m):
    sig, when = led.sig, led.when
    banks = m.banks

    @block.tensor
    def _(pe):
        def mm(out, lhsT, rhs, start=True, stop=True):
            return nc.tensor.matmul(out, lhsT, rhs, start=start, stop=stop)

        def tr(out, in_):
            k = in_.shape[0]
            return nc.tensor.transpose(out, in_, m.ident[0:k, 0:k])

        n_tile = [0]

        def ptile(lhs, rhs, kts=KT, used=None, ready=None):
            n = n_tile[0]
            n_tile[0] += 1
            if n >= 2:
                pe.wait_ge(*when("set_free", n - 2))
            for k in range(kts):
                if ready is not None:
                    pe.wait_ge(*when(*ready[k]))
                for c, (t0, t1) in enumerate(CHUNKS):
                    last = mm(banks[:, 3 * (n % 2) + c, 0:CH], lhs(k), rhs(k)[:, t0:t1], k == 0, k == kts - 1)
            last.then_inc(*sig("pe", ("set_done", n), *([("weights_used", used)] if used is not None else [])))

        def norm_steps(layer, w):
            return [("h_ready", layer, w, k) for k in range(KT)]

        def dense_tiles(n0, items, src, ready=None):
            for n in range(n0, n0 + items):
                pe.wait_ge(*when("weights_in", n))
                for half in range(2):
                    w = m.wblock(n)[:, :, half * P:half * P + P]
                    ptile(lambda k: w[:, k, :], lambda k: src[:, k, :], used=n if half else None,
                          ready=ready if n == n0 and not half else None)

        pe.wait_ge(*when("consts"))
        pe.wait_ge(*when("params_in"))
        tr(banks[:, 0, 0:N_VEC], m.vrows[0:N_VEC, :])
        tr(banks[:, 0, 128:224], m.brows)
        for k in range(ZT):
            last = tr(banks[:, 2, k * NB:k * NB + NB], m.srows[:, k * P:k * P + P])
        last.then_inc(*sig("pe", ("vecs_turned",)))
        pe.wait_ge(*when("silu"))
        for k in range(KT):
            last = tr(banks[:, 1, k * 9:k * 9 + 9], m.crows[:, k * P:k * P + P])
        last.then_inc(*sig("pe", ("cond_turned",)))

        for i, (t0, n) in enumerate(TILES):
            pe.wait_ge(*when("xin", i))
            for half in range(2):
                if i:
                    pe.wait_ge(*when("xin_copied", i - 1, half))
                for q in range(4):
                    k = half * 4 + q
                    last = tr(banks[:, 6 + half, q * P:q * P + n], m.yrow[0:n, i % 2, k * P:k * P + P])
                last.then_inc(*sig("pe", ("xin_turned", i, half)))

        def modulation(first, last):
            for n in range(first, last + 1):
                if n == first and n:
                    pe.wait_ge(*when("mod_biased", n - 1))
                elif n >= first + 2:
                    pe.wait_ge(*when("mod_biased" if n >= first + 3 else "mod_copied", n - 3 if n >= first + 3 else n - 2))
                if n < last:
                    pe.wait_ge(*when("weights_in", at_ada(n)))
                    for k in range(KT):
                        ins = mm(banks[0:9, 6 + n % 2, 0:256], m.condT[:, k, :], m.wblock(at_ada(n))[:, k, :],
                                 k == 0, k == KT - 1)
                    ins.then_inc(*sig("pe", ("mod_sums", n), ("weights_used", at_ada(n))))
                if n > first:
                    pe.wait_ge(*when("mod_copied", n - 1))
                    for h in range(2):
                        ins = tr(banks[:, 6 + n % 2, 256 + h * 16:256 + h * 16 + 9], m.modrow[:, h * P:h * P + P])
                    ins.then_inc(*sig("pe", ("mod_turned", n - 1)))

        pe.wait_ge(*when("condT"))
        pe.wait_ge(*when("lam_exps"))
        mm(banks[:, 4, 0:2], m.mean1[0:1, :], m.lam[0:1, 2:4])
        for half in range(2):
            pe.wait_ge(*when("xin_copied", 8, half))
        def norm_sums(tag):
            pe.wait_ge(*when("ssq", tag))
            ptile(lambda k: m.mean1[:, :], lambda k: m.ssq, kts=1)

        def free_banks():
            for n in (n_tile[0] - 2, n_tile[0] - 1):
                if n >= 0:
                    pe.wait_ge(*when("set_free", n))

        norm_sums((0, 0))
        modulation(0, ADA_FIRST)
        dense_tiles(AT_IN, 1, m.hT, norm_steps(0, 0))
        for j in range(N_PAIR):
            rk, vv = at_pair(j), at_pair(j) + 1
            batches = ada_batches(j)
            pe.wait_ge(*when("weights_in", rk))
            ptile(lambda k: m.wblock(rk, P)[:, k, :], lambda k: m.hT[:, k, :])
            ptile(lambda k: m.wblock(rk, P, 1024)[:, k, :], lambda k: m.hT[:, k, :], used=rk)
            pe.wait_ge(*when("weights_in", vv))
            ptile(lambda k: m.wblock(vv, P)[:, k, :], lambda k: m.hT[:, k, :], used=vv)
            js = slice(j * P, j * P + P)
            pe.wait_ge(*when("lora_ready"))
            ptile(lambda k: m.lorw[0:64, 0, js], lambda k: m.lora[0:64, :], kts=1)
            ptile(lambda k: m.lorw[64:128, 0, js], lambda k: m.lora[64:128, :], kts=1)
            pe.wait_ge(*when("sg_ready"))
            ptile(lambda k: m.lorw[:, 1, js], lambda k: m.sgd, kts=1)
            modulation(*next(batches))
            pe.wait_ge(*when("kk_sq", j))
            ptile(lambda k: m.bd1[:, :], lambda k: m.T1, kts=1)
            modulation(*next(batches))
            pe.wait_ge(*when("rk_prod", j))
            ptile(lambda k: m.bd1[:, :], lambda k: m.T1, kts=1)
            last_mod = next(batches)
            modulation(*last_mod)
            pe.wait_ge(*when("mod_biased", last_mod[1] - 1))
            pe.wait_ge(*when("s0_in", j))
            for b in range(NB):
                last = tr(banks[:, 6 + b // 4, (b % 4) * P:(b % 4) * P + P], m.S0in[:, b, :])
            last.then_inc(*sig("pe", ("s0_turned", j)))
            pe.wait_ge(*when("s0_copied", j))
            free_banks()
            for k, stage in tile_stages():
                tensor_rwkv_stage(pe, led, m, mm, tr, j, k, stage)
            tensor_rwkv_sample(pe, led, m, mm, tr, j)
            pe.wait_ge(*when("states_final", j))
            for i in range(9):
                last = tr(banks[:, i // 4, (i % 4) * P:(i % 4) * P + P], m.SBD[:, i, :])
            last.then_inc(*sig("pe", ("sfin_turned", j)))
            pe.wait_ge(*when("sout_ready", j))
            pe.wait_ge(*when("o_ready", j))
            ptile(lambda k: m.bd1[:, :], lambda k: m.QO, kts=1)
            pe.wait_ge(*when("gn_sq", j))
            ptile(lambda k: m.bd1[:, :], lambda k: m.T1, kts=1)

        free_banks()
        for k in range(ZT):
            last = tr(banks[0:9, k // 4, (k % 4) * P:(k % 4) * P + P], m.lastz[:, k, :])
        last.then_inc(*sig("pe", ("shift_turned",)))
        pe.wait_ge(*when("usa_zero"))
        pe.wait_ge(*when("shout_ready"))
        for half in range(2):
            n = AT_U + half
            pe.wait_ge(*when("weights_in", n))
            for q in range(12):
                i = half * 12 + q
                if i >= 4:
                    pe.wait_ge(*when("u_copied", i - 4))
                if q < 8:
                    out, cols = banks[:, i % 4, 0:256], slice(q, TP, L8)
                else:
                    out, cols = banks[0:NB, i % 4, 0:256], slice(TP + q - 8, T, TS)
                for k in range(KT):
                    last = mm(out, m.hT[:, k, cols], m.wblock(n)[:, k, :], k == 0, k == KT - 1)
                last.then_inc(*sig("pe", ("u_done", i), *([("weights_used", n)] if q == 11 else [])))
                if i == 5:
                    pe.wait_ge(*when("s5_in"))
                    pe.wait_ge(*when("d_rows"))
                    for r in range(3):
                        last = tr(banks[:, 6, r * 32:r * 32 + 32], m.s5rows[0:32, r, :])
                    last.then_inc(*sig("pe", ("s5_turned",)))
                if 8 <= i < 20:
                    k = i - 8
                    pe.wait_ge(*when("crow_in", k))
                    if k >= 2:
                        pe.wait_ge(*when("crow_copied", k - 2))
                    tr(banks[:, 4 + k % 2, 0:P], m.rows2[:, k % 2, :]).then_inc(*sig("pe", ("crow_turned", k)))

        for q in range(4):
            tensor_s5_quarter(pe, led, m, mm, tr, q)
        pe.wait_ge(*when("s5_states"))
        for i in range(2):
            tr(banks[:, 7, i * P:i * P + P], m.h4[:, 4 * i:4 * i + 4, :].rearrange("p b g -> p (b g)"))
        tr(banks[0:32, 7, 256:384], m.hfin).then_inc(*sig("pe", ("s5_states_turned",)))
        for part in range(3):
            pe.wait_ge(*when("y_copied", 3, part))
        pe.wait_ge(*when("weights_in", AT_GLU))
        for ft in range(4):
            w = m.slot(AT_GLU).rearrange("p (k c) -> p k c", k=4)
            ptile(lambda k: w[:, k, ft * P:ft * P + P], lambda k: m.yT[:, k, :], kts=4,
                  used=AT_GLU if ft == 3 else None)

        def out_and_mlp(layer, mixer_steps):
            dense_tiles(AT_OUT[layer], 4, m.mT, mixer_steps)
            norm_sums((layer, 1))
            for q in range(4):
                dense_tiles(AT_MLP[layer] + 8 * q, 4, m.hT, norm_steps(layer, 1) if q == 0 else None)
                pe.wait_ge(*when("hidden", layer, q))
                dense_tiles(AT_MLP[layer] + 8 * q + 4, 4, m.mT)

        out_and_mlp(0, [("mix_ready", k) for k in range(4)] + [("glu_used", k) for k in range(4)])

        norm_sums((1, 0))
        dense_tiles(AT_QKV, 8, m.hT, norm_steps(1, 0))
        for n in range(AT_QKV + 8, AT_QKV + 12):
            pe.wait_ge(*when("weights_in", n))
            for i, (t0, cnt) in enumerate(TILES):
                e = (n - AT_QKV - 8) * 9 + i
                if e >= 2:
                    pe.wait_ge(*when("v_copied", e - 2))
                for k in range(KT):
                    last = mm(banks[0:cnt, 6 + e % 2, 0:256], m.hT[:, k, t0:t0 + cnt], m.wblock(n)[:, k, :],
                              k == 0, k == KT - 1)
                last.then_inc(*sig("pe", ("v_done", e), *([("weights_used", n)] if i == 8 else [])))
        free_banks()
        for i, (t0, cnt) in enumerate(TILES):
            for half in range(2):
                if i:
                    pe.wait_ge(*when("k_copied", i - 1, half))
                for qq in range(4):
                    last = tr(banks[0:cnt, half, qq * P:qq * P + P], m.kT[:, half * 4 + qq, t0:t0 + cnt])
                last.then_inc(*sig("pe", ("k_turned", i, half)))
        for half in range(2):
            pe.wait_ge(*when("k_copied", 8, half))
        for e in (34, 35):
            pe.wait_ge(*when("v_copied", e))
        steps = [(h, i) for h in range(H_C) for i in range(8)]

        for s in range(len(steps) + 2):
            for c in range(2):
                if s < len(steps):
                    h, i = steps[s]
                    cs = slice(64 * c, 64 * c + 64)
                    if s:
                        pe.wait_ge(*when("scores_free", s - 1, c))
                    for k0 in range(0, (i + 1) * P, 512):
                        k1 = min(k0 + 512, (i + 1) * P)
                        last = mm(banks[:, 2 * c + k0 // 512, 0:k1 - k0], m.qT[cs, h, i * P:i * P + P], m.kT[cs, h, k0:k1])
                    last.then_inc(*sig("pe", ("scores", s, c)))
                if s < 2:
                    continue
                h, i = steps[s - 2]
                if c == 0:
                    pe.wait_ge(*when("probs", s - 2))
                    if s >= 3:
                        pe.wait_ge(*when("pt_copied", s - 3))
                    for kb in range(i + 1):
                        last = tr(banks[:, 4 + kb // 4, (kb % 4) * P:(kb % 4) * P + P],
                                  m.Pp[:, (s - 2) % 3, 0, kb * P:kb * P + P])
                    last.then_inc(*sig("pe", ("pt_turned", s - 2)))
                else:
                    pe.wait_ge(*when("pt_copied", s - 2))
                    if s >= 4:
                        pe.wait_ge(*when("o_copied", s - 4))
                    for kb in range(i + 1):
                        last = mm(banks[:, 6 + s % 2, 0:P], m.V[:, kb, h * P:h * P + P], m.PTp[:, kb, :], kb == 0, kb == i)
                    last.then_inc(*sig("pe", ("o_done", s - 2)))
        tensor_sample_attention(pe, led, m, mm, tr)
        pe.wait_ge(*when("oT_done"))
        for h in range(H_C):
            pe.wait_ge(*when("o_sq", h))
            ptile(lambda k: m.mean1[:, :], lambda k: m.sq2[:, h % 2, :], kts=1)
        out_and_mlp(1, [("o_normed", h) for h in range(H_C)])
        norm_sums((2, 0))
        for i, (t0, cnt) in enumerate(TILES):
            for half in range(2):
                if i:
                    pe.wait_ge(*when("y_row_copied", i - 1, half))
                for q in range(4):
                    if i == 0:
                        pe.wait_ge(*when("h_ready", 2, 0, half * 4 + q))
                    last = tr(banks[0:cnt, 6 + half, q * P:q * P + P], m.hT[:, half * 4 + q, t0:t0 + cnt])
                last.then_inc(*sig("pe", ("y_row_turned", i, half)))


def tensor_rwkv_stage(pe, led, m, mm, tr, j, k, stage):
    sig, when = led.sig, led.when
    banks, p, t0 = m.banks, k % 2, k * P
    a, b, c, d = range(4 * p, 4 * p + 4)
    FF, FT, PW, TM, XY, KR = m.FF, m.FT, m.PW, m.TM, m.XY, m.KR
    A_KK, A_RK, D_T, A_RB = range(4)
    us = (2 * p, 2 * p + 1)

    def cell(bank, i, cols=P):
        return banks[:, bank, i * P:i * P + cols]

    if stage == S_TM:
        if k >= 2:
            pe.wait_ge(*when("rw_free", j, k - 2))
        for i, src in enumerate((m.KH, m.BH, m.Vf, KR[:, 0, :])):
            last = tr(cell(a, i), src[:, t0:t0 + P])
        last.then_inc(*sig("pe", ("tm_turned", j, k)))
        for h, full in enumerate((b, c)):
            hs = slice(64 * h, 64 * h + 64)
            both = KR[hs, :, t0:t0 + P]
            mm(banks[:, full, 0:256].rearrange("p (i t) -> p i t", i=2), m.Kf[hs, t0:t0 + P], both)
            mm(banks[:, full, 256:512].rearrange("p (i t) -> p i t", i=2), m.Af[hs, t0:t0 + P], both)
        mm(cell(d, 0), KR[64:128, 0, t0:t0 + P], m.Af[64:128, t0:t0 + P])
        pe.wait_ge(*when("tm_ready", j, k))
        last = mm(cell(a, 0), KR[0:64, 0, t0:t0 + P], m.Af[0:64, t0:t0 + P])
        last.then_inc(*sig("pe", ("grams", j, k)))
    elif stage == S_D2:
        pe.wait_ge(*when("gram_masked", j, k))
        for h in range(2):
            mm(cell(b, h), m.G4[:, p, h, D_T, :], m.G3[:, p, h, 0, :])
            last = mm(cell(c, h), m.G3[:, p, h, 0, :], m.G4[:, p, h, D_T, :])
        last.then_inc(*sig("pe", ("d2", j, k)))
    elif stage == S_D4:
        pe.wait_ge(*when("d2_copied", j, k))
        pe.wait_ge(*when("d2_copied_t", j, k))
        for h, u in enumerate(us):
            mm(cell(d, h), PW[:, 0, u, :], FF[:, u, :])
            mm(cell(a, h), PW[:, 1, u, :], PW[:, 0, u, :])
            last = mm(cell(c, h), PW[:, 0, u, :], PW[:, 1, u, :])
        last.then_inc(*sig("pe", ("d4", j, k)))
    elif stage == S_D8:
        pe.wait_ge(*when("d4_copied", j, k))
        pe.wait_ge(*when("d4_copied_t", j, k))
        for h, u in enumerate(us):
            mm(cell(d, h), PW[:, 0, u, :], FF[:, u, :])
            last = mm(cell(a, h), PW[:, 1, u, :], PW[:, 0, u, :])
        last.then_inc(*sig("pe", ("d8", j, k)))
    elif stage == S_F:
        pe.wait_ge(*when("d8_added", j, k))
        pe.wait_ge(*when("d8_copied", j, k))
        for h, u in enumerate(us):
            mm(cell(d, h), PW[:, 0, u, :], FF[:, u, :])
            last = mm(banks[:, a, h * C64:h * C64 + C64], m.G4[:, p, h, A_KK, :], TM[:, p, 2, h * C64:h * C64 + C64])
        last.then_inc(*sig("pe", ("f4p", j, k)))
    elif stage in (S_L1, S_M1):
        lv = int(stage == S_M1)
        pe.wait_ge(*when("f_level", j, k, lv))
        for h, u in enumerate(us):
            tr(cell(b, h), FF[:, u, :])
            last = mm(cell(c, h), m.G3[:, p, h, 1 + lv, :], FF[:, u, :])
        last.then_inc(*sig("pe", ("level_p1", j, k, lv)))
    elif stage in (S_L2, S_M2):
        lv = int(stage == S_M2)
        pe.wait_ge(*when("level_copied", j, k, lv))
        pe.wait_ge(*when("level_copied_t", j, k, lv))
        for h, u in enumerate(us):
            last = mm(cell(d, h), FT[:, u, :], PW[:, 0, u, :])
        last.then_inc(*sig("pe", ("level_p2", j, k, lv)))
    elif stage == S_XY:
        pe.wait_ge(*when("f_level", j, k, 2))
        pe.wait_ge(*when("rhs_ready", j, k))
        for h, u in enumerate(us):
            last = mm(cell(b, h), FF[:, u, :], m.RHS[:, p, h, :, :])
        last.then_inc(*sig("pe", ("xy", j, k)))
    elif stage == S_ZQ:
        pe.wait_ge(*when("xy_copied", j, k))
        zz, qq = (banks[:, bank, 0:256].rearrange("p (h t) -> p h t", h=2) for bank in (c, d))
        mm(zz, XY[:, p, 0, :, :], m.G4[:, p, :, A_RB, :])
        mm(qq, TM[:, p, 2, :], m.G4[:, p, :, A_RK, :], True, False)
        mm(qq, XY[:, p, 1, :, :], m.G4[:, p, :, A_RB, :], False, True)
        for ch, bank in enumerate((a, b)):
            cs = slice(64 * ch, 64 * ch + 64)
            last = mm(cell(bank, 0), XY[cs, p, 0, :, :], TM[cs, p, 1, :])
        last.then_inc(*sig("pe", ("zq", j, k)))
    else:
        ch = stage - S_C0
        q = 2 * k + ch
        cs = slice(64 * ch, 64 * ch + 64)
        if ch == 0:
            pe.wait_ge(*when("tt_ready", j, k))
            pe.wait_ge(*when("q_copied", j, k))
        if q:
            pe.wait_ge(*when("state", j, q))
        mm(banks[:, (a, b)[ch], 0:C64], m.SBD[:, 0, :], m.ZTt[:, p, 64 * ch:64 * ch + 64])
        mm(cell(c, ch), m.TT[:, us[ch], :], m.SBD[:, 0, :], True, False)
        mm(cell(c, ch), TM[cs, p, 0, :], TM[cs, p, 2, :], False, False)
        last = mm(cell(c, ch), TM[cs, p, 1, :], XY[cs, p, 1, :, :], False, True)
        last.then_inc(*sig("pe", ("state_new", j, q)))


def tensor_rwkv_sample(pe, led, m, mm, tr, j):
    sig, when = led.sig, led.when
    banks, n, t0 = m.banks, NS, TP
    FF, PW, TM, XY, KR = m.FF, m.PW, m.TM, m.XY, m.KR
    SBD, TT, ZTt = m.SBD, m.TT, m.ZTt
    A_KK, A_RK, D_T, A_RB = range(4)

    def cell(bank, i, rows=n, cols=n):
        return banks[0:rows, bank, i * P:i * P + cols]

    pe.wait_ge(*when("rw_free", j, N_TILE - 2))
    pe.wait_ge(*when("rw_free", j, N_TILE - 1))
    for i, src in enumerate((m.KH, m.BH, m.Vf, KR[:, 0, :])):
        last = tr(cell(0, i, n, P), src[:, t0:t0 + n])
    last.then_inc(*sig("pe", ("tm_turned", j, N_TILE)))
    for h in range(2):
        hs = slice(64 * h, 64 * h + 64)
        both = KR[hs, :, t0:t0 + n]
        full = banks[0:n, 2 + h, :].rearrange("p (g i t) -> p g i t", g=2, i=2)
        mm(full[:, 0, :, 0:n], m.Kf[hs, t0:t0 + n], both)
        mm(full[:, 1, :, 0:n], m.Af[hs, t0:t0 + n], both)
        last = mm(cell(6 + h, 0), KR[hs, 0, t0:t0 + n], m.Af[hs, t0:t0 + n])
    last.then_inc(*sig("pe", ("grams", j, N_TILE)))
    pe.wait_ge(*when("tm_ready", j, N_TILE))
    pe.wait_ge(*when("gram_masked", j, N_TILE))
    for h in range(2):
        last = mm(cell(0, h), m.G4[0:n, 0, h, D_T, 0:n], m.G3[0:n, 0, h, 0, 0:n])
    for h in range(2):
        last = mm(banks[0:n, 4, h * C64:h * C64 + C64], m.G4[0:n, 0, h, A_KK, 0:n], TM[0:n, 0, 2, h * C64:h * C64 + C64])
    last.then_inc(*sig("pe", ("d2", j, N_TILE)))
    pe.wait_ge(*when("d2_copied", j, N_TILE))
    for h in range(2):
        last = mm(cell(7, h), PW[0:n, 0, h, 0:n], FF[0:n, h, 0:n])
    last.then_inc(*sig("pe", ("d4", j, N_TILE)))
    pe.wait_ge(*when("f_level", j, N_TILE, 2))
    pe.wait_ge(*when("rhs_ready", j, N_TILE))
    for h in range(2):
        last = mm(cell(5, h, n, P), FF[0:n, h, 0:n], m.RHS[0:n, 0, h, :, :])
    last.then_inc(*sig("pe", ("xy", j, N_TILE)))
    pe.wait_ge(*when("xy_copied", j, N_TILE))
    zz, qq = (banks[:, bank, 0:256].rearrange("p (h t) -> p h t", h=2)[:, :, 0:n] for bank in (0, 2))
    mm(zz, XY[0:n, 0, 0, :, :], m.G4[0:n, 0, :, A_RB, 0:n])
    mm(qq, TM[0:n, 0, 2, :], m.G4[0:n, 0, :, A_RK, 0:n], True, False)
    mm(qq, XY[0:n, 0, 1, :, :], m.G4[0:n, 0, :, A_RB, 0:n], False, True).then_inc(*sig("pe", ("zq", j, N_TILE)))
    pe.wait_ge(*when("zq_copied", j))
    for b in range(NB):
        last = mm(banks[:, 0, b * TS:b * TS + TS], SBD[:, 1 + b, :], ZTt[:, 0, TS * b:TS * b + TS])
    last.then_inc(*sig("pe", ("o_sample", j)))
    for half in range(2):
        pe.wait_ge(*when("mb_ready", j, half))
        for q in range(4):
            last = mm(cell(6 + half, q, P, P), XY[0:NS, 0, 0, :, :], m.MB[0:NS, q, 1, :])
        last.then_inc(*sig("pe", ("tts", j, half)))
        pe.wait_ge(*when("tts_ready", j, half))
        for q in range(4):
            out = cell(4 + half, q, P, P)
            mm(out, TT[:, q, :], SBD[:, 1 + half * 4 + q, :], True, False)
            mm(out, m.MB[0:NS, q, 0, :], TM[0:NS, 0, 2, :], False, False)
            last = mm(out, m.MB[0:NS, q, 1, :], XY[0:NS, 0, 1, :, :], False, True)
        last.then_inc(*sig("pe", ("states_new", j, half)))


def tensor_s5_quarter(pe, led, m, mm, tr, q):
    sig, when = led.sig, led.when
    banks = m.banks
    pe.wait_ge(*when("u_copied", 23))
    if q:
        for part in range(3):
            pe.wait_ge(*when("y_copied", q - 1, part))
    for gg in range(8):
        g, c0 = 8 * q + gg, (gg % 2) * 256
        tr(banks[:, gg // 2, c0:c0 + P], m.U[:, g, :, :].rearrange("p j n -> p (j n)"))
        tr(banks[:, gg // 2, c0 + 128:c0 + 136], m.UsA[:, g, 4:12, :].rearrange("p j n -> p (j n)"))
        last = tr(banks[:, gg // 2, c0 + 136:c0 + 144], m.UsA[:, g, 0:8, :].rearrange("p j n -> p (j n)"))
    last.then_inc(*sig("pe", ("ut_turned", q)))
    pe.wait_ge(*when("powers", q))
    for gg in range(8):
        for j in range(L8):
            last = mm(banks[:, 4 + gg // 4, (gg % 4) * P:(gg % 4) * P + P],
                      m.BBp[:, gg, 7 - j:15 - j, :].rearrange("p j n -> p (j n)"),
                      m.CAp[:, gg, 7 - j:15 - j, :].rearrange("p j n -> p (j n)"), j == 0, j == L8 - 1)
    for gg in range(8):
        last = tr(banks[:, 6 + gg // 4, (gg % 4) * P:(gg % 4) * P + P], m.ABx[:, gg, :, :].rearrange("p j n -> p (j n)"))
    last.then_inc(*sig("pe", ("toeplitz", q)))
    pe.wait_ge(*when("etx_copied", q))
    for gg in range(8):
        last = tr(banks[:, 6 + gg // 4, (gg % 4) * P:(gg % 4) * P + P], m.ABy[:, gg, :, :].rearrange("p j n -> p (j n)"))
    last.then_inc(*sig("pe", ("ety_turned", q)))
    pe.wait_ge(*when("ety_copied", q))
    pe.wait_ge(*when("ut_copied", q))
    for gg in range(8):
        c0 = (gg % 2) * 256
        mm(banks[:, gg // 2, c0:c0 + 144], m.ETx[:, gg, :], m.UT[:, gg, :])
        last = mm(banks[:, 4 + gg // 2, c0:c0 + 144], m.ETy[:, gg, :], m.UT[:, gg, :])
    last.then_inc(*sig("pe", ("left", q)))
    pe.wait_ge(*when("h_states", q))
    for gg in range(8):
        g = 8 * q + gg
        out = banks[:, gg // 4, (gg % 4) * P:(gg % 4) * P + P]
        outs = banks[0:NB, 2 + gg // 4, (gg % 4) * P:(gg % 4) * P + P]
        carry = m.CAp[:, gg, 8:16, :].rearrange("p j n -> p (j n)")
        mm(out, m.UT[:, gg, 0:P], m.Tm[:, gg, :], True, False)
        mm(out, m.Hs[:, gg, 0:P], carry, False, True)
        mm(outs, m.UT[:, gg, P:P + NB], m.Tm[:, gg, :], True, False)
        last = mm(outs, m.h0[:, 0, :, g], carry, False, True)
    last.then_inc(*sig("pe", ("y_done", q)))
    pe.wait_ge(*when("gelu_done", q))
    for part in range(3):
        for jj in range(4):
            c0 = jj * P
            if part < 2:
                last = tr(banks[:, 4 + part, c0:c0 + P], m.Yq[:, 4 * part + jj, :])
            else:
                last = tr(banks[:, 6, c0:c0 + NB], m.Yqs[:, jj, :])
    last.then_inc(*sig("pe", ("y_turned", q)))


def tensor_sample_attention(pe, led, m, mm, tr):
    sig, when = led.sig, led.when
    banks = m.banks
    pe.wait_ge(*when("o_copied", 63))
    pe.wait_ge(*when("o_copied", 62))

    def turn_page(b, p):
        n = b * 2 * N_PAGES + p
        e = b * N_PAGES + p
        pe.wait_ge(*when("page_in", n))
        for half in range(2):
            if e:
                pe.wait_ge(*when("page_copied", e - 1, half))
            for q in range(4):
                h = half * 4 + q
                last = tr(banks[:, 4 + half, q * P:q * P + P], m.page(n)[:, h * P:h * P + P])
            last.then_inc(*sig("pe", ("page_turned", e, half), *([("page_used", n)] if half else [])))

    def turn_outputs(b):
        pe.wait_ge(*when("os_copied", b))
        for h in range(H_C):
            last = tr(banks[:, 7, h * NS:h * NS + NS], m.Os[:, h * P:h * P + P])
        last.then_inc(*sig("pe", ("os_turned", b)))

    for b in range(NB):
        pe.wait_ge(*when("qpad", b))
        turn_page(b, 0)
        if b:
            pe.wait_ge(*when("os_copied", b - 1))
        qp = m.qpad[:, b % 2, :].rearrange("p (h s) -> p h s", s=72)

        def qh(h):
            return m.qpad[:, b % 2, h * 64:h * 64 + 64]
        for h in range(H_C):
            last = mm(banks[0:64, 6, 0:NS], qh(h), m.kTs[:, h, :], h == 0, h == H_C - 1)
        last.then_inc(*sig("pe", ("s_new", b)))
        for p in range(N_PAGES):
            if p + 1 < N_PAGES:
                turn_page(b, p + 1)
            e = b * N_PAGES + p
            for h in range(H_C):
                if h % 4 == 0:
                    pe.wait_ge(*when("page_copied", e, h // 4))
                last = mm(banks[0:64, p // 4, (p % 4) * P:(p % 4) * P + P], qh(h), m.KTp[:, p % 2, h, :],
                          h == 0, h == H_C - 1)
            last.then_inc(*sig("pe", ("page_scored", e)))
            if b and p == 0:
                turn_outputs(b - 1)
        pe.wait_ge(*when("s_coef", b))
        pe.wait_ge(*when("s_exp", b))
        pe.wait_ge(*when("page_copied", b * N_PAGES + 15, 0))
        pe.wait_ge(*when("page_copied", b * N_PAGES + 15, 1))
        for p in range(N_PAGES):
            mm(banks[:, 4, p * NS:p * NS + NS], m.Ps[:, p * P:p * P + P], m.Cm)
        mm(banks[0:NS, 5, 0:NS], m.Ps[:, 2048:2048 + NS], m.Cm).then_inc(*sig("pe", ("pts_done", b)))
        pe.wait_ge(*when("pts_copied", b))
        if b:
            pe.wait_ge(*when("os_done", b - 1))
        for p in range(N_PAGES + 1):
            n = (b * 2 + 1) * N_PAGES + p
            if p < N_PAGES:
                pe.wait_ge(*when("page_in", n))
            for half in range(2):
                hs = slice(half * 512, half * 512 + 512)
                if p < N_PAGES:
                    last = mm(banks[0:NS, 6 + half, :], m.PTs[:, p, :], m.page(n)[:, hs], p == 0, False)
                else:
                    last = mm(banks[0:NS, 6 + half, :], m.PTs[0:NS, p, :], m.V[0:NS, 8, hs], False, True)
            if p < N_PAGES:
                last.then_inc(*sig("pe", ("page_used", n), *([("pages_done",)] if (b, p) == (NB - 1, N_PAGES - 1) else [])))
            else:
                last.then_inc(*sig("pe", ("os_ready", b)))
    turn_outputs(NB - 1)


def vector_program(nc, block, led, m):
    sig, when = led.sig, led.when
    banks, v = m.banks, nc.vector
    vec, mask = m.vec, m.mask

    @block.vector
    def _(ve):
        def do(ins, *steps):
            steps = steps or (("step",),)
            ins.then_inc(*sig("vector", *steps))
            ve.wait_ge(*led.own("vector", steps[0]))

        def tt(out, x, y, op, *steps):
            do(v.tensor_tensor(out, x, y, op), *steps)

        def ts(out, x, s1, o1, s2=None, o2=None, steps=()):
            do(v.tensor_scalar(out, x, s1, None, o1) if o2 is None else v.tensor_scalar(out, x, s1, s2, o1, o2), *steps)

        def stt(out, x, s, y, o1, o2, *steps):
            do(v.scalar_tensor_tensor(out=out, in0=x, scalar=s, in1=y, op0=o1, op1=o2), *steps)

        def cp(out, x, *steps):
            do(v.tensor_copy(out, x), *steps)

        def red(out, x, op, *steps):
            do(v.tensor_reduce(out, x, AX.X, op), *steps)

        n_tile = [0]

        def next_set():
            n = n_tile[0]
            n_tile[0] += 1
            return n, 3 * (n % 2)

        V_ = dict(ve=ve, do=do, tt=tt, ts=ts, stt=stt, cp=cp, red=red)
        ident = m.ident

        ve.wait_ge(*when("masks"))
        tt(m.msk[:, L64, :], m.msk[:, L64, :], m.msk[:, L32, :], ALU.subtract)
        tt(m.msk[:, L32, :], m.msk[:, L32, :], m.msk[:, L16, :], ALU.subtract)
        ts(m.msk[:, NUI64, :], m.msk[:, UI64, :], -1.0, ALU.mult)
        ts(m.msk4[:, NUI4, :], m.msk4[:, UI4, :], -1.0, ALU.mult, steps=[("consts",)])
        ve.wait_ge(*when("cond_sig"))
        tt(m.crows, m.crows, m.csig, ALU.mult, ("silu",))
        ve.wait_ge(*when("vecs_turned"))
        cp(m.vecT[:, 0:N_VEC], banks[:, 0, 0:N_VEC])
        cp(m.bT[:, :], banks[:, 0, 128:224])
        cp(m.shiftT[:, :, :], banks[:, 2, 0:ZT * NB].rearrange("p (k b) -> p k b", b=NB))
        ve.wait_ge(*when("cond_turned"))
        cp(m.condT[:, :, :], banks[:, 1, 0:72].rearrange("p (k b) -> p k b", b=9), ("condT",))
        ve.wait_ge(*when("params_in"))
        for i in range(2):
            q, k = m.lrows[:, 128 * i:128 * i + 64], m.lrows[:, 128 * i + 64:128 * i + 128]
            tt(q, q, k, ALU.mult)
            red(m.lam[0:1, i:i + 1], q, ALU.add, *([("lam_dots",)] if i else []))
        def add_squares(tag, k):
            ve.wait_ge(*when("squares", tag, k))
            tt(m.ssq, m.ssq, m.sq[:, k % 2, :], ALU.add, ("sq_added", tag, k), *([("ssq", tag)] if k == KT - 1 else []))

        for k in range(1, KT):
            add_squares((0, 0), k)
        ve.wait_ge(*when("mod_sums", 0))
        cp(m.lam[:, 4:6], banks[:, 4, 0:2])
        tt(m.lam[:, 6:7], m.lam[:, 4:5], m.lam[:, 5:6], ALU.subtract)
        ts(m.lam[:, 6:7], m.lam[:, 6:7], -float(D), ALU.mult, -LAM0, ALU.add)
        def gains(layer, w):
            sc, r = (SC_M, SC_F)[w], VEC[("norm_mix", "norm_mlp")[w]][0] + 8 * layer
            g = m.gain[:, layer, w, :, :]
            ts(g, m.modT[:, layer, sc:sc + 8, :], 1.0, ALU.add)
            tt(g, g, rep(m.vecT[:, r:r + 8], 9), ALU.mult)

        ve.wait_ge(*when("mod_biased", ADA_FIRST - 1))
        gains(0, 0)

        def norm(layer, w):
            next_set()
            ve.wait_ge(*when("std", (layer, w)))
            do(v.reciprocal(m.rstd, m.rstd))
            for k in range(KT):
                h, x = m.hT[:, k, :], m.xT[:, k, :]
                last = [("h_ready", layer, w, k)] + ([("h_ready", layer, w)] if k == KT - 1 else [])
                if layer == 2:
                    stt(h, x, vec("norm_f", k), m.rstd, ALU.mult, ALU.mult, *last)
                    continue
                G, sh = m.gain[:, layer, w, k, :], m.modT[:, layer, (SH_M, SH_F)[w] + k, :]
                stt(h[:, 0:TP], x[:, 0:TP], G[:, 0:1], m.rstd[:, 0:TP], ALU.mult, ALU.mult)
                ts(h[:, 0:TP], h[:, 0:TP], sh[:, 0:1], ALU.add)
                tt(smp(h), smp(x), smp(m.rstd), ALU.mult)
                tt(smp(h), smp(h), rep(G[:, 1:9], TS), ALU.mult)
                tt(smp(h), smp(h), rep(sh[:, 1:9], TS), ALU.add, *last)

        norm(0, 0)
        ve.wait_ge(*when("spilled", 0))
        do(v.memset(m.rowm, 1.0))
        do(v.memset(m.rowm[:, 0:TP:C64], 0.0))
        do(v.memset(m.rowm[:, TP:T:TS], 0.0))
        red(m.eb, ident[:, 0:NS].rearrange("p (b q) -> p b q", q=TS), ALU.add)

        def shifted(dst, zi, n):
            mu = vec("rwkv_mu", zi)
            z, zp = m.zb[:, 1:1 + TP], m.zb[:, 0:TP]
            s = m.zb[:, 1025:1065].rearrange("p (b q) -> p b q", q=5)
            ve.wait_ge(*when("zb_ready", n))
            tt(dst[:, 0:TP], zp, z, ALU.subtract)
            stt(dst[:, 0:TP], dst[:, 0:TP], mu, z, ALU.mult, ALU.add)
            tt(smp(dst), s[:, :, 0:4], s[:, :, 1:5], ALU.subtract)
            stt(smp(dst), smp(dst), mu, s[:, :, 1:5], ALU.mult, ALU.add, ("zb_used", n))

        shifted(m.lora, 12, next_set()[0])
        shifted(m.sgd, 13, next_set()[0])
        for j in range(N_PAIR):
            KR, Kf, Vf, Af, T1, KH, BH, LW, Lc, QO, WC = (m.KR, m.Kf, m.Vf, m.Af, m.T1, m.KH, m.BH, m.LW, m.Lc,
                                                          m.QO, m.WC)
            for zi, dst in ((0, KR[:, 1, :]), (4, Kf), (8, Vf)):
                shifted(dst, zi + j, next_set()[0])
            for _ in range(3):
                next_set()
            ve.wait_ge(*when("lw_sig", j))
            ts(LW, LW, -DECAY, ALU.mult)
            KK = KR[:, 0, :]
            ts(KK, Kf, vec("rwkv_k_k", j), ALU.mult)
            tt(T1, KK, KK, ALU.mult, ("kk_sq", j))
            next_set()
            ve.wait_ge(*when("kk_norm", j))
            ts(T1, T1, 1e-12, ALU.max)
            do(v.reciprocal(T1, T1))
            tt(KK, KK, T1, ALU.mult)
            ve.wait_ge(*when("a_ready", j))
            ts(T1, Af, -1.0, ALU.add, vec("rwkv_k_a", j), ALU.mult)
            stt(Kf, T1, 1.0, Kf, ALU.add, ALU.mult)
            stt(T1, KR[:, 1, :], vec("rwkv_r_k", j), Kf, ALU.mult, ALU.mult, ("rk_prod", j))
            n, s = next_set()
            ve.wait_ge(*when("set_done", n))
            for c, (t0, t1) in enumerate(CHUNKS):
                tt(m.BON[:, t0:t1], banks[:, s + c, 0:CH], Vf[:, t0:t1], ALU.mult, *([("set_free", n)] if c == 2 else []))
            do(v.tensor_tensor_scan(Lc, m.rowm, LW, 0.0, ALU.mult, ALU.add))
            tt(T1, Lc, LW, ALU.subtract, ("lx", j))
            tt(Af, KK, Af, ALU.mult)
            ve.wait_ge(*when("e_lx", j))
            tt(KK, KK, T1, ALU.mult)
            ve.wait_ge(*when("e_l", j))
            tt(KR[:, 1, :], KR[:, 1, :], KH, ALU.mult)
            cp(WC[:, 0:16], KH[:, 63:TP:C64])
            cp(WC[:, 16:24], KH[:, TP + 3:T:TS])
            ve.wait_ge(*when("e_nl", j))
            tt(Kf, Kf, BH, ALU.mult)
            tt(Af, Af, BH, ALU.mult)

            def ch(ap):
                return ap[:, 0:TP].rearrange("p (c t) -> p c t", t=C64)
            wcp, wcs = rep(WC[:, 0:16], C64), rep(WC[:, 16:24], TS)
            tt(ch(KH), ch(Kf), wcp, ALU.mult)
            tt(smp(KH), smp(Kf), wcs, ALU.mult)
            tt(ch(BH), ch(Af), wcp, ALU.mult)
            tt(smp(BH), smp(Af), wcs, ALU.mult)
            ts(BH, BH, -1.0, ALU.mult)
            do(v.memset(m.SBD[:, 0, :], 0.0))
            ve.wait_ge(*when("s0_turned", j))
            for half in range(2):
                cp(m.SBD[:, 1 + 4 * half:5 + 4 * half, :], banks[:, 6 + half, :].rearrange("p (b k) -> p b k", b=4),
                   *([("s0_copied", j)] if half else []))
            for k, stage in tile_stages():
                vector_rwkv_stage(led, m, V_, j, k, stage)
            vector_rwkv_sample(led, m, V_, j)
            ve.wait_ge(*when("sfin_turned", j))
            if j:
                ve.wait_ge(*when("sout_out", j - 1))
            for i0, cnt, bank in ((0, 4, 0), (4, 4, 1), (8, 1, 2)):
                for hh in range(2):
                    hs = slice(64 * hh, 64 * hh + 64)
                    cp(m.SOUT[hs, i0:i0 + cnt, :],
                       banks[hs, bank, 0:cnt * P].rearrange("p (i k) -> p i k", k=P)[:, :, 64 * hh:64 * hh + 64],
                       *([("sout_ready", j)] if (i0, hh) == (8, 1) else []))
            n, s = next_set()
            ve.wait_ge(*when("set_done", n))
            for c, (t0, t1) in enumerate(CHUNKS):
                stt(QO[:, t0:t1], banks[:, s + c, 0:CH], -1.0 / C64, QO[:, t0:t1], ALU.mult, ALU.add,
                    *([("set_free", n)] if c == 2 else []))
            tt(T1, QO, QO, ALU.mult, ("gn_sq", j))
            next_set()
            ve.wait_ge(*when("gn_std", j))
            do(v.reciprocal(T1, T1))
            tt(QO, QO, T1, ALU.mult)
            ts(QO, QO, vec("rwkv_lnx_w", j), ALU.mult, vec("rwkv_lnx_b", j), ALU.add)
            tt(QO, QO, m.BON, ALU.add)
            ve.wait_ge(*when("g_ready", j))
            tt(m.mT[:, j, :], QO, m.Gf, ALU.mult, ("mix_ready", j))

        ve.wait_ge(*when("mod_biased", N_ADA - 1))
        gains(0, 1)
        gains(1, 0)
        gains(1, 1)
        vector_s5(nc, led, m, V_)
        for ft in range(4):
            n, s = next_set()
            ve.wait_ge(*when("glu_sig", ft))
            tt(m.mT[:, 4 + ft, :], m.yT[:, ft, :], m.sT, ALU.mult, ("glu_used", ft), *([("mixed", 0)] if ft == 3 else []))

        def residual(layer, gsec, tiles, final, tag=None):
            for k in range(tiles):
                n, s = next_set()
                ve.wait_ge(*when("set_done", n))
                gate, x = m.modT[:, layer, gsec + k, :], m.xT[:, k, :]
                tail = TP - 2 * CH
                ps = banks[:, s + 2, tail:CH].rearrange("p (b q) -> p b q", q=TS)
                for c in range(3):
                    t0, t1 = CHUNKS[c][0], min(CHUNKS[c][1], TP)
                    stt(x[:, t0:t1], banks[:, s + c, 0:t1 - t0], gate[:, 0:1], x[:, t0:t1], ALU.mult, ALU.add)
                tmp = m.rstd[:, 0:NS].rearrange("p (b q) -> p b q", q=TS)
                tt(tmp, ps, rep(gate[:, 1:9], TS), ALU.mult, ("set_free", n))
                tt(smp(x), smp(x), tmp, ALU.add, ("x_tile", tag if tag else final, k), *([final] if k == tiles - 1 else []))
                if tag and k >= 2:
                    add_squares(tag, k - 1)
            if tag:
                add_squares(tag, KT - 1)

        def out_and_mlp(layer):
            ve.wait_ge(*when("x_back", layer))
            residual(layer, G_M, 8, ("x_mid", layer), (layer, 1))
            norm(layer, 1)
            for q in range(4):
                for k in range(8):
                    n, s = next_set()
                    ve.wait_ge(*when("relu", n))
                    tt(m.mT[:, k, :], m.mT[:, k, :], m.mT[:, k, :], ALU.mult, *([("hidden", layer, q)] if k == 7 else []))
                residual(layer, G_F, 8, ("x_ready", layer + 1) if q == 3 else ("x_part", layer, q),
                         (layer + 1, 0) if q == 3 else None)

        out_and_mlp(0)

        norm(1, 0)
        for _ in range(16):
            next_set()
        for s in range(65):
            if s < 64:
                i = s % 8
                nk = (i + 1) * P
                st = m.st[:, s % 3, :]
                for c in range(2):
                    ve.wait_ge(*when("scores", s, c))
                    diag = banks[:, 2 * c + i // 4, (i % 4) * P:(i % 4) * P + P]
                    tt(diag, diag, mask(CAUSAL), ALU.add)
                    row = banks[:, 2 * c:2 * c + 2, :].rearrange("p b k -> p (b k)")[:, 0:nk]
                    do(v.tensor_reduce(st[:, 2 + c:3 + c], row, AX.X, ALU.max, negate=True), ("row_max", s, c))
            if s >= 1:
                nk = ((s - 1) % 8 + 1) * P
                P0, P1, st = m.Pp[:, (s - 1) % 3, 0, 0:nk], m.Pp[:, (s - 1) % 3, 1, 0:nk], m.st[:, (s - 1) % 3, :]
                ve.wait_ge(*when("scores_free", s - 1, 1))
                do(v.reciprocal(st[:, 6:8], st[:, 4:6]))
                tt(st[:, 8:9], st[:, 7:8], m.lam[:, 6:7], ALU.mult)
                ts(P0, P0, st[:, 6:7], ALU.mult)
                stt(P0, P1, st[:, 8:9], P0, ALU.mult, ALU.add, ("probs", s - 1))
        vector_sample_attention(nc, led, m, V_)
        ts(m.st[:, 0, 0:1], vec("diff_subln"), 1.0 - LAM0, ALU.mult)
        for h in range(H_C):
            next_set()
            ve.wait_ge(*when("o_std", h))
            do(v.reciprocal(m.r2[:, h % 2, :], m.r2[:, h % 2, :]))
            stt(m.oT[:, h, :], m.oT[:, h, :], m.st[:, 0, 0:1], m.r2[:, h % 2, :], ALU.mult, ALU.mult, ("o_normed", h))
        out_and_mlp(1)
        norm(2, 0)


def masked_grams(m, tt, stt, n, p, full, single, step):
    mk = m.msk if n == P else m.msk4
    F = m.FF[0:n, 2 * p:2 * p + 2, 0:n]
    src = full.rearrange("p h (i c) -> p h i c", c=P)[:, :, :, 0:n]
    tt(m.G4[0:n, p, :, :, 0:n], src, mk[0:n, 0:4, :].unsqueeze(1).to_broadcast([n, 2, 4, n]), ALU.mult)
    parts = 3 if n == P else 1
    tt(m.G3[0:n, p, :, 0:parts, 0:n], single[:, :, 0:n].unsqueeze(2).to_broadcast([n, 2, parts, n]),
       mk[0:n, 4:4 + parts, :].unsqueeze(1).to_broadcast([n, 2, parts, n]), ALU.mult)
    stt(F, m.G4[0:n, p, :, 2, 0:n], -1.0, mid(m.ident[0:n, 0:n], 2), ALU.mult, ALU.add, step)


def vector_rwkv_stage(led, m, V_, j, k, stage):
    ve, do, tt, ts, stt, cp = (V_[x] for x in ("ve", "do", "tt", "ts", "stt", "cp"))
    when, banks, p, t0 = led.when, m.banks, k % 2, k * P
    a, b, c, d = range(4 * p, 4 * p + 4)
    us = slice(2 * p, 2 * p + 2)
    F, PW = m.FF[:, us, :], m.PW

    def cells(bank):
        return banks[:, bank, 0:256].rearrange("p (u t) -> p u t", t=P)

    if stage == S_TM:
        ve.wait_ge(*when("grams", j, k))
        masked_grams(m, tt, stt, P, p, banks[:, b:c + 1, :], banks[:, a:d + 1:3, 0:P], ("gram_masked", j, k))
    elif stage == S_D2:
        ve.wait_ge(*when("d2", j, k))
        cp(PW[:, 0, us, :], cells(b), ("d2_copied", j, k))
    elif stage == S_D4:
        ve.wait_ge(*when("d4", j, k))
        tt(F, F, cells(d), ALU.add)
        cp(PW[:, 0, us, :], cells(a), ("d4_copied", j, k))
    elif stage == S_D8:
        ve.wait_ge(*when("d8", j, k))
        tt(F, F, cells(d), ALU.add, ("d8_added", j, k))
    elif stage == S_F:
        ve.wait_ge(*when("f4p", j, k))
        tt(F, F, cells(d), ALU.add, ("f_level", j, k, 0))
    elif stage in (S_L1, S_M1):
        lv = int(stage == S_M1)
        ve.wait_ge(*when("level_p1", j, k, lv))
        cp(PW[:, 0, us, :], cells(c), ("level_copied", j, k, lv))
    elif stage in (S_L2, S_M2):
        lv = int(stage == S_M2)
        ve.wait_ge(*when("level_p2", j, k, lv))
        tt(F, F, cells(d), ALU.subtract, ("f_level", j, k, lv + 1))
    elif stage == S_ZQ:
        ve.wait_ge(*when("zq", j, k))
        for h in range(2):
            hs = slice(64 * h, 64 * h + 64)
            tt(m.ZTt[hs, p, :], m.KR[hs, 1, t0:t0 + P], banks[hs, c, h * P:h * P + P], ALU.add)
        tt(m.TT[:, us, :], banks[:, a:b + 1, 0:P], mid(m.bd1[:, :], 2), ALU.mult)
        for ch in range(2):
            q = 2 * k + ch
            stt(m.TT[:, 2 * p + ch, :], m.ident[:, :], m.WC[:, q:q + 1], m.TT[:, 2 * p + ch, :], ALU.mult, ALU.add,
                *([("tt_ready", j, k)] if ch else []))
    elif stage in (S_C0, S_C1):
        ch = stage - S_C0
        q = 2 * k + ch
        ve.wait_ge(*when("state_new", j, q))
        tt(m.SBD[:, 0, :], banks[:, c, ch * P:ch * P + P], m.bd1[:, :], ALU.mult, ("state", j, q + 1))
        tt(m.QO[:, q * C64:q * C64 + C64], banks[:, (a, b)[ch], 0:C64], m.QTt[:, p, ch * C64:ch * C64 + C64],
           ALU.add, *([("rw_free", j, k)] if ch else []))


def vector_rwkv_sample(led, m, V_, j):
    ve, do, tt, ts, stt, cp = (V_[x] for x in ("ve", "do", "tt", "ts", "stt", "cp"))
    when, banks, n = led.when, m.banks, NS
    F, TT, SBD, QO, WC = m.FF[0:n, 0:2, 0:n], m.TT, m.SBD, m.QO, m.WC

    def cells(bank):
        return banks[0:n, bank, 0:256].rearrange("p (u t) -> p u t", t=P)[:, :, 0:n]

    ve.wait_ge(*when("grams", j, N_TILE))
    masked_grams(m, tt, stt, n, 0, banks[0:n, 2:4, :], banks[0:n, 6:8, 0:P], ("gram_masked", j, N_TILE))
    ve.wait_ge(*when("d2", j, N_TILE))
    cp(m.PW[0:n, 0, 0:2, 0:n], cells(0), ("d2_copied", j, N_TILE))
    cp(m.RHS[0:n, 0, :, 1, :], banks[0:n, 4, 0:2 * C64].rearrange("p (h v) -> p h v", h=2))
    cp(m.RHS[0:n, 0, :, 0, :], m.TM[0:n, 0, 3, :].rearrange("p (h v) -> p h v", h=2), ("rhs_ready", j, N_TILE))
    ve.wait_ge(*when("d4", j, N_TILE))
    tt(F, F, cells(7), ALU.add, ("f_level", j, N_TILE, 2))
    ve.wait_ge(*when("xy", j, N_TILE))
    cp(m.XY[0:n, 0, :, :, :], banks[0:n, 5, 0:256].rearrange("p (h i v) -> p i h v", h=2, i=2), ("xy_copied", j, N_TILE))
    ve.wait_ge(*when("zq", j, N_TILE))
    for h in range(2):
        hs = slice(64 * h, 64 * h + 64)
        tt(m.ZTt[hs, 0, 0:n], m.KR[hs, 1, TP:T], banks[hs, 0, h * P:h * P + n], ALU.add)
        cp(m.QTt[hs, 0, 0:n], banks[hs, 2, h * P:h * P + n], *([("zq_copied", j)] if h else []))
    ve.wait_ge(*when("o_sample", j))
    tt(QO[:, TP:T], banks[:, 0, 0:NS], m.QTt[:, 0, 0:NS], ALU.add, ("o_ready", j))
    for half in range(2):
        for q in range(4):
            b = half * 4 + q
            ts(m.MB[0:NS, q, :, :], m.TM[0:NS, 0, 0:2, :], m.eb[0:NS, b:b + 1], ALU.mult,
               steps=[("mb_ready", j, half)] if q == 3 else [])
        ve.wait_ge(*when("tts", j, half))
        tt(TT, banks[:, 6 + half, :].rearrange("p (u t) -> p u t", t=P), mid(m.bd1[:, :], 4), ALU.mult)
        for q in range(4):
            b = half * 4 + q
            stt(TT[:, q, :], m.ident[:, :], WC[:, 16 + b:17 + b], TT[:, q, :], ALU.mult, ALU.add,
                *([("tts_ready", j, half)] if q == 3 else []))
        ve.wait_ge(*when("states_new", j, half))
        tt(SBD[:, 1 + 4 * half:5 + 4 * half, :], banks[:, 4 + half, :].rearrange("p (b k) -> p b k", b=4),
           mid(m.bd1[:, :], 4), ALU.mult, *([("states_final", j)] if half else []))


def vector_s5(nc, led, m, V_):
    when = led.when
    ve, do, tt, ts, stt, cp = (V_[x] for x in ("ve", "do", "tt", "ts", "stt", "cp"))
    banks, v = m.banks, nc.vector
    A, S, M = ALU.add, ALU.subtract, ALU.mult
    LI, DT, AR, AI, MAG8, FR, FI, C1, S1, A4R, A4I, P8C, P8S, LR, DC, TH, W1, W2, W3, W4 = (
        m.c[name] for name in S5_ROWS[1:])
    ve.wait_ge(*when("s5_in"))
    rows = m.s5rows
    for jj in range(1, L8):
        cp(rows[0:32, 2, jj * 16:jj * 16 + 16], rows[0:32, 2, 0:16], *([("d_rows",)] if jj == 7 else []))
    ts(m.BY[64:128, :, :], m.BY[64:128, :, :], -1.0, M)
    ve.wait_ge(*when("s5_turned"))
    cp(LR, banks[:, 6, 0:32])
    cp(LI, banks[:, 6, 32:64])
    cp(DC, banks[:, 6, 64:96])
    ve.wait_ge(*when("dt_exp"))
    tt(W1, LR, DT, M)
    tt(TH, LI, DT, M)
    ts(W2, TH, 1.0 / (2 * math.pi), M, ROUND, A)
    ts(W2, W2, ROUND, S)
    stt(TH, W2, -TWO_PI_HI, TH, M, A)
    stt(TH, W2, -TWO_PI_LO, TH, M, A)
    ts(W3, TH, PI_IN, ALU.min, -PI_IN, ALU.max)
    ts(W4, W3, math.pi / 2, A)
    ts(W2, W4, math.pi, ALU.is_gt, -2 * math.pi, M)
    tt(W4, W4, W2, A)
    ts(W4, W4, PI_IN, ALU.min, -PI_IN, ALU.max, steps=[("angles",)])
    ve.wait_ge(*when("s5_funcs"))
    tt(AR, W1, C1, M)
    tt(AI, W1, S1, M)

    def cmul(xr, xi, yr, yi, outr, outi, t1, t2):
        tt(t1, xr, yr, M)
        tt(t2, xi, yi, M)
        tt(t1, t1, t2, S)
        tt(t2, xr, yi, M)
        tt(outi, xi, yr, M)
        tt(outi, outi, t2, A)
        cp(outr, t1)

    tt(W2, LR, LR, M)
    tt(W3, LI, LI, M)
    tt(W2, W2, W3, A)
    do(v.reciprocal(W2, W2))
    ts(W3, AR, -1.0, A)
    tt(FR, W3, LR, M)
    tt(W4, AI, LI, M)
    tt(FR, FR, W4, A)
    tt(FR, FR, W2, M)
    tt(FI, AI, LR, M)
    tt(W4, W3, LI, M)
    tt(FI, FI, W4, S)
    tt(FI, FI, W2, M)
    fr, fi = rep(FR, G_CH), rep(FI, G_CH)
    t1, t2 = m.q3.rearrange("p g c -> p (g c)")[:, 0:512].rearrange("p (g n) -> p g n", n=G_CH), \
        m.q3.rearrange("p g c -> p (g c)")[:, 512:1024].rearrange("p (g n) -> p g n", n=G_CH)
    tt(t1, m.BX, fr, M)
    tt(t2, m.BY, fi, M)
    tt(t1, t1, t2, S)
    tt(t2, m.BX, fi, M)
    tt(m.BY, m.BY, fr, M)
    tt(m.BY, m.BY, t2, A)
    cp(m.BX, t1)
    cmul(AR, AI, AR, AI, A4R, A4I, W2, W3)
    tt(W2, A4R, A4R, M)
    tt(W3, A4I, A4I, M)
    tt(W4, A4R, A4I, M)
    tt(A4R, W2, W3, S)
    tt(A4I, W4, W4, A)
    x, y = C1, S1
    for _ in range(3):
        tt(W2, x, x, M)
        tt(W3, y, y, M)
        tt(W4, x, y, M)
        tt(P8C, W2, W3, S)
        tt(P8S, W4, W4, A)
        x, y = P8C, P8S
    for k in range(12):
        ve.wait_ge(*when("crow_turned", k))
        src = banks[:, 4 + k % 2, 0:P]
        if k < 8:
            dst = (m.CX, m.CY)[k % 2][:, 8 * (k // 2):8 * (k // 2) + 8, :]
            neg = k % 2 == 0
            src = src.rearrange("p (g n) -> p g n", n=G_CH)
        else:
            dst = m.h0[:, k % 2, 4 * ((k - 8) // 2):4 * ((k - 8) // 2) + 4, :]
            neg = k % 2 == 1
            src = src.rearrange("p (b g) -> p b g", g=N_G)
        cp(dst[0:64], src[0:64])
        ts(dst[64:128], src[64:128], -1.0 if neg else 1.0, M, steps=[("crow_copied", k)])
    ve.wait_ge(*when("shift_out"))
    do(v.memset(m.BBp, 0.0))
    do(v.memset(m.Hs[:, :, 0:1], 0.0))
    for q in range(4):
        gs = slice(8 * q, 8 * q + 8)
        ar, ai = rep(AR[:, gs], G_CH), rep(AI[:, gs], G_CH)
        ve.wait_ge(*when("u_copied", 23))
        if q:
            ve.wait_ge(*when("y_done", q - 1))
        do(v.memset(m.CAp[:, :, 0:7, :], 0.0))

        def power(xo, yo, xi, yi):
            tt(xo, xi, ar, M)
            tt(m.q1, yi, ai, M)
            tt(m.q2, xi, ai, M)
            tt(xo, xo, m.q1, S)
            tt(yo, yi, ar, M)
            tt(yo, yo, m.q2, A)
        cp(m.CAp[:, :, 7, :], m.CX[:, gs, :])
        cp(m.CYr, m.CY[:, gs, :])
        for i in range(8):
            power(m.CAp[:, :, 8 + i, :], m.CYr, m.CAp[:, :, 7 + i, :], m.CYr)
        cp(m.ABx[:, :, 7, :], m.BX[:, gs, :])
        cp(m.ABy[:, :, 7, :], m.BY[:, gs, :])
        cp(m.BBp[:, :, 7, :], m.BX[:, gs, :])
        for i in range(7, 0, -1):
            power(m.ABx[:, :, i - 1, :], m.ABy[:, :, i - 1, :], m.ABx[:, :, i, :], m.ABy[:, :, i, :])
        cp(m.phc[:, 0, :], P8C[:, gs])
        cp(m.phc[:, 1, :], P8S[:, gs], ("powers", q))
        COS, SIN, ph = m.COS, m.SIN, m.phc
        do(v.memset(COS[:, :, 0:1], 1.0))
        do(v.memset(SIN[:, :, 0:1], 0.0))
        n = 1
        while n < NC8:
            pc, ps_ = rep(ph[:, 0, :], n), rep(ph[:, 1, :], n)
            lo, hi, tmp = slice(0, n), slice(n, 2 * n), m.G1[:, :, 0:n]
            tt(COS[:, :, hi], COS[:, :, lo], pc, M)
            tt(tmp, SIN[:, :, lo], ps_, M)
            tt(COS[:, :, hi], COS[:, :, hi], tmp, S)
            tt(SIN[:, :, hi], SIN[:, :, lo], pc, M)
            tt(tmp, COS[:, :, lo], ps_, M)
            tt(SIN[:, :, hi], SIN[:, :, hi], tmp, A)
            tt(ph[:, 2, :], ph[:, 0, :], ph[:, 0, :], M)
            tt(ph[:, 3, :], ph[:, 1, :], ph[:, 1, :], M)
            tt(ph[:, 1, :], ph[:, 0, :], ph[:, 1, :], M)
            ts(ph[:, 1, :], ph[:, 1, :], 2.0, M)
            tt(ph[:, 0, :], ph[:, 2, :], ph[:, 3, :], S)
            n *= 2
        ve.wait_ge(*when("toeplitz", q))
        for gg in range(8):
            g = 8 * q + gg
            stt(m.Tm[:, gg, :], m.ident[:, :], DC[:, g:g + 1], banks[:, 4 + gg // 4, (gg % 4) * P:(gg % 4) * P + P], M, A)
        for half in range(2):
            cp(m.ETx[:, 4 * half:4 * half + 4, :], banks[:, 6 + half, :].rearrange("p (g c) -> p g c", g=4),
               *([("etx_copied", q)] if half else []))
        ve.wait_ge(*when("ety_turned", q))
        for half in range(2):
            cp(m.ETy[:, 4 * half:4 * half + 4, :], banks[:, 6 + half, :].rearrange("p (g c) -> p g c", g=4),
               *([("ety_copied", q)] if half else []))
        ve.wait_ge(*when("left", q))
        for half in range(4):
            hs = slice(2 * half, 2 * half + 2)
            bx = banks[:, half, :].rearrange("p (g c) -> p g c", g=2)
            by = banks[:, 4 + half, :].rearrange("p (g c) -> p g c", g=2)
            cos, sin, tmp = COS[:, hs, :], SIN[:, hs, :], m.q3[:, hs, :]
            tt(m.G1[:, hs, :], bx[:, :, 0:P], cos, M)
            tt(tmp, by[:, :, 0:P], sin, M)
            tt(m.G1[:, hs, :], m.G1[:, hs, :], tmp, A)
            tt(m.G2[:, hs, :], by[:, :, 0:P], cos, M)
            tt(tmp, bx[:, :, 0:P], sin, M)
            tt(m.G2[:, hs, :], m.G2[:, hs, :], tmp, S)
            g2 = slice(8 * q + 2 * half, 8 * q + 2 * half + 2)
            t, u = m.q1[:, 0:2, 0:NB], m.q1[:, 2:4, 0:NB]
            tt(t, m.h0[:, 0, :, g2].rearrange("p b g -> p g b"), rep(A4R[:, g2], NB), M)
            tt(t, t, bx[:, :, 136:144], A)
            tt(u, m.h0[:, 1, :, g2].rearrange("p b g -> p g b"), rep(A4I[:, g2], NB), M)
            tt(m.h4[:, :, g2].rearrange("p b g -> p g b"), t, u, S)
        for gg in range(8):
            g = 8 * q + gg
            mag = MAG8[:, g:g + 1].to_broadcast([P, NC8])
            for G in (m.G1, m.G2):
                do(v.tensor_tensor_scan(G[:, gg, :], mag, G[:, gg, :], 0.0, M, A))
        tt(m.Hs[:, :, 1:129], m.G1, COS, M)
        tt(m.q3, m.G2, SIN, M)
        tt(m.Hs[:, :, 1:129], m.Hs[:, :, 1:129], m.q3, S)
        cp(m.hfin[:, gs], m.Hs[:, :, 128], ("h_states", q), *([("s5_states",)] if q == 3 else []))


def vector_sample_attention(nc, led, m, V_):
    when = led.when
    ve, do, tt, ts, stt, cp, red = (V_[x] for x in ("ve", "do", "tt", "ts", "stt", "cp", "red"))
    banks, v, ident = m.banks, nc.vector, m.ident
    ve.wait_ge(*when("o_done", 63))
    ve.wait_ge(*when("qs_saved"))
    id64 = ident[0:64, 0:64]
    red(m.csel[0:64, :].rearrange("p (h q) -> p h q", q=4), id64.rearrange("p (h c q) -> p h q c", c=2, q=4), ALU.add)
    c1 = id64.rearrange("p (h c q) -> p h c q", c=2, q=4)[:, :, 1, :]
    tmp = m.Sn[:, 0:32]
    cp(tmp.rearrange("p (h q) -> p h q", q=4), c1)
    red(m.ss[0:64, 8:9], tmp, ALU.add)
    ts(m.ss[0:64, 9:10], m.lam[0:64, 6:7], -1.0, ALU.add)
    tt(m.ss[0:64, 8:9], m.ss[0:64, 8:9], m.ss[0:64, 9:10], ALU.mult)
    ts(m.ss[0:64, 8:9], m.ss[0:64, 8:9], 1.0, ALU.add)
    red(m.sel4[0:64, :], id64.rearrange("p (a q) -> p q a", q=4), ALU.add)
    do(v.memset(m.nmask[0:64, :, :], NEG))
    nm = m.nmask[0:64, 7, :]
    do(v.memset(nm[:, 0:1], 0.0))
    for i in range(1, 4):
        tt(nm[:, i:i + 1], nm[:, i - 1:i], m.sel4[0:64, i - 1:i], ALU.add)
    ts(nm, nm, NEG, ALU.mult)
    do(v.memset(m.qpad, 0.0), ("qpad_zero",))

    def qpad(b):
        if b >= 2:
            ve.wait_ge(*when("page_scored", (b - 2) * N_PAGES + 15))
        pad = m.qpad[:, b % 2, :].rearrange("p (h s) -> p h s", s=72)
        for c in range(2):
            cs = slice(64 * c, 64 * c + 64)
            cp(pad[cs, :, 4 * c:4 * c + 4], m.qTs[cs, :, b * 4:b * 4 + 4], *([("qpad", b)] if c else []))

    def outputs(b):
        ve.wait_ge(*when("os_turned", b))
        src = banks[:, 7, 0:256].rearrange("p (h s) -> p h s", s=32)
        for h in range(H_C):
            cp(m.oT[:, h, TP + 4 * b:TP + 4 * b + 4], src[:, h, 4 * h:4 * h + 4],
               *([("os_done", b)] + ([("oT_done",)] if b == NB - 1 else []) if h == H_C - 1 else []))

    qpad(0)
    qpad(1)
    for b in range(NB):
        ss = m.ss[0:64, :]
        ve.wait_ge(*when("s_new", b))
        if b:
            ve.wait_ge(*when("pts_done", b - 1))
        tt(m.Sn, banks[0:64, 6, 0:NS], m.nmask[0:64, 7 - b:15 - b, :].rearrange("p b k -> p (b k)"), ALU.add)
        red(ss[:, 10:11], m.Sn, ALU.max)
        for p in range(N_PAGES):
            e = b * N_PAGES + p
            ve.wait_ge(*when("page_turned", e, 1))
            if e >= 2:
                ve.wait_ge(*when("page_scored", e - 2))
            cp(m.KTp[:, p % 2, 4:8, :], banks[:, 5, :].rearrange("p (h k) -> p h k", h=4), ("page_copied", e, 1))
            if p in (5, 9, 13):
                red(ss[:, 10 + p // 4:11 + p // 4], banks[0:64, p // 4 - 1, :], ALU.max)
            if b and p == 2:
                outputs(b - 1)
        ve.wait_ge(*when("page_scored", b * N_PAGES + 15))
        red(ss[:, 14:15], banks[0:64, 3, :], ALU.max)
        red(ss[:, 2:3], ss[:, 10:15], ALU.max)
        ts(ss[:, 3:4], ss[:, 2:3], -1.0, ALU.mult, steps=[("s_max", b)])
        ve.wait_ge(*when("s_exp", b))
        tt(ss[:, 6:7], ss[:, 4:5], ss[:, 5:6], ALU.add)
        do(v.reciprocal(ss[:, 6:7], ss[:, 6:7]))
        tt(ss[:, 6:7], ss[:, 6:7], ss[:, 8:9], ALU.mult)
        ts(m.Cm, m.csel[0:64, :], ss[:, 6:7], ALU.mult, steps=[("s_coef", b)])
        ve.wait_ge(*when("pts_done", b))
        cp(m.PTs[:, 0:16, :], banks[:, 4, :].rearrange("p (a q) -> p a q", a=16))
        cp(m.PTs[0:NS, 16, :], banks[0:NS, 5, 0:NS], ("pts_copied", b))
        if b + 2 < NB:
            qpad(b + 2)
        ve.wait_ge(*when("os_ready", b))
        cp(m.Os[:, 0:512], banks[0:NS, 6, :])
        cp(m.Os[:, 512:1024], banks[0:NS, 7, :], ("os_copied", b))
    outputs(NB - 1)


def scalar_program(nc, block, led, m):
    sig, when = led.sig, led.when
    banks, vec = m.banks, m.vec

    @block.scalar
    def _(ac):
        def do(ins, *steps):
            steps = steps or (("step",),)
            ins.then_inc(*sig("scalar", *steps))
            ac.wait_ge(*led.own("scalar", steps[0]))

        def act(out, x, f, *steps, bias=0.0, scale=1.0, accum=None):
            kw = {"accum_out": accum} if accum is not None else {}
            do(nc.scalar.activation(out, x, f, bias=bias, scale=scale, **kw), *steps)

        def cp(out, x, *steps):
            do(nc.scalar.copy(out, x), *steps)

        n_tile = [0]

        def next_set():
            n = n_tile[0]
            n_tile[0] += 1
            return n, 3 * (n % 2)

        ac.wait_ge(*when("params_in"))
        act(m.csig, m.crows, ACT.Sigmoid, ("cond_sig",))
        for i, (t0, n) in enumerate(TILES):
            for half in range(2):
                ac.wait_ge(*when("xin_turned", i, half))
                cp(m.xT[:, 4 * half:4 * half + 4, t0:t0 + n],
                   banks[:, 6 + half, :].rearrange("p (q t) -> p q t", q=4)[:, :, 0:n], ("xin_copied", i, half),
                   *([("xin_used", i)] + ([("x_ready", 0)] if i == 8 else []) if half else []))
        ac.wait_ge(*when("lam_dots"))
        act(m.lam[0:1, 2:4], m.lam[0:1, 0:2], ACT.Exp, ("lam_exps",))

        def modulation(first, last):
            for n in range(first, last + 1):
                if n < last:
                    ac.wait_ge(*when("mod_sums", n))
                    if n > first:
                        ac.wait_ge(*when("mod_turned", n - 1))
                    cp(m.modrow, banks[0:9, 6 + n % 2, 0:256], ("mod_copied", n))
                if n > first:
                    ac.wait_ge(*when("mod_turned", n - 1))
                    layer, s = (n - 1) // 24, ((n - 1) % 24) * 2
                    for h in range(2):
                        act(m.modT[:, layer, s + h, :], banks[:, 6 + n % 2, 256 + h * 16:256 + h * 16 + 9], ACT.Identity,
                            *([("mod_biased", n - 1)] if h else []), bias=m.bT[:, layer * 48 + s + h:layer * 48 + s + h + 1])

        def roots(dst, step, **kw):
            n, s = next_set()
            ac.wait_ge(*when("set_done", n))
            for c, (t0, t1) in enumerate(CHUNKS):
                act(dst[:, t0:t1], banks[:, s + c, 0:CH], ACT.Sqrt, *([step, ("set_free", n)] if c == 2 else []), **kw)

        def squares(layer, w):
            for k in range(KT):
                if (layer, w) != (0, 0):
                    ac.wait_ge(*when("x_tile", (layer, w), k))
                if k >= 3:
                    ac.wait_ge(*when("sq_added", (layer, w), k - 2))
                act(m.sq[:, k % 2, :] if k else m.ssq, m.xT[:, k, :], ACT.Square, ("squares", (layer, w), k))
            roots(m.rstd, ("std", (layer, w)), bias=m.eps[:, 0:1])

        squares(0, 0)
        modulation(0, ADA_FIRST)
        last_z = [None]

        def z_rows(zi):
            n, s = next_set()
            ac.wait_ge(*when("set_done", n))
            if last_z[0] is None:
                ac.wait_ge(*when("zb_zero"))
            else:
                ac.wait_ge(*when("zb_used", last_z[0]))
            last_z[0] = n
            sv = m.zb[:, 1025:1065].rearrange("p (b q) -> p b q", q=5)
            cp(sv[:, :, 0], m.shiftT[:, zi, :])
            cp(m.zb[:, 1:1 + CH], banks[:, s, 0:CH])
            cp(m.zb[:, 1 + CH:1 + 2 * CH], banks[:, s + 1, 0:CH])
            cp(m.zb[:, 1 + 2 * CH:1 + TP], banks[:, s + 2, 0:TP - 2 * CH])
            cp(sv[:, :, 1:5], banks[:, s + 2, TP - 2 * CH:CH].rearrange("p (b q) -> p b q", q=TS),
               ("zb_ready", n), ("set_free", n))
            cp(m.lastz[:, zi, 0:1], m.zb[:, TP:TP + 1])
            cp(m.lastz[:, zi, 1:9], sv[:, :, 4])

        z_rows(12)
        ac.wait_ge(*when("zb_used", last_z[0]))
        act(m.lora[0:64, :], m.lora[0:64, :], ACT.Tanh, ("lora_ready",))
        z_rows(13)
        ac.wait_ge(*when("zb_used", last_z[0]))
        act(m.sgd, m.sgd, ACT.Sigmoid, ("sg_ready",))
        for j in range(N_PAIR):
            batches = ada_batches(j)
            for base in (0, 4, 8):
                z_rows(base + j)
            ac.wait_ge(*when(*(("mix_ready", j - 1) if j else ("spilled", 0))))
            for dst, func, bias, step in ((m.LW, ACT.Sigmoid, "rwkv_w0", "lw_sig"), (m.Af, ACT.Sigmoid, "rwkv_a0", "a_ready"),
                                          (m.Gf, None, None, "g_ready")):
                n, s = next_set()
                ac.wait_ge(*when("set_done", n))
                for c, (t0, t1) in enumerate(CHUNKS):
                    steps = [(step, j), ("set_free", n)] if c == 2 else []
                    if func is None:
                        cp(dst[:, t0:t1], banks[:, s + c, 0:CH], *steps)
                    else:
                        act(dst[:, t0:t1], banks[:, s + c, 0:CH], func, *steps, bias=vec(bias, j))
                if step == "g_ready":
                    modulation(*next(batches))
            roots(m.T1, ("kk_norm", j))
            modulation(*next(batches))
            next_set()
            ac.wait_ge(*when("lx", j))
            act(m.T1, m.T1, ACT.Exp, ("e_lx", j))
            act(m.KH, m.Lc, ACT.Exp, ("e_l", j))
            act(m.BH, m.Lc, ACT.Exp, ("e_nl", j), scale=-1.0)
            modulation(*next(batches))
            for k, stage in tile_stages():
                scalar_rwkv_stage(ac, led, m, cp, j, k, stage)
            ac.wait_ge(*when("tm_turned", j, N_TILE))
            cp(m.TM[0:NS, 0, :, :], banks[0:NS, 0, :].rearrange("p (i f) -> p i f", i=4), ("tm_ready", j, N_TILE))
            next_set()
            roots(m.T1, ("gn_std", j), scale=1.0 / C64, bias=m.eps[:, 1:2])

        ac.wait_ge(*when("shift_turned"))
        ac.wait_ge(*when("mix_ready", 3))
        ac.wait_ge(*when("sout_out", 3))
        for i, (bank, cnt) in enumerate(((0, 512), (1, 512), (2, 512), (3, 256))):
            cp(m.shout[:, i * 512:i * 512 + cnt], banks[0:9, bank, 0:cnt], *([("shout_ready",)] if i == 3 else []))
        ac.wait_ge(*when("usa_zero"))
        c = m.c
        for i in range(24):
            half, q = i // 12, i % 12
            gs = slice(16 * half, 16 * half + 16)
            ac.wait_ge(*when("u_done", i))
            if q < 8:
                cp(m.U[:, gs, q, :], banks[:, i % 4, 0:256].rearrange("p (g n) -> p g n", n=G_CH), ("u_copied", i))
            else:
                cp(m.UsA[:, gs, q - 4, :], banks[0:NB, i % 4, 0:256].rearrange("p (g n) -> p g n", n=G_CH), ("u_copied", i))
            if i == 5:
                ac.wait_ge(*when("s5_in"))
                act(c["DT"], c["LOGDT"], ACT.Exp, ("dt_exp",))
            if i == 9:
                ac.wait_ge(*when("angles"))
                act(c["MAG8"], c["W1"], ACT.Exp, scale=float(L8))
                act(c["W1"], c["W1"], ACT.Exp)
                act(c["S1"], c["W3"], ACT.Sin)
                act(c["C1"], c["W4"], ACT.Sin, ("s5_funcs",))
        for q in range(4):
            ac.wait_ge(*when("ut_turned", q))
            if q:
                ac.wait_ge(*when("y_done", q - 1))
            for i in range(4):
                cp(m.UT[:, 2 * i:2 * i + 2, :], banks[:, i, :].rearrange("p (g c) -> p g c", g=2)[:, :, 0:144],
                   *([("ut_copied", q)] if i == 3 else []))
            ac.wait_ge(*when("y_done", q))
            for i in range(2):
                g0 = 64 * i
                src = banks[:, i, :].rearrange("p (g j n) -> p g j n", g=4, n=G_CH)
                dst = m.Yq[:, :, g0:g0 + 64].rearrange("p j (g n) -> p g j n", n=G_CH)
                for gg in range(4):
                    act(dst[:, gg], src[:, gg], ACT.Gelu_apprx_tanh)
                src = banks[0:NB, 2 + i, :].rearrange("p (g j n) -> p g j n", g=4, n=G_CH)[:, :, 0:4, :]
                dst = m.Yqs[:, :, g0:g0 + 64].rearrange("p j (g n) -> p g j n", n=G_CH)
                for gg in range(4):
                    act(dst[:, gg], src[:, gg], ACT.Gelu_apprx_tanh, *([("gelu_done", q)] if (i, gg) == (1, 3) else []))
            ac.wait_ge(*when("y_turned", q))
            for part in range(3):
                src = banks[:, 4 + part, :].rearrange("p (j c) -> p j c", j=4)
                if part < 2:
                    dst = m.yT[:, q, 0:TP].rearrange("p (c j) -> p j c", j=L8)[:, 4 * part:4 * part + 4, :]
                else:
                    dst, src = smp(m.yT[:, q, :]).rearrange("p b j -> p j b"), src[:, :, 0:NB]
                cp(dst, src, ("y_copied", q, part))
        ac.wait_ge(*when("s5_states_turned"))
        cp(m.s5rows[:, 0, :], banks[:, 7, 0:P], ("sfin_rows", 0))
        cp(m.s5rows[:, 1, :], banks[:, 7, P:2 * P], ("sfin_rows", 1))
        cp(m.s5rows[0:32, 2, :], banks[0:32, 7, 256:384], ("sfin_rows", 2))
        for ft in range(4):
            n, s = next_set()
            ac.wait_ge(*when("set_done", n))
            if ft:
                ac.wait_ge(*when("glu_used", ft - 1))
            for c, (t0, t1) in enumerate(CHUNKS):
                act(m.sT[:, t0:t1], banks[:, s + c, 0:CH], ACT.Sigmoid, *([("glu_sig", ft), ("set_free", n)] if c == 2 else []),
                    bias=vec("s5_b_glu", ft))

        def out_and_mlp(layer):
            for _ in range(8):
                next_set()
            squares(layer, 1)
            for q in range(4):
                for k in range(8):
                    n, s = next_set()
                    ac.wait_ge(*when("set_done", n))
                    for c, (t0, t1) in enumerate(CHUNKS):
                        act(m.mT[:, k, t0:t1], banks[:, s + c, 0:CH], ACT.Relu,
                            *([("relu", n), ("set_free", n)] if c == 2 else []))
                for _ in range(8):
                    next_set()

        out_and_mlp(0)
        squares(1, 0)
        ac.wait_ge(*when("h_ready", 1, 0))
        ac.wait_ge(*when("spilled", 1))
        for i in range(16):
            n, s = next_set()
            ac.wait_ge(*when("set_done", n))
            for c, (t0, t1) in enumerate(CHUNKS):
                steps = [("set_free", n)] + ([("qk_ready",)] if i == 15 else []) if c == 2 else []
                if i < 8:
                    act(m.qT[:, i, t0:t1], banks[:, s + c, 0:CH], ACT.Copy, *steps, scale=0.125)
                else:
                    cp(m.kT[:, i - 8, t0:t1], banks[:, s + c, 0:CH], *steps)
        ac.wait_ge(*when("s5_out"))
        cp(m.kTs, m.kT[:, :, TP:T])
        cp(m.qTs, m.qT[:, :, TP:T], ("qs_saved",))
        for e in range(36):
            i, t0, cnt = e % 9, *TILES[e % 9]
            c0 = (e // 9) * 256
            ac.wait_ge(*when("v_done", e))
            cp(m.V[0:cnt, i, c0:c0 + 256], banks[0:cnt, 6 + e % 2, 0:256], ("v_copied", e),
               *([("v_rows", i)] if e >= 27 else []))
        for i, (t0, cnt) in enumerate(TILES):
            for half in range(2):
                ac.wait_ge(*when("k_turned", i, half))
                if i >= 4 and half == 0:
                    ac.wait_ge(*when("k_out", i - 4))
                cp(m.kout[0:cnt, i % 4, half * 512:half * 512 + 512], banks[0:cnt, half, :], ("k_copied", i, half),
                   *([("k_rows", i)] if half else []))
        for i in range(5, 9):
            ac.wait_ge(*when("k_out", i))
        for s in range(66):
            for c in range(2):
                if s < 64:
                    nk = (s % 8 + 1) * P
                    st = m.st[:, s % 3, :]
                    ac.wait_ge(*when("row_max", s, c))
                    if s >= 3 and c == 0:
                        ac.wait_ge(*when("pt_turned", s - 3))
                    row = banks[:, 2 * c:2 * c + 2, :].rearrange("p b k -> p (b k)")[:, 0:nk]
                    act(m.Pp[:, s % 3, c, 0:nk], row, ACT.Exp, ("scores_free", s, c),
                        bias=st[:, 2 + c:3 + c], accum=st[:, 4 + c:5 + c])
                if s < 2:
                    continue
                h, i = (s - 2) // 8, (s - 2) % 8
                if c == 0:
                    ac.wait_ge(*when("pt_turned", s - 2))
                    if s >= 3:
                        ac.wait_ge(*when("o_done", s - 3))
                    cp(m.PTp[:, 0:i + 1, :], banks[:, 4:6, :].rearrange("p b (c q) -> p (b c) q", q=P)[:, 0:i + 1, :],
                       ("pt_copied", s - 2))
                else:
                    ac.wait_ge(*when("o_done", s - 2))
                    cp(m.oT[:, h, i * P:i * P + P], banks[:, 6 + s % 2, 0:P], ("o_copied", s - 2))
        scalar_sample_attention(nc, ac, led, m, act, cp)
        ac.wait_ge(*when("oT_done"))
        act(m.sq2[:, 0, :], m.oT[:, 0, :], ACT.Square, ("o_sq", 0))
        for h in range(H_C):
            if h + 1 < H_C:
                act(m.sq2[:, (h + 1) % 2, :], m.oT[:, h + 1, :], ACT.Square, ("o_sq", h + 1))
            if h >= 2:
                ac.wait_ge(*when("o_normed", h - 2))
            roots(m.r2[:, h % 2, :], ("o_std", h), scale=float(D // P), bias=m.eps[:, 0:1])
        out_and_mlp(1)
        squares(2, 0)
        for i, (t0, cnt) in enumerate(TILES):
            for half in range(2):
                ac.wait_ge(*when("y_row_turned", i, half))
                if i >= 2 and half == 0:
                    ac.wait_ge(*when("y_out", i - 2))
                cp(m.yrow[0:cnt, i % 2, half * 512:half * 512 + 512], banks[0:cnt, 6 + half, :],
                   ("y_row_copied", i, half), *([("y_rows", i)] if half else []))


def scalar_rwkv_stage(ac, led, m, cp, j, k, stage):
    when, banks, p = led.when, m.banks, k % 2
    a, b, c, d = range(4 * p, 4 * p + 4)
    us = slice(2 * p, 2 * p + 2)

    def cells(bank):
        return banks[:, bank, 0:256].rearrange("p (u t) -> p u t", t=P)

    if stage == S_TM:
        ac.wait_ge(*when("tm_turned", j, k))
        cp(m.TM[:, p, :, :], banks[:, a, :].rearrange("p (i f) -> p i f", i=4), ("tm_ready", j, k))
    elif stage == S_D2:
        ac.wait_ge(*when("d2", j, k))
        cp(m.PW[:, 1, us, :], cells(c), ("d2_copied_t", j, k))
    elif stage == S_D4:
        ac.wait_ge(*when("d4", j, k))
        cp(m.PW[:, 1, us, :], cells(c), ("d4_copied_t", j, k))
    elif stage == S_D8:
        ac.wait_ge(*when("d8", j, k))
        cp(m.PW[:, 0, us, :], cells(a), ("d8_copied", j, k))
    elif stage == S_F:
        ac.wait_ge(*when("f4p", j, k))
        cp(m.RHS[:, p, :, 1, :], banks[:, a, 0:2 * C64].rearrange("p (h v) -> p h v", h=2))
        cp(m.RHS[:, p, :, 0, :], m.TM[:, p, 3, :].rearrange("p (h v) -> p h v", h=2), ("rhs_ready", j, k))
    elif stage in (S_L1, S_M1):
        lv = int(stage == S_M1)
        ac.wait_ge(*when("level_p1", j, k, lv))
        cp(m.FT[:, us, :], cells(b), ("level_copied_t", j, k, lv))
    elif stage == S_XY:
        ac.wait_ge(*when("xy", j, k))
        cp(m.XY[:, p, :, :, :], banks[:, b, 0:256].rearrange("p (h i v) -> p i h v", h=2, i=2), ("xy_copied", j, k))
    elif stage == S_ZQ:
        ac.wait_ge(*when("zq", j, k))
        for h in range(2):
            hs = slice(64 * h, 64 * h + 64)
            cp(m.QTt[hs, p, :], banks[hs, d, h * P:h * P + P], *([("q_copied", j, k)] if h else []))


def scalar_sample_attention(nc, ac, led, m, act, cp):
    when = led.when
    banks = m.banks
    for b in range(NB):
        for p in range(N_PAGES):
            e = b * N_PAGES + p
            ac.wait_ge(*when("page_turned", e, 0))
            if e >= 2:
                ac.wait_ge(*when("page_scored", e - 2))
            cp(m.KTp[:, p % 2, 0:4, :], banks[:, 4, :].rearrange("p (h k) -> p h k", h=4), ("page_copied", e, 0))
        ac.wait_ge(*when("s_max", b))
        ss = m.ss[0:64, :]
        if b:
            ac.wait_ge(*when("pts_done", b - 1))
        act(m.Ps[:, 0:2048], banks[0:64, 0:4, :].rearrange("p b k -> p (b k)"), ACT.Exp, bias=ss[:, 3:4],
            accum=ss[:, 4:5])
        act(m.Ps[:, 2048:2048 + NS], m.Sn, ACT.Exp, ("s_exp", b), bias=ss[:, 3:4], accum=ss[:, 5:6])


_OUTS = [("y_prompt", (1, 1024, 1024)), ("y_sample", (8, 4, 1024)), ("p_shift", (1, 1792)), ("p_wkv", (1, 8, 64, 64)),
         ("p_ssm_re", (1, 32, 64)), ("p_ssm_im", (1, 32, 64)), ("p_k", (1, 1024, 8, 128)), ("p_v", (1, 1024, 8, 128)),
         ("s_shift", (8, 1792)), ("s_wkv", (8, 8, 64, 64)), ("s_ssm_re", (8, 32, 64)), ("s_ssm_im", (8, 32, 64)),
         ("s_k", (8, 4, 8, 128)), ("s_v", (8, 4, 8, 128))]


def kernel(**inputs):
    import concourse.bacc as bacc
    from concourse.bass_utils import run_bass_kernel_spmd as run

    arrays = {f"in_{k}": np.ascontiguousarray(v) for k, v in inputs.items()}

    def build(known):
        nc = bacc.Bacc("TRN2", target_bir_lowering=False, num_devices=1)
        a = {k[3:]: nc.dram_tensor(k, v.shape, mybir.dt.from_np(v.dtype), kind="ExternalInput").ap()
             for k, v in arrays.items()}
        o = {n: nc.dram_tensor(f"out_{n}", s, F32, kind="ExternalOutput").ap() for n, s in _OUTS}
        return nc, decoder_step(nc, a, o, known)

    _, known = build(None)
    nc, _ = build(known)
    r = run(nc, [arrays], core_ids=[0])
    return tuple(r.results[0][f"out_{n}"] for n, _ in _OUTS)
```
